# Optimizing a Trainium2 kernel written in Bass

```python
import math
import jax, jax.numpy as jnp
from jax import lax
import numpy as np
import jax
import jax.numpy as jnp

D_MODEL = 1024
BATCH = 1
SEQ = 256
DEPTH = 1

CHUNK = 64
Q_BLOCK = 128
HEAD_DIM = 64
H_DIFF = 4
H_FOX = 6
H_CHUNK = 6
N_PREV_CHUNKS = 8
REL_CLIP = 128
D_FF = 2816
CONV_WIDTH = 3
PLE_DIM = 256
EPS = 1e-6
NEG_INF = -1e30

W_DIFF = H_DIFF * HEAD_DIM
W_FOX = H_FOX * HEAD_DIM
W_CHUNK = H_CHUNK * HEAD_DIM
MIX_WIDTH = W_DIFF + W_FOX + W_CHUNK
IN_SIZES = (W_DIFF,) * 5 + (W_FOX,) * 3 + (H_FOX,) + (W_CHUNK,) * 3
IN_COLS = sum(IN_SIZES)
IN_SPLITS = tuple(int(c) for c in np.cumsum(IN_SIZES)[:-1])
ALIBI_SLOPES = tuple(2.0 ** (-8.0 * (h + 1) / H_DIFF) for h in range(H_DIFF))


def rms_norm(x, g):
    xf = x.astype(jnp.float32)
    y = xf * lax.rsqrt(jnp.mean(xf * xf, axis=-1, keepdims=True) + EPS)
    return (y * g.astype(jnp.float32)).astype(x.dtype)

def split_heads(t, n_heads):
    return t.reshape(t.shape[0], t.shape[1], n_heads, HEAD_DIM)

def query_blocks(q):
    b, s = q.shape[0], q.shape[1]
    q = q.reshape((b, s // Q_BLOCK, Q_BLOCK) + q.shape[2:])
    return jnp.swapaxes(q, 0, 1)

def merge_blocks(o):
    nb, b, qb, h, d = o.shape
    return jnp.swapaxes(o, 0, 1).reshape(b, nb * qb, h * d)

def diff_attention(q1, q2, k1, k2, v, lam, subln_g, lam_init):
    S = k1.shape[1]
    slopes = jnp.asarray(ALIBI_SLOPES, jnp.float32)
    kpos = jnp.arange(S)
    scale = HEAD_DIM ** -0.5

    def block(args):
        q1b, q2b, blk = args
        qpos = blk * Q_BLOCK + jnp.arange(Q_BLOCK)
        dist = jnp.abs(qpos[:, None] - kpos[None, :]).astype(jnp.float32)
        bias = -slopes[:, None, None] * dist
        allowed = (kpos[None, :] // CHUNK) <= (qpos[:, None] // CHUNK)

        def probs(qb, k):
            s = jnp.einsum('bqhd,bkhd->bhqk', qb, k).astype(jnp.float32) * scale + bias
            s = jnp.where(allowed, s, NEG_INF)
            return jax.nn.softmax(s, axis=-1)

        a = probs(q1b, k1) - lam * probs(q2b, k2)
        return jnp.einsum('bhqk,bkhd->bqhd', a.astype(v.dtype), v)

    nb = S // Q_BLOCK
    o = lax.map(block, (query_blocks(q1), query_blocks(q2), jnp.arange(nb)))
    o = rms_norm(o, subln_g) * (1.0 - lam_init)
    return merge_blocks(o)

def forgetting_attention(q, k, v, log_f):
    B, S, H, _ = q.shape
    F = jnp.cumsum(log_f, axis=1)
    F_k = jnp.transpose(F, (0, 2, 1))
    F_q = jnp.transpose(query_blocks(F), (0, 1, 3, 2))
    kpos = jnp.arange(S)
    scale = HEAD_DIM ** -0.5

    def block(args):
        qb, fq, blk = args
        qpos = blk * Q_BLOCK + jnp.arange(Q_BLOCK)
        s = jnp.einsum('bqhd,bkhd->bhqk', qb, k).astype(jnp.float32) * scale
        s = s + fq[..., None] - F_k[:, :, None, :]
        allowed = kpos[None, :] <= qpos[:, None]
        s = jnp.where(allowed, s, NEG_INF)
        pr = jax.nn.softmax(s, axis=-1)
        return jnp.einsum('bhqk,bkhd->bqhd', pr.astype(v.dtype), v)

    nb = S // Q_BLOCK
    o = lax.map(block, (query_blocks(q), F_q, jnp.arange(nb)))
    return merge_blocks(o)

def chunk_band(t):
    b, s, h, d = t.shape
    nc = s // CHUNK
    tc = t.reshape(b, nc, CHUNK, h, d)
    tp = jnp.pad(tc, ((0, 0), (N_PREV_CHUNKS, 0), (0, 0), (0, 0), (0, 0)))
    return jnp.concatenate([tp[:, j:j + nc] for j in range(N_PREV_CHUNKS + 1)], axis=2)

def chunk_attention(q, k, v, rel_table):
    B, S, H, d = q.shape
    nc = S // CHUNK
    band_len = (N_PREV_CHUNKS + 1) * CHUNK
    qc = q.reshape(B, nc, CHUNK, H, d)
    kb = chunk_band(k)
    vb = chunk_band(v)
    qq = np.arange(CHUNK)[:, None]
    kk = np.arange(band_len)[None, :]
    rel = N_PREV_CHUNKS * CHUNK + qq - kk
    idx = np.clip(rel, -REL_CLIP, REL_CLIP) + REL_CLIP
    bias = rel_table[:, idx].astype(jnp.float32)
    key_chunk = (jnp.arange(nc)[:, None] - N_PREV_CHUNKS
                 + (jnp.arange(band_len) // CHUNK)[None, :])
    valid = (key_chunk >= 0)[:, None, None, :]
    s = jnp.einsum('bcqhd,bckhd->bchqk', qc, kb).astype(jnp.float32) * (HEAD_DIM ** -0.5) + bias
    s = jnp.where(valid, s, NEG_INF)
    pr = jax.nn.softmax(s, axis=-1)
    o = jnp.einsum('bchqk,bckhd->bcqhd', pr.astype(v.dtype), vb)
    return o.reshape(B, S, H * d)

def conv_gated_mlp(h, w_up, conv_w, conv_b, w_down):
    u = h @ w_up
    S = u.shape[1]
    up = jnp.pad(u, ((0, 0), (CONV_WIDTH - 1, 0), (0, 0)))
    c = conv_b
    for j in range(CONV_WIDTH):
        c = c + conv_w[j] * up[:, j:j + S]
    gate, val = jnp.split(c, 2, axis=-1)
    return (jax.nn.silu(gate) * val) @ w_down

def first_inputs(seed: int = 0) -> dict:
    key = jax.random.key(seed)
    ks = jax.random.split(key, 20)
    f32 = jnp.float32
    nrm = lambda k, shape, s: jax.random.normal(k, shape, f32) * s
    gain = lambda k, shape: 1.0 + 0.05 * jax.random.normal(k, shape, f32)
    return {
        "x": jax.random.normal(ks[0], (BATCH, SEQ, D_MODEL), f32),
        "p": jax.random.normal(ks[1], (DEPTH, BATCH, SEQ, PLE_DIM), f32),
        "ln_mix": gain(ks[2], (DEPTH, D_MODEL)),
        "w_in": nrm(ks[3], (DEPTH, D_MODEL, IN_COLS), D_MODEL ** -0.5),
        "qk_gain": gain(ks[4], (DEPTH, 6, HEAD_DIM)),
        "lam_params": nrm(ks[5], (DEPTH, 4, HEAD_DIM), 0.1),
        "subln_gain": gain(ks[6], (DEPTH, HEAD_DIM)),
        "fgate_bias": jax.random.uniform(ks[7], (DEPTH, H_FOX), f32, 1.0, 4.0),
        "rel_bias": nrm(ks[8], (DEPTH, H_CHUNK, 2 * REL_CLIP + 1), 0.1),
        "w_out": nrm(ks[9], (DEPTH, MIX_WIDTH, D_MODEL), MIX_WIDTH ** -0.5),
        "ln_ffn": gain(ks[10], (DEPTH, D_MODEL)),
        "w_up": nrm(ks[11], (DEPTH, D_MODEL, 2 * D_FF), D_MODEL ** -0.5),
        "conv_w": nrm(ks[12], (DEPTH, CONV_WIDTH, 2 * D_FF), CONV_WIDTH ** -0.5),
        "conv_b": nrm(ks[13], (DEPTH, 2 * D_FF), 0.02),
        "w_down": nrm(ks[14], (DEPTH, D_FF, D_MODEL), D_FF ** -0.5),
        "ln_ple": gain(ks[15], (DEPTH, D_MODEL)),
        "w_ple_gate": nrm(ks[16], (DEPTH, D_MODEL, D_MODEL), D_MODEL ** -0.5),
        "w_ple_proj": nrm(ks[17], (DEPTH, PLE_DIM, D_MODEL), PLE_DIM ** -0.5),
    }

def first_block(x, p, ln_mix, w_in, qk_gain, lam_params, subln_gain, fgate_bias, rel_bias,
              w_out, ln_ffn, w_up, conv_w, conv_b, w_down, ln_ple, w_ple_gate, w_ple_proj):
    h = x
    for i in range(DEPTH):
        hn = rms_norm(h, ln_mix[i])
        z = hn @ w_in[i]
        (q1, q2, k1, k2, va, qf, kf, vf, fg, qc, kc, vc) = jnp.split(z, IN_SPLITS, axis=-1)
        g = qk_gain[i]
        q1 = rms_norm(split_heads(q1, H_DIFF), g[0])
        q2 = rms_norm(split_heads(q2, H_DIFF), g[0])
        k1 = rms_norm(split_heads(k1, H_DIFF), g[1])
        k2 = rms_norm(split_heads(k2, H_DIFF), g[1])
        va = split_heads(va, H_DIFF)
        lp = lam_params[i].astype(jnp.float32)
        lam_init = 0.8 - 0.6 * math.exp(-0.3 * i)
        lam = jnp.exp(jnp.sum(lp[0] * lp[1])) - jnp.exp(jnp.sum(lp[2] * lp[3])) + lam_init
        o_a = diff_attention(q1, q2, k1, k2, va, lam, subln_gain[i], lam_init)
        qf = rms_norm(split_heads(qf, H_FOX), g[2])
        kf = rms_norm(split_heads(kf, H_FOX), g[3])
        vf = split_heads(vf, H_FOX)
        log_f = jax.nn.log_sigmoid(fg.astype(jnp.float32) + fgate_bias[i].astype(jnp.float32))
        o_b = forgetting_attention(qf, kf, vf, log_f)
        qc = rms_norm(split_heads(qc, H_CHUNK), g[4])
        kc = rms_norm(split_heads(kc, H_CHUNK), g[5])
        vc = split_heads(vc, H_CHUNK)
        o_c = chunk_attention(qc, kc, vc, rel_bias[i])
        h = h + jnp.concatenate([o_a, o_b, o_c], axis=-1) @ w_out[i]
        h = h + conv_gated_mlp(rms_norm(h, ln_ffn[i]), w_up[i], conv_w[i], conv_b[i], w_down[i])
        gate = jax.nn.sigmoid(rms_norm(h, ln_ple[i]) @ w_ple_gate[i])
        h = h + (p[i] @ w_ple_proj[i]) * gate
    return h


DEPTH_2 = 2

MEM_LEN = 256
N_EVEN = (DEPTH_2 + 1) // 2
N_ODD = DEPTH_2 // 2

MLSTM_HEADS = 4
MLSTM_DQK = 64
MLSTM_DV = 128
MLSTM_CHUNK = 64
GATE_SOFTCAP = 15.0

SB_HEADS = 4
SB_DH = 128
SB_BLOCK = 128

GDN_HEADS = 8
GDN_DK = 128
GDN_DV = 128
GDN_CONV = 4
GDN_CHUNK = 64

XA_HEADS = 4
XA_DH = D_MODEL // XA_HEADS
D_FF_2 = 4 * D_MODEL

ML_QK = MLSTM_HEADS * MLSTM_DQK
ML_V = MLSTM_HEADS * MLSTM_DV
SB_W = SB_HEADS * SB_DH
AB_SIZES = (ML_QK, ML_QK, ML_V, ML_V, MLSTM_HEADS, MLSTM_HEADS, SB_W, SB_W, SB_W)
AB_IN = sum(AB_SIZES)
AB_OUT = ML_V + SB_W

GDN_QK = GDN_HEADS * GDN_DK
GDN_VW = GDN_HEADS * GDN_DV
GDN_CONV_CH = 2 * GDN_QK + GDN_VW
C_SIZES = (GDN_CONV_CH, GDN_VW, GDN_HEADS, GDN_HEADS)
C_IN = sum(C_SIZES)


def _split(y, sizes):
    return jnp.split(y, np.cumsum(sizes)[:-1].tolist(), axis=-1)

def rmsnorm(x, g):
    xf = x.astype(jnp.float32)
    y = xf * lax.rsqrt(jnp.mean(xf * xf, axis=-1, keepdims=True) + EPS)
    return (y * g.astype(jnp.float32)).astype(x.dtype)

def l2norm(x):
    xf = x.astype(jnp.float32)
    return xf * lax.rsqrt(jnp.sum(xf * xf, axis=-1, keepdims=True) + EPS)

def _to_chunks(a, L):
    B, T = a.shape[0], a.shape[1]
    a = a.reshape((B, T // L, L) + a.shape[2:])
    return jnp.moveaxis(a, (1, 3), (0, 2))

def _from_chunks(a):
    a = jnp.moveaxis(a, (0, 2), (1, 3))
    nc, L = a.shape[1], a.shape[2]
    return a.reshape((a.shape[0], nc * L) + a.shape[3:])

def mlstm(q, k, v, i_pre, f_pre):
    f32 = jnp.float32
    B, T, H, dk = q.shape
    dv = v.shape[-1]
    L = MLSTM_CHUNK
    log_i = GATE_SOFTCAP * jnp.tanh(i_pre.astype(f32) / GATE_SOFTCAP)
    log_f = jax.nn.log_sigmoid(f_pre.astype(f32))
    xs = (_to_chunks(q.astype(f32), L),
          _to_chunks(k.astype(f32) * (dk ** -0.5), L),
          _to_chunks(v.astype(f32), L),
          _to_chunks(log_i, L),
          _to_chunks(log_f, L))
    causal = jnp.tril(jnp.ones((L, L), dtype=bool))

    def step(carry, inp):
        C, n, m = carry
        qc, kc, vc, li, lf = inp
        b = jnp.cumsum(lf, axis=-1)
        d = jnp.where(causal, b[..., :, None] - b[..., None, :] + li[..., None, :], -jnp.inf)
        inter = b + m[..., None]
        m_t = jnp.maximum(inter, jnp.max(d, axis=-1))
        w_inter = jnp.exp(inter - m_t)
        s = jnp.einsum('bhtd,bhsd->bhts', qc, kc) * jnp.exp(d - m_t[..., None])
        num = jnp.einsum('bhts,bhsv->bhtv', s, vc) + w_inter[..., None] * jnp.einsum('bhvd,bhtd->bhtv', C, qc)
        den = jnp.sum(s, axis=-1) + w_inter * jnp.einsum('bhd,bhtd->bht', n, qc)
        h = num / jnp.maximum(jnp.abs(den), jnp.exp(-m_t))[..., None]
        m_new = m_t[..., -1]
        w_old = jnp.exp(b[..., -1] + m - m_new)
        w_s = jnp.exp(b[..., -1:] - b + li - m_new[..., None])
        C = w_old[..., None, None] * C + jnp.einsum('bhsv,bhsd->bhvd', vc * w_s[..., None], kc)
        n = w_old[..., None] * n + jnp.einsum('bhs,bhsd->bhd', w_s, kc)
        return (C, n, m_new), h

    init = (jnp.zeros((B, H, dv, dk), f32), jnp.zeros((B, H, dk), f32), jnp.zeros((B, H), f32))
    _, h = lax.scan(step, init, xs)
    return _from_chunks(h)

def stick_breaking(q, k, v):
    f32 = jnp.float32
    B, T, H, dh = q.shape
    scale = dh ** -0.5
    qf, kf, vf = q.astype(f32), k.astype(f32), v.astype(f32)
    outs = []
    for t0 in range(0, T, SB_BLOCK):
        t1 = t0 + SB_BLOCK
        z = jnp.einsum('bqhd,bkhd->bhqk', qf[:, t0:t1], kf[:, :t1]) * scale
        qpos = t0 + jnp.arange(SB_BLOCK)
        kpos = jnp.arange(t1)
        strict = kpos[None, :] < qpos[:, None]
        log_beta = jnp.where(strict, jax.nn.log_sigmoid(z), -jnp.inf)
        log_1m = jnp.where(strict, jax.nn.log_sigmoid(-z), 0.0)
        acc = lax.cumsum(log_1m, axis=3, reverse=True) - log_1m
        w = jnp.exp(log_beta + acc)
        outs.append(jnp.einsum('bhqk,bkhd->bqhd', w, vf[:, :t1]))
    return jnp.concatenate(outs, axis=1)

def short_conv(x, w):
    K = w.shape[0]
    T = x.shape[1]
    xp = jnp.pad(x, ((0, 0), (K - 1, 0), (0, 0)))
    return sum(xp[:, j:j + T] * w[j] for j in range(K))

def gated_deltanet(q, k, v, beta, log_alpha):
    f32 = jnp.float32
    B, T, H, dk = q.shape
    dv = v.shape[-1]
    L = GDN_CHUNK
    qc = _to_chunks(q.astype(f32) * (dk ** -0.5), L)
    kc = _to_chunks(k.astype(f32), L)
    vc = _to_chunks(v.astype(f32), L)
    bc = _to_chunks(beta.astype(f32), L)
    g = jnp.cumsum(_to_chunks(log_alpha.astype(f32), L), axis=-1)
    incl = jnp.tril(jnp.ones((L, L), dtype=bool))
    strict = jnp.tril(jnp.ones((L, L), dtype=bool), k=-1)
    decay = jnp.where(incl, jnp.exp(jnp.where(incl, g[..., :, None] - g[..., None, :], 0.0)), 0.0)
    kk = jnp.einsum('nbhtd,nbhsd->nbhts', kc, kc)
    lower = jnp.where(strict, bc[..., :, None] * kk * decay, 0.0)
    eye = jnp.eye(L, dtype=f32)
    rhs = jnp.concatenate([vc * bc[..., None], kc * (bc * jnp.exp(g))[..., None]], axis=-1)
    sol = lax.linalg.triangular_solve(lower + eye, rhs, left_side=True, lower=True, unit_diagonal=True)
    u_c, w_c = sol[..., :dv], sol[..., dv:]
    attn = jnp.einsum('nbhtd,nbhsd->nbhts', qc, kc) * decay
    q_dec = qc * jnp.exp(g)[..., None]
    g_last = g[..., -1]
    k_dec = kc * jnp.exp(g_last[..., None] - g)[..., None]

    def step(S, inp):
        u, wk, att, qd, kd, gl = inp
        v_new = u - jnp.einsum('bhtk,bhkv->bhtv', wk, S)
        o = jnp.einsum('bhtk,bhkv->bhtv', qd, S) + jnp.einsum('bhts,bhsv->bhtv', att, v_new)
        S = S * jnp.exp(gl)[..., None, None] + jnp.einsum('bhsk,bhsv->bhkv', kd, v_new)
        return S, o

    S0 = jnp.zeros((B, H, dk, dv), f32)
    _, o = lax.scan(step, S0, (u_c, w_c, attn, q_dec, k_dec, g_last))
    return _from_chunks(o)

def ab_mixer(h, w_in, b_i, b_f, head_gain, w_out):
    B, T, _ = h.shape
    mq, mk, mv, mo, mi, mf, sq, sk, sv = _split(h @ w_in, AB_SIZES)
    hm = mlstm(mq.reshape(B, T, MLSTM_HEADS, MLSTM_DQK),
               mk.reshape(B, T, MLSTM_HEADS, MLSTM_DQK),
               mv.reshape(B, T, MLSTM_HEADS, MLSTM_DV),
               mi + b_i, mf + b_f)
    hm = rmsnorm(hm, head_gain) * jax.nn.sigmoid(mo.reshape(B, T, MLSTM_HEADS, MLSTM_DV).astype(jnp.float32))
    hs = stick_breaking(sq.reshape(B, T, SB_HEADS, SB_DH),
                        sk.reshape(B, T, SB_HEADS, SB_DH),
                        sv.reshape(B, T, SB_HEADS, SB_DH))
    out = jnp.concatenate([hm.reshape(B, T, ML_V), hs.reshape(B, T, SB_W)], axis=-1).astype(h.dtype)
    return out @ w_out

def c_mixer(h, w_in, conv_w, a_log, dt_bias, head_gain, w_out):
    B, T, _ = h.shape
    qkv, gate, b, a = _split(h @ w_in, C_SIZES)
    qkv = jax.nn.silu(short_conv(qkv, conv_w))
    q, k, v = _split(qkv, (GDN_QK, GDN_QK, GDN_VW))
    q = l2norm(q.reshape(B, T, GDN_HEADS, GDN_DK))
    k = l2norm(k.reshape(B, T, GDN_HEADS, GDN_DK))
    v = v.reshape(B, T, GDN_HEADS, GDN_DV)
    beta = jax.nn.sigmoid(b.astype(jnp.float32))
    log_alpha = -jnp.exp(a_log.astype(jnp.float32)) * jax.nn.softplus(a.astype(jnp.float32) + dt_bias.astype(jnp.float32))
    o = gated_deltanet(q, k, v, beta, log_alpha)
    o = rmsnorm(o, head_gain) * jax.nn.silu(gate.reshape(B, T, GDN_HEADS, GDN_DV).astype(jnp.float32))
    return o.reshape(B, T, GDN_VW).astype(h.dtype) @ w_out

def mem_cross_attn(h, memn, wq, wk, wv, wo):
    B, T, _ = h.shape
    M = memn.shape[1]
    q = (h @ wq).reshape(B, T, XA_HEADS, XA_DH)
    k = (memn @ wk).reshape(B, M, XA_HEADS, XA_DH)
    v = (memn @ wv).reshape(B, M, XA_HEADS, XA_DH)
    s = jnp.einsum('bthd,bmhd->bhtm', q, k).astype(jnp.float32) * (XA_DH ** -0.5)
    p = jax.nn.softmax(s, axis=-1).astype(v.dtype)
    o = jnp.einsum('bhtm,bmhd->bthd', p, v).reshape(B, T, XA_HEADS * XA_DH)
    return o @ wo

def sq_relu_mlp(h, w1, w2):
    return jnp.square(jax.nn.relu(h @ w1)) @ w2

def second_inputs(seed: int = 0) -> dict:
    key = jax.random.key(seed)
    ks = jax.random.split(key, 32)
    f32 = jnp.float32

    def w(k, shape, fan_in):
        return jax.random.normal(k, shape, f32) * (fan_in ** -0.5)

    def gain(k, shape):
        return 1.0 + 0.02 * jax.random.normal(k, shape, f32)

    x = jax.random.normal(ks[0], (BATCH, SEQ, D_MODEL), f32)
    mem = jax.random.normal(ks[1], (BATCH, MEM_LEN, D_MODEL), f32)
    mix_norm = gain(ks[2], (DEPTH_2, D_MODEL))
    ab_w_in = w(ks[3], (N_EVEN, D_MODEL, AB_IN), D_MODEL)
    ab_b_i = 0.1 * jax.random.normal(ks[4], (N_EVEN, MLSTM_HEADS), f32)
    ab_b_f = jnp.linspace(3.0, 6.0, MLSTM_HEADS, dtype=f32)[None, :] + 0.1 * jax.random.normal(ks[5], (N_EVEN, MLSTM_HEADS), f32)
    ab_head_gain = gain(ks[6], (N_EVEN, MLSTM_HEADS, MLSTM_DV))
    ab_w_out = w(ks[7], (N_EVEN, AB_OUT, D_MODEL), AB_OUT)
    c_w_in = w(ks[8], (N_ODD, D_MODEL, C_IN), D_MODEL)
    c_conv_w = w(ks[9], (N_ODD, GDN_CONV, GDN_CONV_CH), GDN_CONV)
    c_a_log = jnp.log(jax.random.uniform(ks[10], (N_ODD, GDN_HEADS), f32, 1.0, 16.0))
    dt = jnp.exp(jax.random.uniform(ks[11], (N_ODD, GDN_HEADS), f32, float(np.log(1e-3)), float(np.log(1e-1))))
    c_dt_bias = dt + jnp.log(-jnp.expm1(-dt))
    c_head_gain = gain(ks[12], (N_ODD, GDN_DV))
    c_w_out = w(ks[13], (N_ODD, GDN_VW, D_MODEL), GDN_VW)
    xa_norm = gain(ks[14], (DEPTH_2, D_MODEL))
    mem_norm = gain(ks[15], (D_MODEL,))
    xa_wq = w(ks[16], (DEPTH_2, D_MODEL, D_MODEL), D_MODEL)
    xa_wk = w(ks[17], (DEPTH_2, D_MODEL, D_MODEL), D_MODEL)
    xa_wv = w(ks[18], (DEPTH_2, D_MODEL, D_MODEL), D_MODEL)
    xa_wo = w(ks[19], (DEPTH_2, D_MODEL, D_MODEL), D_MODEL)
    mlp_norm = gain(ks[20], (DEPTH_2, D_MODEL))
    mlp_w1 = w(ks[21], (DEPTH_2, D_MODEL, D_FF_2), D_MODEL)
    mlp_w2 = w(ks[22], (DEPTH_2, D_FF_2, D_MODEL), D_FF_2)
    final_norm = gain(ks[23], (D_MODEL,))
    return {'x': x, 'mem': mem, 'mix_norm': mix_norm,
            'ab_w_in': ab_w_in, 'ab_b_i': ab_b_i, 'ab_b_f': ab_b_f,
            'ab_head_gain': ab_head_gain, 'ab_w_out': ab_w_out,
            'c_w_in': c_w_in, 'c_conv_w': c_conv_w, 'c_a_log': c_a_log,
            'c_dt_bias': c_dt_bias, 'c_head_gain': c_head_gain, 'c_w_out': c_w_out,
            'xa_norm': xa_norm, 'mem_norm': mem_norm, 'xa_wq': xa_wq, 'xa_wk': xa_wk,
            'xa_wv': xa_wv, 'xa_wo': xa_wo, 'mlp_norm': mlp_norm, 'mlp_w1': mlp_w1,
            'mlp_w2': mlp_w2, 'final_norm': final_norm}

def second_block(x, mem, mix_norm, ab_w_in, ab_b_i, ab_b_f, ab_head_gain, ab_w_out,
              c_w_in, c_conv_w, c_a_log, c_dt_bias, c_head_gain, c_w_out,
              xa_norm, mem_norm, xa_wq, xa_wk, xa_wv, xa_wo,
              mlp_norm, mlp_w1, mlp_w2, final_norm):
    memn = rmsnorm(mem, mem_norm)
    for l in range(DEPTH_2):
        j = l // 2
        h = rmsnorm(x, mix_norm[l])
        if l % 2 == 0:
            x = x + ab_mixer(h, ab_w_in[j], ab_b_i[j], ab_b_f[j], ab_head_gain[j], ab_w_out[j])
        else:
            x = x + c_mixer(h, c_w_in[j], c_conv_w[j], c_a_log[j], c_dt_bias[j], c_head_gain[j], c_w_out[j])
        x = x + mem_cross_attn(rmsnorm(x, xa_norm[l]), memn, xa_wq[l], xa_wk[l], xa_wv[l], xa_wo[l])
        x = x + sq_relu_mlp(rmsnorm(x, mlp_norm[l]), mlp_w1[l], mlp_w2[l])
    return rmsnorm(x, final_norm)


def setup_inputs(seed=0):
    out = dict(first_inputs(seed))
    for name, value in second_inputs(seed + 1).items():
        if name != "x":
            out[name + "_2"] = value
    return out


def reference(
    x, p, ln_mix, w_in, qk_gain, lam_params, subln_gain, fgate_bias, rel_bias, w_out, ln_ffn,
    w_up, conv_w, conv_b, w_down, ln_ple, w_ple_gate, w_ple_proj, mem_2, mix_norm_2, ab_w_in_2,
    ab_b_i_2, ab_b_f_2, ab_head_gain_2, ab_w_out_2, c_w_in_2, c_conv_w_2, c_a_log_2,
    c_dt_bias_2, c_head_gain_2, c_w_out_2, xa_norm_2, mem_norm_2, xa_wq_2, xa_wk_2, xa_wv_2,
    xa_wo_2, mlp_norm_2, mlp_w1_2, mlp_w2_2, final_norm_2,
):
    x = first_block(
        x, p, ln_mix, w_in, qk_gain, lam_params, subln_gain, fgate_bias, rel_bias, w_out,
        ln_ffn, w_up, conv_w, conv_b, w_down, ln_ple, w_ple_gate, w_ple_proj,
    )
    return second_block(
        x, mem_2, mix_norm_2, ab_w_in_2, ab_b_i_2, ab_b_f_2, ab_head_gain_2, ab_w_out_2,
        c_w_in_2, c_conv_w_2, c_a_log_2, c_dt_bias_2, c_head_gain_2, c_w_out_2, xa_norm_2,
        mem_norm_2, xa_wq_2, xa_wk_2, xa_wv_2, xa_wo_2, mlp_norm_2, mlp_w1_2, mlp_w2_2,
        final_norm_2,
    )


_drawn_inputs = setup_inputs


def setup_inputs(seed=0):
    import zlib

    import numpy as np

    out = dict(_drawn_inputs(seed))
    spreads = {}
    factors = {'rel_bias': 5.333,
     'conv_b': 3.318,
     'ln_ple': 5.499,
     'mix_norm_2': 3.103,
     'ab_b_i_2': 8.0,
     'ab_head_gain_2': 8.0,
     'c_head_gain_2': 8.0,
     'xa_norm_2': 8.0,
     'mem_norm_2': 8.0,
     'mlp_norm_2': 2.761,
     'final_norm_2': 2.856}
    for name, (base, spread) in spreads.items():
        noise = np.random.default_rng([zlib.crc32(name.encode()), seed]).standard_normal(out[name].shape)
        drawn = base * np.exp(spread * noise) if base else spread * noise
        out[name] = jnp.asarray(drawn.astype(out[name].dtype))
    for name, factor in factors.items():
        out[name] = (out[name] * factor).astype(out[name].dtype)
    return out
```

```python
from contextlib import ExitStack

import concourse.bass as bass
from concourse import mybir

P = 128
T = 256
TT = T // P
D = 1024
DC = D // P
EPS = 1e-6
BIG = 1e30
RING = 8
UNIT = 2048

F32 = mybir.dt.float32
ALU = mybir.AluOpType
ACT = mybir.ActivationFunctionType
AX = mybir.AxisListType

LN_MIX, LN_FFN, LN_PLE, LN_MEM, LN_MIX0, LN_XA0, LN_MLP0, LN_MIX1, LN_XA1, LN_MLP1 = range(10)
ROW_SUBLN, ROW_ABHEAD, ROW_CHEAD, ROW_LAM, ROW_FINAL, ROW_LEN = 0, 64, 576, 704, 960, 1984

D_FF = 2816
FF_TILES = D_FF // P
D_FF_2 = 4096
FF2_TILES = D_FF_2 // P
LAM_INIT = 0.2


def weight_plan():
    plan = []

    def cols(stage, w, starts):
        plan.extend((stage, w, "cols", c) for c in starts)

    def rows(stage, w, chunks, c0=0, width=D):
        per = UNIT // width
        for k in range(0, chunks, per):
            plan.append((stage, w, "rows", (k, min(per, chunks - k), c0, width)))

    cols("qk", "w_in", range(0, 2560, 256))
    rows("v", "w_in", DC, 2560)
    rows("w_out", "w_out", DC)
    for j in range(D_FF // 256):
        cols("up", "w_up", (256 * j, D_FF + 256 * j))
    rows("down", "w_down", FF_TILES)
    rows("ple_gate", "w_ple_gate", DC)
    rows("ple_proj", "w_ple_proj", 2)
    cols("ab_qk", "ab_w_in", range(0, 1536, 256))
    rows("ab_vo", "ab_w_in", DC, 1536)
    rows("ab_sv", "ab_w_in", DC, 2560, 512)
    rows("ab_out", "ab_w_out", DC)
    for l in range(2):
        if l:
            cols("c_qkv", "c_w_in", range(0, 3072, 256))
            rows("c_gate", "c_w_in", DC, 3072)
            rows("c_out", "c_w_out", DC)
        cols(f"xk{l}", f"xa_wk{l}", range(0, D, 256))
        rows(f"xv{l}", f"xa_wv{l}", DC)
        cols(f"xq{l}", f"xa_wq{l}", range(0, D, 256))
        rows(f"xo{l}", f"xa_wo{l}", DC)
        cols(f"m1{l}", f"mlp_w1{l}", range(0, D_FF_2, 256))
        rows(f"m2{l}", f"mlp_w2{l}", FF2_TILES)
    return plan


def build_two_blocks(nc, I, out, scratch, stop=None):
    plan = weight_plan()
    first_unit = {}
    for n, (stage, *_r) in enumerate(plan):
        first_unit.setdefault(stage, n)

    with ExitStack() as ctx:
        def sb(name, shape):
            return ctx.enter_context(nc.sbuf_tensor(name, shape, F32))

        def sem(name):
            return ctx.enter_context(nc.semaphore(name))

        X = sb("resid", [P, TT, D])
        HN = sb("normed", [P, TT, D])
        HT = sb("normed_t", [P, DC, T])
        MEMT = sb("mem_t", [P, DC, T])
        ring = sb("ring", [P, RING, UNIT])
        arena = sb("arena", [P, 84 * 256])
        ident = sb("ident", [P, P])
        ones = sb("ones", [P, P])
        halves = sb("halves", [P, P])
        tri = sb("tri", [P, P])
        sel = sb("sel", [8, 8, P])
        neg_ge = sb("neg_ge", [P, 3, P])
        neg_gt = sb("neg_gt", [P, 3, P])
        ln_cols = sb("ln_cols", [P, 10, DC])
        qk_cols = sb("qk_cols", [P, 6])
        qk_fold = sb("qk_fold", [P, 6])
        row = sb("row", [P, ROW_LEN])
        conv_cols = sb("conv_cols", [P, 2 * FF_TILES, 4])
        cconv_cols = sb("cconv_cols", [P, 24, 4])
        gate_w = sb("gate_w", [P, DC, 30])
        gate_p = sb("gate_p", [8, 5])
        stat = sb("stat", [P, 2])
        lnv = sb("lnv", [P, 2])
        rstd = sb("rstd", [P, 2])
        eps_c = sb("eps_c", [P, 1])
        eps64_c = sb("eps64_c", [P, 1])
        one_c = sb("one_c", [P, 1])
        lam = sb("lam", [P, 8])
        PS = ctx.enter_context(nc.psum_tensor("ps", [P, 8, 512], F32))
        G, A = 0, 4

        def view(first, shape, parts=P):
            n = 1
            for s in shape:
                n *= s
            v = arena[0:parts, first:first + n]
            if len(shape) == 1:
                return v
            names = "abcd"[:len(shape)]
            spec = {c: s for c, s in zip(names, shape)}
            return v.rearrange(f"p ({' '.join(names)}) -> p {' '.join(names)}", **spec)

        s_x_in = sem("x_loaded")
        s_small = sem("small_loaded")
        s_const = sem("constants_built")
        s_pool_chain = sem("pool_chain")
        s_act_chain = sem("act_chain")
        s_dve_chain = sem("dve_chain")
        s_unit = [sem(f"unit_landed_{i}") for i in range(RING)]
        s_unit_used = sem("unit_used")
        s_x = sem("resid_ready")
        s_stat = sem("norm_squares")
        s_rstd = sem("norm_rstd")
        s_hn0 = sem("normed_tile0")
        s_hn1 = sem("normed_tile1")
        s_tp = sem("transposed")
        s_tpd = sem("turned_by_dve")
        s_tpa = sem("turned_by_act")
        s_acc = sem("rows_product_done")
        s_out = sem("out_stored")

        S = {}

        def named(name):
            if name not in S:
                S[name] = sem(name)
            return S[name]

        chain_n = {"act": 0, "dve": 0, "pool": 0}

        def act_then(ins):
            chain_n["act"] += 1
            ins.then_inc(s_act_chain, 1)
            nc.scalar.wait_ge(s_act_chain, chain_n["act"])

        def dve_then(ins):
            chain_n["dve"] += 1
            ins.then_inc(s_dve_chain, 1)
            nc.vector.wait_ge(s_dve_chain, chain_n["dve"])

        def pool_then(ins):
            chain_n["pool"] += 1
            ins.then_inc(s_pool_chain, 1)
            nc.gpsimd.wait_ge(s_pool_chain, chain_n["pool"])

        dve, act, pool, pe = nc.vector, nc.scalar, nc.gpsimd, nc.tensor

        def weights_sp(sp):
            for n, (stage, w, kind, at) in enumerate(plan):
                if stop and n >= stop_unit:
                    break
                slot = n % RING
                if n >= RING:
                    sp.wait_ge(s_unit_used, n - RING + 1)
                W = I[w]
                if kind == "cols":
                    dst = ring[:, slot, :].rearrange("p (c n) -> p c n", c=DC)
                    src = W[:, at:at + 256].rearrange("(c p) n -> p c n", p=P)
                else:
                    k, per, c0, width = at
                    dst = ring[:, slot, 0:per * width].rearrange("p (c n) -> p c n", c=per)
                    src = W[k * P:(k + per) * P, c0:c0 + width].rearrange("(c p) n -> p c n", p=P)
                sp.dma_start(dst, src).then_inc(s_unit[slot], 16)

        def landed(n):
            pe.wait_ge(s_unit[n % RING], 16 * (n // RING + 1))

        def cols_unit(stage, u, rhs, bank, free=None, ready=None):
            n = first_unit[stage] + u
            landed(n)
            if free:
                free(u)
            w = ring[:, n % RING, :].rearrange("p (c n) -> p c n", c=DC)
            for f in range(2):
                for k in range(DC):
                    if ready and u == 0 and f == 0:
                        ready(k)
                    mm = pe.matmul(PS[:, bank, f * T:(f + 1) * T], w[:, k, f * P:(f + 1) * P],
                                   rhs[:, k, :], start=(k == 0), stop=(k == DC - 1))
            mm.then_inc(s_unit_used, 1)
            return mm

        def cols_done(eng, stage, u):
            eng.wait_ge(s_unit_used, first_unit[stage] + u + 1)

        ROWS = {}
        acc = 0
        for stage, width in (("v", D), ("w_out", D), ("down", D), ("ple_gate", D), ("ple_proj", D), ("ab_vo", D),
                             ("ab_sv", 512), ("ab_out", D), ("xv0", D), ("xo0", D), ("m20", D), ("c_gate", D),
                             ("c_out", D), ("xv1", D), ("xo1", D), ("m21", D)):
            banks = TT * width // 512
            last = max(n for n, x in enumerate(plan) if x[0] == stage)
            ROWS[stage] = (banks, acc, last)
            acc += banks - 1

        def rows_done(eng, stage, b):
            banks, before, last = ROWS[stage]
            if b < banks - 1:
                eng.wait_ge(s_acc, before + b + 1)
            else:
                eng.wait_ge(s_unit_used, last + 1)

        def rows_product(stage, lhs, chunks, width=D, base=G, ready=None, free=None):
            per = UNIT // width
            nb = width // 512
            for u in range(-(-chunks // per)):
                n = first_unit[stage] + u
                landed(n)
                w = ring[:, n % RING, :].rearrange("p (c n) -> p c n", c=per)
                for kk in range(min(per, chunks - u * per)):
                    k = u * per + kk
                    if ready:
                        ready(k)
                    if k == 0 and free:
                        free()
                    for t in range(TT):
                        for b in range(nb):
                            mm = pe.matmul(PS[:, base + nb * t + b, :], lhs[:, k, t * P:(t + 1) * P],
                                           w[:, kk, b * 512:(b + 1) * 512],
                                           start=(k == 0), stop=(k == chunks - 1))
                            if k == chunks - 1 and not (t == TT - 1 and b == nb - 1):
                                mm.then_inc(s_acc, 1)
                mm.then_inc(s_unit_used, 1)

        def norm_dve(i, src, ready):
            ready(dve)
            dve.tensor_tensor_reduce(out=HN[:, 0, :], in0=src[:, 0, :], in1=src[:, 0, :], scale=1.0, scalar=0.0,
                                     op0=ALU.mult, op1=ALU.add, accum_out=stat[:, 0:1]).then_inc(s_stat, 1)
            dve.wait_ge(s_rstd, i + 1)
            dve.tensor_scalar(HN[:, 0, :], src[:, 0, :], rstd[:, 0:1], None, ALU.mult).then_inc(s_hn0, 1)

        def norm_act(i, src, ready):
            ready(act)
            act.activation(HN[:, 1, :], src[:, 1, :], ACT.Square, accum_out=stat[:, 1:2]).then_inc(s_stat, 1)
            act.wait_ge(s_stat, 2 * (i + 1))
            act_then(act.activation(lnv[:, :], stat[:, :], ACT.Ln, bias=eps_c[:, 0:1], scale=1.0 / D))
            act.activation(rstd[:, :], lnv[:, :], ACT.Exp, scale=-0.5).then_inc(s_rstd, 1)
            act.wait_ge(s_rstd, i + 1)
            act.activation(HN[:, 1, :], src[:, 1, :], ACT.Copy, scale=rstd[:, 1:2]).then_inc(s_hn1, 1)

        def turn_pe(m, src, ready, free=None):
            if free:
                free()
            for c2 in range(4):
                for c in (2 * c2, 2 * c2 + 1):
                    for t in range(TT):
                        if c2 == 0:
                            ready(t)
                        mm = pe.transpose(PS[:, A + c2, (c % 2) * T + t * P:(c % 2) * T + (t + 1) * P],
                                          src[:, t, c * P:(c + 1) * P], ident[:, :])
                mm.then_inc(s_tp, 1)

        def turn_dve(m, dst, gain=None):
            for c2 in (0, 2):
                dve.wait_ge(s_tp, 4 * m + c2 + 1)
                o = dst[:, 2 * c2:2 * c2 + 2, :]
                i = PS[:, A + c2, :].rearrange("p (c n) -> p c n", c=2)
                if gain is None:
                    dve.tensor_copy(o, i).then_inc(s_tpd, 1)
                else:
                    g = ln_cols[:, gain, 2 * c2:2 * c2 + 2].unsqueeze(2).to_broadcast([P, 2, T])
                    dve.tensor_tensor(o, i, g, ALU.mult).then_inc(s_tpd, 1)

        def turn_act(m, dst, gain=None):
            for c2 in (1, 3):
                act.wait_ge(s_tp, 4 * m + c2 + 1)
                if gain is None:
                    act.activation(dst[:, 2 * c2:2 * c2 + 2, :], PS[:, A + c2, :].rearrange("p (c n) -> p c n", c=2),
                                   ACT.Copy).then_inc(s_tpa, 1)
                else:
                    for c in (0, 1):
                        ins = act.activation(dst[:, 2 * c2 + c, :], PS[:, A + c2, c * T:(c + 1) * T], ACT.Copy,
                                             scale=ln_cols[:, gain, 2 * c2 + c:2 * c2 + c + 1])
                    ins.then_inc(s_tpa, 1)

        def turned(m, eng):
            def ready(k):
                if k == 0:
                    eng.wait_ge(s_tpd, 2 * m + 1)
                elif k == 2:
                    eng.wait_ge(s_tpa, 2 * m + 1)
                elif k == 4:
                    eng.wait_ge(s_tpd, 2 * m + 2)
                elif k == 6:
                    eng.wait_ge(s_tpa, 2 * m + 2)
            return ready

        def norm_ready_pe(i):
            def ready(t):
                pe.wait_ge((s_hn0, s_hn1)[t], i + 1)
            return ready

        def resid(r):
            def ready(eng):
                if r:
                    eng.wait_ge(s_x, 4 * r)
                else:
                    eng.wait_ge(s_x_in, 16)
            return ready

        def resid_add_dve(stage):
            for b in range(4):
                rows_done(dve, stage, b)
                x = X[:, b // 2, (b % 2) * 512:(b % 2 + 1) * 512]
                dve.tensor_tensor(x, PS[:, G + b, :], x, ALU.add).then_inc(s_x, 1)

        MEM = view(60 * 256, (TT, D))
        relrow = view(80 * 256 + 128, (257,), 6)
        relext = view(82 * 256, (511,), 6)
        qkT = view(0, (20, T))
        V1 = view(20 * 256, (TT, D))
        OM = view(28 * 256, (TT, D))
        BT = view(36 * 256, (11, T))
        SN = view(47 * 256, (3, T))
        PT = view(50 * 256, (3, T))
        SQ = view(53 * 256, (2, 512))
        RS = view(57 * 256, (2, 512))
        FG = view(61 * 256, (8, T), 8)
        FL = view(69 * 256, (T,), 102)
        FR = view(70 * 256, (6, T), 102)
        MN = view(76 * 256, (40,))
        LS = view(76 * 256 + 40, (40,))
        RL = view(76 * 256 + 80, (40,))
        OD = view(77 * 256, (2, 64))
        DSQ = view(78 * 256, (8, 64))
        DST = view(80 * 256, (3, 8))

        N_SMALL = 10

        def small_sp(sp):
            sp.dma_start(MEM, I["mem"].rearrange("(t p) d -> p t d", p=P)).then_inc(s_mem, 16)
            sp.dma_start(X[:, :, :], I["x"].rearrange("(t p) d -> p t d", p=P)).then_inc(s_x_in, 16)
            for dst, src in ((ln_cols[:, :, :], I["ln_cols"].rearrange("p (a b) -> p a b", a=10)),
                             (qk_cols[:, :], I["qk_cols"]),
                             (gate_p[:, :], I["gate_p"]),
                             (relrow[:, :], I["rel_rev"]),
                             (row[:, :], I["row"].to_broadcast([P, ROW_LEN])),
                             (conv_cols[:, :, :], I["conv_cols"].rearrange("p (a b) -> p a b", b=4)),
                             (cconv_cols[:, :, :], I["cconv_cols"].rearrange("p (a b) -> p a b", b=4)),
                             (gate_w[:, :, :], I["gate_w"].rearrange("(c p) n -> p c n", p=P)),
                             (PIN, I["p"].rearrange("(t p) d -> p t d", p=P))):
                sp.dma_start(dst, src).then_inc(s_small, 16)

        N_SMALL = 9
        PIN_t = sb("p_in", [P, TT, 256])
        PIN = PIN_t[:, :, :]
        s_mem = sem("mem_loaded")

        def consts_pool():
            sel_ge = ALU.is_ge
            pool_then(pool.memset(ident[:, :], 0.0))
            pool_then(pool.affine_select(out=ident[:, :], in_=ident[:, :], compare_op=ALU.not_equal, fill=1.0,
                                         base=0, pattern=[[-1, P]], channel_multiplier=1))
            pool.memset(ones[:, :], 1.0)
            pool.memset(eps_c[:, :], EPS)
            pool.memset(eps64_c[:, :], 64 * EPS)
            pool_then(pool.memset(one_c[:, :], 1.0))
            pool.sem_inc(s_const, 1)
            pool.memset(halves[:, :], 0.0)
            pool.memset(tri[:, :], 1.0)
            pool.memset(sel[:, :, :], 0.0)
            pool.memset(neg_ge[:, :, :], 0.0)
            pool_then(pool.memset(neg_gt[:, :, :], 0.0))
            pool_then(pool.memset(halves[0:64, 0:64], 1.0))
            pool_then(pool.memset(halves[64:128, 64:128], 1.0))
            pool.affine_select(out=tri[:, :], in_=tri[:, :], compare_op=sel_ge, fill=0.0, base=0,
                               pattern=[[-1, P]], channel_multiplier=1)
            pool.affine_select(out=sel[:, :, :], in_=sel[:, :, :], compare_op=ALU.not_equal, fill=1.0, base=0,
                               pattern=[[-1, 8], [0, P]], channel_multiplier=1)
            for b in (0, 2):
                pool.affine_select(out=neg_gt[:, b, :], in_=neg_gt[:, b, :], compare_op=sel_ge, fill=-BIG,
                                   base=-1, pattern=[[1, P]], channel_multiplier=-1)
                last = pool.affine_select(out=neg_ge[:, b, :], in_=neg_ge[:, b, :], compare_op=sel_ge, fill=-BIG,
                                          base=0, pattern=[[1, P]], channel_multiplier=-1)
            pool_then(last)
            pool.sem_inc(s_const, 1)
            pool.iota(BT[:, 0, :], pattern=[[-1, T]], base=P, channel_multiplier=1,
                      allow_small_or_imprecise_dtypes=True).then_inc(named("dist"), 1)
            pool_then(pool.memset(BT[:, 4, :], 0.0))
            pool.affine_select(out=BT[:, 4, :], in_=BT[:, 4, :], compare_op=sel_ge, fill=BIG, base=P,
                               pattern=[[-1, T]], channel_multiplier=1).then_inc(named("causal"), 1)
            pool.wait_ge(named("relext"), 1)
            pool.dma_start(scratch[:, :, :], relext[:, :].unsqueeze(1).to_broadcast([6, P, 511])
                           ).then_inc(named("rel_out"), 16)
            pool.wait_ge(named("rel_out"), 16)
            for h in range(6):
                src = bass.AP(scratch.tensor, h * P * 511 + 127, [[510, P], [1, T]])
                pool.dma_start(BT[:, 5 + h, :], src).then_inc(named("rel_in"), 16)

        def biases_dve():
            dve.wait_ge(s_small, 16 * N_SMALL)
            dve.tensor_copy(relext[:, 127:384], relrow[:, :])
            dve.tensor_copy(relext[:, 0:127], relrow[:, 0:1].to_broadcast([6, 127]))
            dve_then(dve.tensor_copy(relext[:, 384:511], relrow[:, 256:257].to_broadcast([6, 127])))
            dve.sem_inc(named("relext"), 1)
            r = row[:, ROW_LAM:ROW_LAM + 256].rearrange("p (a n) -> p a n", a=4)
            for j in range(2):
                dve.tensor_tensor_reduce(out=HN[:, 0, 64 * j:64 * j + 64], in0=r[:, 2 * j, :], in1=r[:, 2 * j + 1, :],
                                         scale=1.0, scalar=0.0, op0=ALU.mult, op1=ALU.add,
                                         accum_out=lam[:, j:j + 1]).then_inc(named("lam_dots"), 1)
            dve.wait_ge(named("lam_exp"), 1)
            dve_then(dve.tensor_tensor(lam[:, 4:5], lam[:, 3:4], lam[:, 2:3], ALU.subtract))
            dve_then(dve.tensor_scalar(lam[:, 5:6], lam[:, 4:5], -LAM_INIT, None, ALU.add))
            for j in range(6):
                dve.tensor_scalar(qk_fold[:, j:j + 1], qk_cols[:, j:j + 1], (-1.0, 8.0)[j % 2], None, ALU.mult)
            dve_then(dve.tensor_scalar(row[:, ROW_SUBLN:ROW_SUBLN + 64], row[:, ROW_SUBLN:ROW_SUBLN + 64],
                                       1.0 - LAM_INIT, None, ALU.mult))
            dve.wait_ge(named("dist"), 1)
            for h in (1, 2, 3, 0):
                slope = 2.0 ** (-2.0 * (h + 1))
                dve_then(dve.tensor_scalar(BT[:, h, :], BT[:, 0, :], slope, None, ALU.mult))
            dve_then(dve.scalar_tensor_tensor(out=BT[:, 0:4, :], in0=BT[:, 0:4, :], scalar=-1.0, in1=BT[:, 0:4, :],
                                              op0=ALU.mult, op1=ALU.max))
            dve.wait_ge(named("rel_in"), 16 * 6)
            dve_then(dve.tensor_scalar(BT[:, 5:11, :], BT[:, 5:11, :], -1.0, None, ALU.mult))
            dve.memset(BT[0:64, 0:4, 192:256], BIG)
            dve_then(dve.memset(BT[0:64, 5:11, 192:256], BIG))

        def lam_act():
            act.wait_ge(named("lam_dots"), 2)
            act.activation(lam[:, 2:4], lam[:, 0:2], ACT.Exp).then_inc(named("lam_exp"), 1)

        QGAIN = [0] * 4 + [1] * 4 + [2] * 3 + [3] * 3 + [4] * 3 + [5] * 3

        def qk_pe():
            def free(u):
                if u >= 4:
                    pe.wait_ge(named("qk_done"), 2 * (u - 3))

            def squares(u):
                pe.wait_ge(named("qk_sq"), u + 1)
                if u >= 2:
                    pe.wait_ge(named("qk_rs"), u - 1)
                elif u == 0:
                    pe.wait_ge(s_const, 2)
                    pe.wait_ge(s_tpd, 2 * 2)
                    pe.wait_ge(s_tpa, 2 * 2)
                pe.matmul(PS[:, A + u % 2, :], halves[:, :], SQ[:, u % 2, :], start=True,
                          stop=True).then_inc(named("qk_ss"), 1)

            for u in range(10):
                cols_unit("qk", u, HT, G + u % 4, free, turned(1, pe))
                if u >= 1:
                    squares(u - 1)
            squares(9)

        def qk_act():
            for u in range(11):
                if u < 10:
                    cols_done(act, "qk", u)
                    if u >= 2:
                        act.wait_ge(named("qk_ss"), u - 1)
                    act.activation(SQ[:, u % 2, :], PS[:, G + u % 4, :], ACT.Square).then_inc(named("qk_sq"), 1)
                if u >= 1:
                    v = u - 1
                    act.wait_ge(named("qk_ss"), v + 1)
                    if v >= 2:
                        act.wait_ge(named("qk_done"), 2 * (v - 1))
                    act.activation(RS[:, v % 2, :], PS[:, A + v % 2, :], ACT.Ln,
                                   bias=eps64_c[:, 0:1]).then_inc(named("qk_rs"), 1)
                    act.wait_ge(named("qk_rs"), v + 1)
                    act.activation(RS[:, v % 2, :], RS[:, v % 2, :], ACT.Exp, scale=-0.5).then_inc(named("qk_rsx"), 1)

        def qk_dve():
            for u in range(10):
                dve.wait_ge(named("qk_rsx"), u + 1)
                for f in range(2):
                    j = QGAIN[2 * u + f]
                    dve.scalar_tensor_tensor(out=qkT[:, 2 * u + f, :], in0=PS[:, G + u % 4, f * T:(f + 1) * T],
                                             scalar=qk_fold[:, j:j + 1], in1=RS[:, u % 2, f * T:(f + 1) * T],
                                             op0=ALU.mult, op1=ALU.mult).then_inc(named("qk_done"), 1)

        def v_pe():
            rows_product("v", HT, DC, free=lambda: pe.wait_ge(named("qk_done"), 20))
            pe.wait_ge(named("qk_rs"), 10)
            for k in range(DC):
                mm = pe.matmul(PS[0:6, A, 0:T], gate_w[:, k, 0:6], HT[:, k, :], start=(k == 0), stop=(k == DC - 1))
            mm.then_inc(named("fg_raw"), 1)

        def v_act():
            for b in range(4):
                rows_done(act, "v", b)
                act.activation(V1[:, b // 2, (b % 2) * 512:(b % 2 + 1) * 512], PS[:, G + b, :],
                               ACT.Copy).then_inc(named("v1_ready"), 1)
            act.wait_ge(named("fg_z"), 1)
            act_then(act.activation(FG[0:6, 3, :], FG[0:6, 2, :], ACT.Exp))
            act.activation(FG[0:6, 4, :], FG[0:6, 3, :], ACT.Ln, bias=one_c[0:6, 0:1]).then_inc(named("fg_ln"), 1)

        def fg_dve():
            dve.wait_ge(named("fg_raw"), 1)
            dve_then(dve.tensor_scalar(FG[0:6, 0, :], PS[0:6, A, 0:T], gate_p[0:6, 0:1], None, ALU.add))
            dve_then(dve.tensor_scalar(FG[0:6, 1, :], FG[0:6, 0, :], 0.0, None, ALU.min))
            dve.scalar_tensor_tensor(out=FG[0:6, 2, :], in0=FG[0:6, 1, :], scalar=2.0, in1=FG[0:6, 0, :],
                                     op0=ALU.mult, op1=ALU.subtract).then_inc(named("fg_z"), 1)
            dve.memset(FL[:, :], 0.0)
            dve.memset(FR[:, :, :], 0.0)
            dve.wait_ge(named("fg_ln"), 1)
            dve_then(dve.tensor_tensor(FG[0:6, 5, :], FG[0:6, 1, :], FG[0:6, 4, :], ALU.subtract))
            dve_then(dve.tensor_tensor_scan(FG[0:6, 6, :], FG[0:6, 5, :], FG[0:6, 5, :], 0.0, ALU.add, ALU.bypass))
            for lo in (0, 64):
                dve.tensor_copy(FL[lo:lo + 6, :], FG[0:6, 6, :])
                dve.memset(FL[lo + 32:lo + 38, :], 1.0)
            for h in range(6):
                lo = 64 * (h % 2)
                dve.tensor_scalar(FR[lo:lo + 6, h, 0:P], sel[0:6, h, :], -1.0, None, ALU.mult)
                dve.tensor_scalar(FR[lo:lo + 6, h, P:T], sel[0:6, h, :], -1.0, None, ALU.mult)
                ins = dve.tensor_scalar(FR[lo + 32:lo + 38, h, :], FG[0:6, 6, :], sel[0:6, h, 0:1], None, ALU.mult)
            dve_then(ins)
            dve.sem_inc(named("fg_ready"), 1)

        HEADS = []
        for h in range(4):
            for j in range(2):
                HEADS.append((2 * j + h // 2, 4 + 2 * j + h // 2, h % 2, h, 64 * h, "diff", h, j))
        for h in range(6):
            HEADS.append((8 + h // 2, 11 + h // 2, h % 2, 4, 256 + 64 * h, "fox", h, 0))
        for h in range(6):
            HEADS.append((14 + h // 2, 17 + h // 2, h % 2, 5 + h, 640 + 64 * h, "chunk", h, 0))
        NA = 2 * len(HEADS)

        def attn_pe():
            def scores(n):
                qt, kt, half, _b, _v, kind, h, _j = HEADS[n // 2]
                t, nk = n % 2, P * (n % 2 + 1)
                lo = 64 * half
                if n == 0:
                    pe.wait_ge(named("qk_done"), 20)
                    pe.wait_ge(named("fg_ready"), 1)
                if n >= 2:
                    pe.wait_ge(named("at_max"), n - 1)
                mm = pe.matmul(PS[:, A + n % 2, 0:nk], qkT[lo:lo + 64, qt, t * P:(t + 1) * P],
                               qkT[lo:lo + 64, kt, 0:nk], start=True, stop=(kind != "fox"))
                if kind == "fox":
                    mm = pe.matmul(PS[:, A + n % 2, 0:nk], FL[lo:lo + 38, t * P:(t + 1) * P],
                                   FR[lo:lo + 38, h, 0:nk],
                                   start=False, stop=True)
                mm.then_inc(named("at_s"), 1)

            def turn(n):
                t = n % 2
                pe.wait_ge(named("at_exp"), n + 1)
                if n >= 2:
                    pe.wait_ge(named("at_pt"), n - 1)
                for b in range(t + 1):
                    mm = pe.transpose(PS[:, A + 2 + t, b * P:(b + 1) * P],
                                      SN[:, n % 3, b * P:(b + 1) * P], ident[:, :])
                mm.then_inc(named("at_tp"), 1)

            def weigh(n):
                v = HEADS[n // 2][4]
                t = n % 2
                pe.wait_ge(named("at_pt"), n + 1)
                if n == 0:
                    pe.wait_ge(named("v1_ready"), 4)
                if n >= 2:
                    pe.wait_ge(named("at_o"), n - 1)
                for b in range(t + 1):
                    mm = pe.matmul(PS[:, G + n % 2, 0:64], PT[:, n % 3, b * P:(b + 1) * P],
                                   V1[:, b, v:v + 64], start=(b == 0), stop=(b == t))
                mm.then_inc(named("at_pv"), 1)

            for n in range(NA + 2):
                if n < NA:
                    scores(n)
                if 1 <= n <= NA:
                    turn(n - 1)
                if n >= 2:
                    weigh(n - 2)

        def attn_act():
            for n in range(NA + 1):
                if n < NA:
                    nk = P * (n % 2 + 1)
                    act.wait_ge(named("at_max"), n + 1)
                    act.activation(SN[:, n % 3, 0:nk], SN[:, n % 3, 0:nk], ACT.Exp, bias=MN[:, n:n + 1], scale=-1.0,
                                   accum_out=LS[:, n:n + 1]).then_inc(named("at_exp"), 1)
                if n >= 1:
                    m = n - 1
                    nk = P * (m % 2 + 1)
                    act.wait_ge(named("at_tp"), m + 1)
                    if m >= 3:
                        act.wait_ge(named("at_pv"), m - 2)
                    act.activation(PT[:, m % 3, 0:nk], PS[:, A + 2 + m % 2, 0:nk],
                                   ACT.Copy).then_inc(named("at_pt"), 1)

        def attn_dve():
            def low(n):
                bias = HEADS[n // 2][3]
                t, nk = n % 2, P * (n % 2 + 1)
                dve.wait_ge(named("at_s"), n + 1)
                if n == 8 * 2:
                    dve.wait_ge(named("causal"), 1)
                if n >= 3:
                    dve.wait_ge(named("at_tp"), n - 2)
                dve.tensor_tensor_reduce(out=SN[:, n % 3, 0:nk], in0=PS[:, A + n % 2, 0:nk],
                                         in1=BT[:, bias, T - nk:T], scale=1.0, scalar=3.0e38, op0=ALU.add,
                                         op1=ALU.min, accum_out=MN[:, n:n + 1]).then_inc(named("at_max"), 1)

            def finish(n):
                _q, _k, _half, _b, v, kind, h, j = HEADS[n // 2]
                t = n % 2
                dve.wait_ge(named("at_exp"), n + 1)
                dve_then(dve.reciprocal(RL[:, n:n + 1], LS[:, n:n + 1]))
                o = PS[:, G + n % 2, 0:64]
                if kind == "diff" and j == 0:
                    dve.wait_ge(named("at_pv"), n + 1)
                    dve_then(dve.tensor_scalar(OD[:, t, :], o, RL[:, n:n + 1], None, ALU.mult))
                    dve.sem_inc(named("at_o"), 1)
                elif kind == "diff":
                    dve_then(dve.tensor_tensor(RL[:, n:n + 1], RL[:, n:n + 1], lam[:, 5:6], ALU.mult))
                    dve.wait_ge(named("at_pv"), n + 1)
                    dve.scalar_tensor_tensor(out=OM[:, t, v:v + 64], in0=o, scalar=RL[:, n:n + 1], in1=OD[:, t, :],
                                             op0=ALU.mult, op1=ALU.add).then_inc(named("at_o"), 1)
                else:
                    dve.wait_ge(named("at_pv"), n + 1)
                    dve.tensor_scalar(OM[:, t, v:v + 64], o, RL[:, n:n + 1], None, ALU.mult).then_inc(named("at_o"), 1)

            for n in range(NA + 2):
                if n < NA:
                    low(n)
                if n >= 2:
                    finish(n - 2)
            dve.wait_ge(named("at_o"), NA)
            for t in range(TT):
                o = OM[:, t, 0:256].rearrange("p (h d) -> p h d", h=4)
                dve_then(dve.tensor_tensor(DSQ[:, 4 * t:4 * t + 4, :], o, o, ALU.mult))
            dve.tensor_reduce(DST[:, 0, :], DSQ[:, :, :], AX.X, ALU.add).then_inc(named("sub_sum"), 1)
            dve.wait_ge(named("sub_rs"), 1)
            for t in range(TT):
                o = OM[:, t, 0:256].rearrange("p (h d) -> p h d", h=4)
                dve_then(dve.tensor_tensor(o, o, DST[:, 2, 4 * t:4 * t + 4].unsqueeze(2).to_broadcast([P, 4, 64]), ALU.mult))
                dve.tensor_tensor(o, o, row[:, ROW_SUBLN:ROW_SUBLN + 64].unsqueeze(1).to_broadcast([P, 4, 64]),
                                  ALU.mult).then_inc(named("mix_out"), 1)

        def subln_act():
            act.wait_ge(named("sub_sum"), 1)
            act_then(act.activation(DST[:, 1, :], DST[:, 0, :], ACT.Ln, bias=eps_c[:, 0:1], scale=1.0 / 64))
            act.activation(DST[:, 2, :], DST[:, 1, :], ACT.Exp, scale=-0.5).then_inc(named("sub_rs"), 1)

        GT = view(0, (FF_TILES, T))
        CS = view(22 * 256, (4, 2, T))
        SLU = view(30 * 256, (2, 2, T))
        NUP = 2 * (D_FF // 256)

        def up_pe():
            def free(u):
                if u >= 4:
                    pe.wait_ge(named("up_conv"), u - 3)
                elif u == 0:
                    pe.wait_ge(s_x, 4)

            for u in range(NUP):
                cols_unit("up", u, HT, G + u % 4, free, turned(3, pe))

        def up_tile(u, f):
            return (u % 2) * FF_TILES + 2 * (u // 2) + f

        def up_act():
            def silu(j):
                act.wait_ge(named("up_conv"), 2 * j + 1)
                if j >= 2:
                    act.wait_ge(named("up_g"), j - 1)
                act.activation(SLU[:, j % 2, :, :], CS[:, (2 * j) % 4, :, :], ACT.Silu).then_inc(named("up_silu"), 1)

            for u in range(NUP):
                cols_done(act, "up", u)
                if u >= 4:
                    act.wait_ge(named("up_g"), (u - 4) // 2 + 1)
                for f in range(2):
                    c = conv_cols[:, up_tile(u, f), :]
                    ins = act.activation(CS[:, u % 4, f, :], PS[:, G + u % 4, f * T:(f + 1) * T], ACT.Identity,
                                         bias=c[:, 3:4], scale=c[:, 2:3])
                ins.then_inc(named("up_tap"), 1)
                if u % 2:
                    silu(u // 2)

        def up_dve():
            for u in range(NUP):
                dve.wait_ge(named("up_tap"), u + 1)
                for tap in (1, 0):
                    lag = 2 - tap
                    for f in range(2):
                        c = conv_cols[:, up_tile(u, f), :]
                        ins = dve.scalar_tensor_tensor(
                            out=CS[:, u % 4, f, lag:T], in0=PS[:, G + u % 4, f * T:(f + 1) * T - lag],
                            scalar=c[:, tap:tap + 1], in1=CS[:, u % 4, f, lag:T], op0=ALU.mult, op1=ALU.add)
                        if not (tap == 0 and f == 1):
                            if tap == 1 and f == 1:
                                dve_then(ins)
                ins.then_inc(named("up_conv"), 1)

        def up_pool():
            for j in range(NUP // 2):
                pool.wait_ge(named("up_silu"), j + 1)
                pool.wait_ge(named("up_conv"), 2 * j + 2)
                pool.tensor_tensor(GT[:, 2 * j:2 * j + 2, :], SLU[:, j % 2, :, :], CS[:, (2 * j + 1) % 4, :, :],
                                   ALU.mult).then_inc(named("up_g"), 1)

        def down_pe():
            rows_product("down", GT, FF_TILES, ready=lambda k: pe.wait_ge(named("up_g"), k // 2 + 1),
                         free=lambda: pe.wait_ge(named("up_conv"), NUP))

        PTT = view(0, (2, T))
        SG = view(2 * 256, (TT, D))
        PG = view(10 * 256, (2, 512))

        def ple_pe():
            rows_product("ple_gate", HT, DC, ready=turned(4, pe))
            pe.wait_ge(s_tpd, 2 * 5)
            pe.wait_ge(s_small, 16 * N_SMALL)
            for c in range(2):
                for t in range(TT):
                    mm = pe.transpose(PS[:, A, c * T + t * P:c * T + (t + 1) * P], PIN[:, t, c * P:(c + 1) * P],
                                      ident[:, :])
            mm.then_inc(named("p_turned"), 1)

            def free():
                pe.wait_ge(named("p_t"), 1)
                pe.wait_ge(s_tpa, 2 * 5)
            rows_product("ple_proj", PTT, 2, base=A, free=free)

        def ple_act():
            act.wait_ge(named("p_turned"), 1)
            act.activation(PTT, PS[:, A, :].rearrange("p (c n) -> p c n", c=2), ACT.Copy).then_inc(named("p_t"), 1)
            for b in range(4):
                rows_done(act, "ple_gate", b)
                act.activation(SG[:, b // 2, (b % 2) * 512:(b % 2 + 1) * 512], PS[:, G + b, :],
                               ACT.Sigmoid).then_inc(named("ple_sg"), 1)

        def ple_dve():
            for b in range(4):
                rows_done(dve, "ple_proj", b)
                dve.wait_ge(named("ple_sg"), b + 1)
                dve_then(dve.tensor_tensor(PG[:, b % 2, :], PS[:, A + b, :],
                                           SG[:, b // 2, (b % 2) * 512:(b % 2 + 1) * 512], ALU.mult))
                x = X[:, b // 2, (b % 2) * 512:(b % 2 + 1) * 512]
                dve.tensor_tensor(x, x, PG[:, b % 2, :], ALU.add).then_inc(s_x, 1)

        ABT = view(0, (12, T))
        VA = view(12 * 256, (TT, 4, 129))
        SGM = view(17 * 256, (TT, 512))
        SV = view(21 * 256, (TT, 512))
        OM2 = view(25 * 256, (TT, D))
        ROWSG = view(33 * 256, (12, T), 8)
        GA = view(45 * 256, (T,), 36)
        U3 = view(46 * 256, (2, 384))
        L3 = view(49 * 256, (2, 384))
        SP3 = view(52 * 256, (2, 384))
        W3 = view(55 * 256, (2, 384))
        HSQ = view(58 * 256, (TT, 4, P))
        HST = view(62 * 256, (4, 8))
        GC = view(63 * 256, (TT, 36))
        DN = view(64 * 256, (4, 2, 2))

        def ab_pe():
            def free(u):
                if u >= 4:
                    pe.wait_ge(named(("ab_ca", "ab_cd")[u % 2]), (u - 4) // 2 + 1)
            for u in range(6):
                cols_unit("ab_qk", u, HT, G + u % 4, free, turned(5, pe))
            pe.wait_ge(s_tpd, 2 * 6)
            pe.wait_ge(s_tpa, 2 * 6)
            for g, lo in ((0, 6), (1, 10)):
                for k in range(DC):
                    mm = pe.matmul(PS[0:4, A + 2 + g, 0:T], gate_w[:, k, lo:lo + 4], HT[:, k, :], start=(k == 0),
                                   stop=(k == DC - 1))
                mm.then_inc(named("ab_gates"), 1)

            def free2():
                pe.wait_ge(named("ab_ca"), 3)
                pe.wait_ge(named("ab_cd"), 3)
            rows_product("ab_vo", HT, DC, free=free2)
            rows_product("ab_sv", HT, DC, width=512, base=A)
            pe.wait_ge(named("ab_rows"), 1)
            for t in range(TT):
                mm = pe.transpose(PS[:, A + 2, 36 * t:36 * t + 36], GA[:, t * P:(t + 1) * P], ident[0:36, 0:36])
            mm.then_inc(named("ab_cols"), 1)

            def first(n):
                if n == 0:
                    pe.wait_ge(named("ab_va"), 2)
                    pe.wait_ge(named("ab_sgm"), 2)
                    pe.wait_ge(named("ab_svr"), 2)
                    pe.wait_ge(named("ab_gc"), 1)
                if n >= 2:
                    pe.wait_ge(named("ab_u"), n - 1)
                b = n % 2
                if n < 4:
                    m = ROWSG[0:4, 8, :]
                    pe.matmul(PS[:, b, 0:T], sel[0:4, n, :], m, start=True, stop=True)
                    mm = pe.matmul(PS[:, b, T:384], sel[0:4, n, :], ROWSG[0:4, 8, P:T], start=True, stop=True)
                else:
                    h = n - 4
                    pe.matmul(PS[:, b, 0:T], ABT[:, 4 + h, 0:P], ABT[:, h, :], start=True, stop=True)
                    mm = pe.matmul(PS[:, b, T:384], ABT[:, 4 + h, P:T], ABT[:, h, P:T], start=True, stop=True)
                mm.then_inc(named("ab_first"), 1)

            def second(n):
                b = 2 + n % 2
                if n >= 2:
                    pe.wait_ge(named("ab_sec_read"), n - 1)
                if n < 4:
                    lo = 64 * (n % 2)
                    q, k = ABT[lo:lo + 64, 8 + n // 2, :], ABT[lo:lo + 64, 10 + n // 2, :]
                    pe.matmul(PS[:, b, 0:T], k[:, 0:P], q, start=True, stop=True)
                    mm = pe.matmul(PS[:, b, T:384], k[:, P:T], q[:, P:T], start=True, stop=True)
                else:
                    pe.wait_ge(named("ab_sp"), n - 3)
                    sp3 = SP3[:, n % 2, :]
                    pe.matmul(PS[:, b, 0:384], tri[:, :], sp3, start=True, stop=False)
                    mm = pe.matmul(PS[:, b, P:T], ones[:, :], sp3[:, T:384], start=False, stop=True)
                mm.then_inc(named("ab_second"), 1)

            def weigh(n):
                b = 4 + n % 2
                pe.wait_ge(named("ab_w"), n + 1)
                if n >= 2:
                    pe.wait_ge(named("ab_o"), n - 1)
                w = W3[:, n % 2, :]
                nv = 129 if n < 4 else P
                v = [VA[:, t, n, :] if n < 4 else SV[:, t, (n - 4) * P:(n - 3) * P] for t in range(TT)]
                pe.matmul(PS[:, b, 0:nv], w[:, 0:P], v[0], start=True, stop=True)
                pe.matmul(PS[:, b, nv:2 * nv], w[:, P:T], v[0], start=True, stop=False)
                mm = pe.matmul(PS[:, b, nv:2 * nv], w[:, T:384], v[1], start=False, stop=True)
                mm.then_inc(named("ab_pv"), 1)

            for n in range(10):
                if n < 8:
                    first(n)
                if 1 <= n <= 8:
                    second(n - 1)
                if n >= 2:
                    weigh(n - 2)

        def ab_act():
            for u in range(0, 6, 2):
                cols_done(act, "ab_qk", u)
                act.activation(ABT[:, 2 * u:2 * u + 2, :], PS[:, G + u % 4, :].rearrange("p (c n) -> p c n", c=2),
                               ACT.Copy, scale=(P ** -0.5 if u < 2 else 1.0)).then_inc(named("ab_ca"), 1)
            act.wait_ge(named("ab_zi"), 1)
            act.activation(ROWSG[0:4, 1, :], ROWSG[0:4, 0, :], ACT.Tanh, scale=1.0 / 15).then_inc(named("ab_li"), 1)
            for t in range(TT):
                rows_done(act, "ab_vo", 2 * t + 1)
                act.activation(SGM[:, t, :], PS[:, G + 2 * t + 1, :], ACT.Sigmoid).then_inc(named("ab_sgm"), 1)
            act.wait_ge(named("ab_zf"), 1)
            act_then(act.activation(ROWSG[0:4, 4, :], ROWSG[0:4, 3, :], ACT.Exp))
            act.activation(ROWSG[0:4, 5, :], ROWSG[0:4, 4, :], ACT.Ln, bias=one_c[0:4, 0:1]).then_inc(named("ab_lf"), 1)
            for t in range(TT):
                rows_done(act, "ab_sv", t)
                act.activation(SV[:, t, :], PS[:, A + t, :], ACT.Copy).then_inc(named("ab_svr"), 1)
            act.wait_ge(named("ab_m"), 1)
            act.activation(GA[32:36, :], ROWSG[0:4, 9, :], ACT.Exp, scale=-1.0).then_inc(named("ab_enm"), 1)
            for n in range(9):
                if n < 8:
                    act.wait_ge(named("ab_u"), n + 1)
                    if n < 4:
                        act.activation(L3[:, n % 2, :], U3[:, n % 2, :], ACT.Exp).then_inc(named("ab_l"), 1)
                    else:
                        if n >= 6:
                            act.wait_ge(named("ab_sp"), n - 5)
                        act_then(act.activation(L3[:, n % 2, :], U3[:, n % 2, :], ACT.Abs))
                        act_then(act.activation(L3[:, n % 2, :], L3[:, n % 2, :], ACT.Exp, scale=-1.0))
                        act.activation(L3[:, n % 2, :], L3[:, n % 2, :], ACT.Ln,
                                       bias=one_c[:, 0:1]).then_inc(named("ab_l"), 1)
                if n >= 5:
                    m = n - 1
                    act.wait_ge(named("ab_sec_read"), m + 1)
                    act.wait_ge(named("ab_pv"), m - 1)
                    act.activation(W3[:, m % 2, :], U3[:, m % 2, :], ACT.Exp).then_inc(named("ab_w"), 1)
            act.wait_ge(named("ab_ssq"), 1)
            act_then(act.activation(HST[:, 1, :], HST[:, 0, :], ACT.Ln, bias=eps_c[:, 0:1], scale=1.0 / P))
            act.activation(HST[:, 2, :], HST[:, 1, :], ACT.Exp, scale=-0.5).then_inc(named("ab_hrs"), 1)

        def ab_dve():
            for u in range(1, 6, 2):
                cols_done(dve, "ab_qk", u)
                dve.tensor_scalar(ABT[:, 2 * u:2 * u + 2, :], PS[:, G + u % 4, :].rearrange("p (c n) -> p c n", c=2),
                                  {1: P ** -0.5, 3: 1.0, 5: 64 ** -0.5}[u], None, ALU.mult).then_inc(named("ab_cd"), 1)
            R = lambda j: ROWSG[0:4, j, :]
            dve.wait_ge(named("ab_gates"), 2)
            dve.tensor_scalar(R(0), PS[0:4, A + 2, 0:T], gate_p[0:4, 1:2], None, ALU.add).then_inc(named("ab_zi"), 1)
            dve_then(dve.tensor_scalar(R(6), PS[0:4, A + 3, 0:T], gate_p[0:4, 2:3], None, ALU.add))
            dve_then(dve.tensor_scalar(R(2), R(6), 0.0, None, ALU.min))
            dve.scalar_tensor_tensor(out=R(3), in0=R(2), scalar=2.0, in1=R(6), op0=ALU.mult,
                                     op1=ALU.subtract).then_inc(named("ab_zf"), 1)
            dve.memset(GA[:, :], 0.0)
            dve.memset(VA[:, :, :, 128:129], 1.0)
            for t in range(TT):
                rows_done(dve, "ab_vo", 2 * t)
                dve.tensor_copy(VA[:, t, :, 0:P], PS[:, G + 2 * t, :].rearrange("p (h d) -> p h d", h=4)
                                ).then_inc(named("ab_va"), 1)
            dve.wait_ge(named("ab_lf"), 1)
            dve.wait_ge(named("ab_li"), 1)
            dve_then(dve.tensor_tensor(R(6), R(2), R(5), ALU.subtract))
            dve_then(dve.tensor_tensor_scan(R(7), R(6), R(6), 0.0, ALU.add, ALU.bypass))
            dve_then(dve.scalar_tensor_tensor(out=R(10), in0=R(1), scalar=15.0, in1=R(7), op0=ALU.mult,
                                              op1=ALU.subtract))
            dve_then(dve.tensor_tensor_scan(R(11), R(10), R(10), 0.0, ALU.max, ALU.max))
            dve_then(dve.tensor_scalar(R(8), R(11), -1.0, None, ALU.mult))
            dve.tensor_copy(GA[0:4, :], R(10))
            dve_then(dve.tensor_tensor(R(9), R(7), R(11), ALU.add))
            dve.sem_inc(named("ab_m"), 1)
            dve.wait_ge(named("ab_enm"), 1)
            dve.sem_inc(named("ab_rows"), 1)
            dve.wait_ge(named("ab_cols"), 1)
            dve_then(dve.tensor_copy(GC[:, :, :], PS[:, A + 2, 0:72].rearrange("p (t n) -> p t n", t=2)))
            dve.sem_inc(named("ab_gc"), 1)

            def after_first(n):
                dve.wait_ge(named("ab_first"), n + 1)
                u, z = U3[:, n % 2, :], PS[:, n % 2, 0:384]
                if 2 <= n < 6:
                    dve.wait_ge(named("ab_l"), n - 1)
                if n >= 6:
                    dve.wait_ge(named("ab_w"), n - 1)
                if n < 4:
                    dve.scalar_tensor_tensor(out=u[:, 0:T], in0=z[:, 0:T], scalar=GC[:, 0, n:n + 1],
                                             in1=neg_ge[:, 0:2, :], op0=ALU.add, op1=ALU.add)
                    dve.scalar_tensor_tensor(out=u[:, T:384], in0=z[:, T:384], scalar=GC[:, 1, n:n + 1],
                                             in1=neg_ge[:, 2, :], op0=ALU.add, op1=ALU.add).then_inc(named("ab_u"), 1)
                else:
                    dve.tensor_tensor(u, z, neg_gt[:, :, :].rearrange("p a b -> p (a b)"),
                                      ALU.add).then_inc(named("ab_u"), 1)

            def after_l(n):
                if n < 4:
                    dve.wait_ge(named("ab_l"), n + 1)
                    dve.wait_ge(named("ab_second"), n + 1)
                    if n >= 2:
                        dve.wait_ge(named("ab_pv"), n - 1)
                    dve_then(dve.tensor_tensor(W3[:, n % 2, :], PS[:, 2 + n % 2, 0:384], L3[:, n % 2, :], ALU.mult))
                    dve.sem_inc(named("ab_w"), 1)
                    dve.sem_inc(named("ab_sec_read"), 1)
                else:
                    dve.wait_ge(named("ab_l"), n + 1)
                    if n >= 6:
                        dve.wait_ge(named("ab_second"), n - 1)
                    dve_then(dve.scalar_tensor_tensor(out=SP3[:, n % 2, :], in0=U3[:, n % 2, :], scalar=0.0,
                                                      in1=L3[:, n % 2, :], op0=ALU.max, op1=ALU.add))
                    dve.sem_inc(named("ab_sp"), 1)
                    dve.wait_ge(named("ab_second"), n + 1)
                    dve.scalar_tensor_tensor(out=U3[:, n % 2, :], in0=PS[:, 2 + n % 2, 0:384], scalar=-1.0,
                                             in1=U3[:, n % 2, :], op0=ALU.mult,
                                             op1=ALU.add).then_inc(named("ab_sec_read"), 1)

            def finish(n):
                dve.wait_ge(named("ab_pv"), n + 1)
                b = 4 + n % 2
                if n < 4:
                    o = PS[:, b, 0:258].rearrange("p (t n) -> p t n", t=2)
                    dn = DN[:, n, :, :]
                    dve_then(dve.scalar_tensor_tensor(out=dn[:, 0, :], in0=o[:, :, 128], scalar=-1.0,
                                                      in1=GC[:, :, 32 + n], op0=ALU.mult, op1=ALU.max))
                    dve_then(dve.tensor_tensor(dn[:, 0, :], o[:, :, 128], dn[:, 0, :], ALU.max))
                    dve_then(dve.reciprocal(dn[:, 1, :], dn[:, 0, :]))
                    for t in range(TT):
                        ins = dve.tensor_scalar(OM2[:, t, n * P:(n + 1) * P], o[:, t, 0:P], dn[:, 1, t:t + 1], None,
                                                ALU.mult)
                    ins.then_inc(named("ab_o"), 1)
                else:
                    dve.tensor_copy(OM2[:, :, n * P:(n + 1) * P],
                                    PS[:, b, 0:T].rearrange("p (t n) -> p t n", t=2)).then_inc(named("ab_o"), 1)

            for n in range(10):
                if n < 8:
                    after_first(n)
                if 1 <= n <= 8:
                    after_l(n - 1)
                if n >= 2:
                    finish(n - 2)
            dve.wait_ge(named("ab_o"), 8)
            head_norm_dve(OM2[:, :, 0:512], HSQ, HST, 4, "ab_ssq", "ab_hrs",
                          row[:, ROW_ABHEAD:ROW_ABHEAD + 512].rearrange("p (h d) -> p h d", h=4), SGM, "ab_om")

        def head_norm_dve(o_all, sq, st, heads, told, asked, gain, gate, done):
            for t in range(TT):
                o = o_all[:, t, :].rearrange("p (h d) -> p h d", h=heads)
                q = sq[:, t, :, :] if len(sq.shape) == 4 else sq
                dve_then(dve.tensor_tensor(q, o, o, ALU.mult))
                dve_then(dve.tensor_reduce(st[:, 0, heads * t:heads * (t + 1)], q, AX.X, ALU.add))
            dve.sem_inc(named(told), 1)
            dve.wait_ge(named(asked), 1)
            for t in range(TT):
                o = o_all[:, t, :].rearrange("p (h d) -> p h d", h=heads)
                r = st[:, 2, heads * t:heads * (t + 1)].unsqueeze(2).to_broadcast([P, heads, P])
                dve_then(dve.tensor_tensor(o, o, r, ALU.mult))
                dve_then(dve.tensor_tensor(o, o, gain, ALU.mult))
                dve.tensor_tensor(o, o, gate[:, t, :].rearrange("p (h d) -> p h d", h=heads),
                                  ALU.mult).then_inc(named(done), 1)

        XQ = view(0, (8, T))
        XK = view(8 * 256, (8, T))
        XV = view(16 * 256, (TT, D))
        XO = view(24 * 256, (8, T))
        XP = view(32 * 256, (3, T))
        XPT = view(35 * 256, (2, 2, T))
        XMN = view(39 * 256, (3, 8))
        NX = 8

        def xa_kv_pe(l):
            s0 = NX * l

            def free(u):
                if u == 0:
                    pe.wait_ge(s_x, 4 * (4 + 3 * l))
            for u in range(4):
                cols_unit(f"xk{l}", u, MEMT, G + u, free)
            rows_product(f"xv{l}", MEMT, DC, free=lambda: (pe.wait_ge(named("xk_a"), 2 * l + 2),
                                                           pe.wait_ge(named("xk_d"), 2 * l + 2)))

        def xa_kv_evac(l, eng):
            k = 0 if eng is act else 1
            for u in (k, k + 2):
                cols_done(eng, f"xk{l}", u)
                src = PS[:, G + u, :].rearrange("p (c n) -> p c n", c=2)
                if k:
                    dve.tensor_copy(XK[:, 2 * u:2 * u + 2, :], src).then_inc(named("xk_d"), 1)
                else:
                    act.activation(XK[:, 2 * u:2 * u + 2, :], src, ACT.Copy).then_inc(named("xk_a"), 1)
            for b in (k, k + 2):
                rows_done(eng, f"xv{l}", b)
                dst = XV[:, b // 2, (b % 2) * 512:(b % 2 + 1) * 512]
                if k:
                    dve.tensor_copy(dst, PS[:, G + b, :]).then_inc(named("xv_d"), 1)
                else:
                    act.activation(dst, PS[:, G + b, :], ACT.Copy).then_inc(named("xv_a"), 1)

        def xa_pe(l, turn):
            c0 = NX * l

            def free(u):
                if u == 0:
                    pe.wait_ge(named("xv_a"), 2 * l + 2)
                    pe.wait_ge(named("xv_d"), 2 * l + 2)
            for u in range(4):
                cols_unit(f"xq{l}", u, HT, G + u, free, turned(turn, pe))

            def scores(n):
                h, t = n // 2, n % 2
                if n == 0:
                    pe.wait_ge(s_tpd, 2 * (turn + 1))
                    pe.wait_ge(s_tpa, 2 * (turn + 1))
                pe.wait_ge(named(("xq_a", "xq_d")[h % 2]), 2 * l + h // 2 + 1)
                if n >= 2:
                    pe.wait_ge(named("xa_exp"), c0 + n - 1)
                for c in range(2):
                    mm = pe.matmul(PS[:, A + n % 2, 0:T], XQ[:, 2 * h + c, t * P:(t + 1) * P], XK[:, 2 * h + c, :],
                                   start=(c == 0), stop=(c == 1))
                mm.then_inc(named("xa_s"), 1)

            def turn_p(n):
                pe.wait_ge(named("xa_norm"), c0 + n + 1)
                if n >= 2:
                    pe.wait_ge(named("xa_pt"), c0 + n - 1)
                for b in range(2):
                    mm = pe.transpose(PS[:, A + 2 + n % 2, b * P:(b + 1) * P], XP[:, n % 3, b * P:(b + 1) * P],
                                      ident[:, :])
                mm.then_inc(named("xa_tp"), 1)

            def weigh(h):
                pe.wait_ge(named("xa_pt"), c0 + 2 * h + 2)
                if h >= 2:
                    pe.wait_ge(named("xa_o"), 4 * l + h - 1)
                elif h == 0:
                    pe.wait_ge(named("xq_a"), 2 * l + 2)
                    pe.wait_ge(named("xq_d"), 2 * l + 2)
                for c in range(2):
                    for m in range(2):
                        mm = pe.matmul(PS[:, G + h % 2, c * T:(c + 1) * T],
                                       XV[:, m, h * T + c * P:h * T + (c + 1) * P], XPT[:, h % 2, m, :],
                                       start=(m == 0), stop=(m == 1))
                mm.then_inc(named("xa_pv"), 1)

            for n in range(NX + 2):
                if n < NX:
                    scores(n)
                if 1 <= n <= NX:
                    turn_p(n - 1)
                if n >= 2 and n % 2:
                    weigh((n - 2) // 2)
            rows_product(f"xo{l}", XO, DC, ready=lambda k: pe.wait_ge(named("xa_o"), 4 * l + k // 2 + 1),
                         free=lambda: pe.wait_ge(named("xa_o"), 4 * l + 4))

        def xa_act(l):
            c0 = NX * l
            for u in (0, 2):
                cols_done(act, f"xq{l}", u)
                act.activation(XQ[:, 2 * u:2 * u + 2, :], PS[:, G + u, :].rearrange("p (c n) -> p c n", c=2),
                               ACT.Copy, scale=-1.0 / 16).then_inc(named("xq_a"), 1)
            for n in range(NX + 1):
                if n < NX:
                    act.wait_ge(named("xa_min"), c0 + n + 1)
                    if n >= 3:
                        act.wait_ge(named("xa_tp"), c0 + n - 2)
                    act.activation(XP[:, n % 3, :], PS[:, A + n % 2, 0:T], ACT.Exp, bias=XMN[:, 0, n:n + 1],
                                   scale=-1.0, accum_out=XMN[:, 1, n:n + 1]).then_inc(named("xa_exp"), 1)
                if n >= 1:
                    m = n - 1
                    h, t = m // 2, m % 2
                    act.wait_ge(named("xa_tp"), c0 + m + 1)
                    if h >= 2:
                        act.wait_ge(named("xa_pv"), 4 * l + h - 1)
                    act.activation(XPT[:, h % 2, :, t * P:(t + 1) * P],
                                   PS[:, A + 2 + m % 2, 0:T].rearrange("p (m n) -> p m n", m=2),
                                   ACT.Copy).then_inc(named("xa_pt"), 1)

        def xa_dve(l):
            c0 = NX * l
            for u in (1, 3):
                cols_done(dve, f"xq{l}", u)
                dve.tensor_scalar(XQ[:, 2 * u:2 * u + 2, :], PS[:, G + u, :].rearrange("p (c n) -> p c n", c=2),
                                  -1.0 / 16, None, ALU.mult).then_inc(named("xq_d"), 1)
            for n in range(NX + 3):
                if n < NX:
                    dve.wait_ge(named("xa_s"), c0 + n + 1)
                    dve.tensor_reduce(XMN[:, 0, n:n + 1], PS[:, A + n % 2, 0:T], AX.X,
                                      ALU.min).then_inc(named("xa_min"), 1)
                if 1 <= n <= NX:
                    m = n - 1
                    dve.wait_ge(named("xa_exp"), c0 + m + 1)
                    dve_then(dve.reciprocal(XMN[:, 2, m:m + 1], XMN[:, 1, m:m + 1]))
                    dve.tensor_scalar(XP[:, m % 3, :], XP[:, m % 3, :], XMN[:, 2, m:m + 1], None,
                                      ALU.mult).then_inc(named("xa_norm"), 1)
                if n >= 3 and n % 2:
                    h = (n - 3) // 2
                    if h < 4:
                        xo_out(l, h)

        def xo_out(l, h):
            dve.wait_ge(named("xa_pv"), 4 * l + h + 1)
            dve.tensor_copy(XO[:, 2 * h:2 * h + 2, :],
                            PS[:, G + h % 2, :].rearrange("p (c n) -> p c n", c=2)).then_inc(named("xa_o"), 1)

        HID = view(0, (FF2_TILES, T))
        RLU = view(40 * 256, (2, 2, T))
        NM1 = D_FF_2 // 256

        def mlp_pe(l, turn):
            def free(u):
                if u == 0:
                    pe.wait_ge(s_x, 4 * (5 + 3 * l))
                if u >= 4:
                    pe.wait_ge(named("m1_relu"), NM1 * l + u - 3)
            for u in range(NM1):
                cols_unit(f"m1{l}", u, HT, G + u % 4, free, turned(turn, pe))
            rows_product(f"m2{l}", HID, FF2_TILES, ready=lambda k: pe.wait_ge(named("m1_sq"), NM1 * l + k // 2 + 1),
                         free=lambda: pe.wait_ge(named("m1_relu"), NM1 * (l + 1)))

        def mlp_act(l):
            for u in range(NM1):
                cols_done(act, f"m1{l}", u)
                if u >= 2:
                    act.wait_ge(named("m1_sq"), NM1 * l + u - 1)
                act.activation(RLU[:, u % 2, :, :], PS[:, G + u % 4, :].rearrange("p (c n) -> p c n", c=2),
                               ACT.Relu).then_inc(named("m1_relu"), 1)

        def mlp_dve(l):
            for u in range(NM1):
                dve.wait_ge(named("m1_relu"), NM1 * l + u + 1)
                dve.tensor_tensor(HID[:, 2 * u:2 * u + 2, :], RLU[:, u % 2, :, :], RLU[:, u % 2, :, :],
                                  ALU.mult).then_inc(named("m1_sq"), 1)

        NCU = 12
        QKV = view(0, (24, T))
        CC = view(32 * 256, (4, 2, T))
        SGC = view(24 * 256, (TT, D))
        SQL = view(40 * 256, (2, 512))
        RSL = view(44 * 256, (2, 512))
        DEC = view(36 * 256, (2, 4, P))
        ATC = view(40 * 256, (4, 4, P))
        ATT = view(48 * 256, (4, 4, P))
        RV = view(56 * 256, (4, 4, P))
        RK = view(64 * 256, (2, 4, P))
        KD = view(68 * 256, (2, 4, P))
        QD = view(72 * 256, (2, 4, P))
        GAB = view(72 * 256, (T,), 40)
        CR = view(76 * 256, (8, T), 8)
        LT = view(76 * 256, (4, 4, P))
        XI = view(16 * 256, (4, 4, P))
        XT = view(32 * 256, (4, 4, P))
        YI = view(8 * 256, (4, 4, P))
        VN0 = view(8 * 256, (2, 4, P))
        S1 = view(12 * 256, (2, 4, P))
        NW = view(16 * 256, (2, 4, P))
        VN1 = view(20 * 256, (2, 4, P))
        OC = view(0, (TT, D))
        OSQ = view(40 * 256, (8, P))
        TE = HN[:, 0, :].rearrange("p (a h n) -> p a h n", a=2, h=4)
        TQ = HN[:, 1, 0:512].rearrange("p (h n) -> p h n", h=4)
        LM = sb("level_masks", [P, 7, P])
        GCB = sb("gate_cols", [P, TT, 40])
        GX = sb("gate_col_exps", [P, 4, 8])
        CST = sb("c_stats", [P, 3, 16])
        DG = sb("g_last_diag", [8, 8])
        NEA = sb("a_exp", [8, 1])
        eps128_c = sb("eps128_c", [P, 1])
        LEVELS = 7

        def c_consts_pool():
            pool.memset(eps128_c[:, :], P * EPS)
            pool_then(pool.memset(LM[:, :, :], 0.0))
            for i in range(LEVELS):
                b = 1 << i
                m = LM[:, i, :].rearrange("p (n h b) -> p n h b", h=2, b=b)[:, :, 1, :]
                n = P // (2 * b)
                pool_then(pool.memset(m, 1.0))
                pool_then(pool.affine_select(out=m, in_=m, compare_op=ALU.is_ge, fill=0.0, base=0,
                                             pattern=[[-2 * b, n], [0, b]], channel_multiplier=1))
                pool_then(pool.affine_select(out=m, in_=m, compare_op=ALU.is_ge, fill=0.0, base=b - 1,
                                             pattern=[[2 * b, n], [0, b]], channel_multiplier=-1))
            pool.sem_inc(named("c_consts"), 1)

        def c_pe():
            def free(u):
                if u == 0:
                    pe.wait_ge(s_x, 4 * 6)
                if u >= 4:
                    pe.wait_ge(named("c_conv"), u - 3)
            for u in range(NCU):
                cols_unit("c_qkv", u, HT, G + u % 4, free, turned(9, pe))
            rows_product("c_gate", HT, DC, free=lambda: pe.wait_ge(named("c_conv"), NCU))
            pe.wait_ge(s_tpd, 2 * 10)
            pe.wait_ge(s_tpa, 2 * 10)
            for g, lo in ((0, 14), (1, 22)):
                for k in range(DC):
                    mm = pe.matmul(PS[0:8, A + g, 0:T], gate_w[:, k, lo:lo + 8], HT[:, k, :], start=(k == 0),
                                   stop=(k == DC - 1))
                mm.then_inc(named("c_gates"), 1)
            for i in range(8):
                pe.wait_ge(named("l2_sq"), i + 1)
                if i >= 2:
                    pe.wait_ge(named("l2_ln"), i - 1)
                pe.matmul(PS[:, A + 2 + i % 2, :], ones[:, :], SQL[:, i % 2, :], start=True,
                          stop=True).then_inc(named("l2_ss"), 1)
            pe.wait_ge(named("c_rows"), 1)
            for t in range(TT):
                pe.transpose(PS[:, A, 40 * t:40 * t + 40], GAB[:, t * P:(t + 1) * P], ident[0:40, 0:40])
            pe.matmul(PS[:, A, 128:136], ones[0:8, :], DG[:, :], start=True, stop=True).then_inc(named("c_cols"), 1)
            for gi in range(4):
                hg, c = gi // 2, gi % 2
                pe.wait_ge(named("c_sg"), gi + 1)
                if gi == 0:
                    pe.wait_ge(named("c_silu"), NCU)
                for j in range(4):
                    mm = pe.transpose(PS[:, gi, j * P:(j + 1) * P], QKV[:, 16 + 4 * hg + j, c * P:(c + 1) * P],
                                      ident[:, :])
                mm.then_inc(named("c_vt"), 1)
            for gi in range(4):
                hg, c = gi // 2, gi % 2
                if gi == 0:
                    pe.wait_ge(named("l2_done"), 8)
                    pe.wait_ge(named("c_gcb"), 1)
                for j in range(4):
                    mm = pe.transpose(PS[:, 4 + gi, j * P:(j + 1) * P], QKV[:, 8 + 4 * hg + j, c * P:(c + 1) * P],
                                      ident[:, :])
                mm.then_inc(named("c_kt"), 1)
            for gi in range(4):
                hg, c = gi // 2, gi % 2
                pb = 4 * (gi % 2)
                tok = slice(c * P, (c + 1) * P)
                if gi < 2:
                    pe.wait_ge(named("c_rv" if gi == 0 else "c_rk"), 4)
                else:
                    pe.wait_ge(named("c_prep"), gi - 1)
                for i, r in ((0, 7), (1, 2)):
                    for j in range(4):
                        mm = pe.matmul(PS[:, pb + i, j * P:(j + 1) * P], sel[:, 4 * hg + j, :], CR[:, r, tok],
                                       start=True, stop=True)
                    mm.then_inc(named("c_p"), 1)
                for i, q0 in ((2, 8), (3, 0)):
                    for j in range(4):
                        mm = pe.matmul(PS[:, pb + i, j * P:(j + 1) * P], QKV[:, 8 + 4 * hg + j, tok],
                                       QKV[:, q0 + 4 * hg + j, tok], start=True, stop=True)
                    mm.then_inc(named("c_p"), 1)
            for gi in range(4):
                pe.wait_ge(named("c_lt"), gi + 1)
                if gi == 0:
                    pe.wait_ge(named("c_prep"), 4)
                if gi >= 2:
                    pe.wait_ge(named("c_x"), gi - 1)
                for j in range(4):
                    mm = pe.transpose(PS[:, 6 + gi % 2, j * P:(j + 1) * P], LT[:, gi, j, :], ident[:, :])
                mm.then_inc(named("c_l0"), 1)

            NL = 4 * (LEVELS - 1)

            def y(n):
                gi = n % 4
                pe.wait_ge(named("c_x"), n + 1)
                pe.wait_ge(named("c_lt"), n + 5)
                if n >= 2:
                    pe.wait_ge(named("c_y"), n - 1)
                for j in range(4):
                    mm = pe.matmul(PS[:, gi % 2, j * P:(j + 1) * P], LT[:, gi, j, :], XI[:, gi, j, :], start=True,
                                   stop=True)
                mm.then_inc(named("c_ym"), 1)

            def pq(n):
                gi = n % 4
                pe.wait_ge(named("c_y"), n + 1)
                if n >= 2:
                    pe.wait_ge(named("c_x"), n + 3)
                if n < NL - 4:
                    for j in range(4):
                        pe.matmul(PS[:, 2 + gi % 2, j * P:(j + 1) * P], XT[:, gi, j, :], YI[:, gi, j, :], start=True,
                                  stop=True)
                for j in range(4):
                    mm = pe.matmul(PS[:, 4 + gi % 2, j * P:(j + 1) * P], YI[:, gi, j, :], XT[:, gi, j, :], start=True,
                                   stop=True)
                mm.then_inc(named("c_pq"), 1)

            for n in range(NL + 1):
                if n < NL:
                    y(n)
                if n >= 1:
                    pq(n - 1)

            def quad(bank, terms, told):
                for j in range(4):
                    for i, (l, r) in enumerate(terms):
                        mm = pe.matmul(PS[:, bank, j * P:(j + 1) * P], l[:, j, :], r[:, j, :], start=(i == 0),
                                       stop=(i == len(terms) - 1))
                mm.then_inc(named(told), 1)

            for hg in range(2):
                g0, g1 = 2 * hg, 2 * hg + 1
                pe.wait_ge(named("c_x"), 4 * LEVELS if hg else 4 * LEVELS - 2)
                if hg == 0:
                    pe.wait_ge(named("c_y"), NL)
                quad(hg, [(XT[:, g0], RV[:, g0])], "c_u0")
                quad(6 + hg, [(RK[:, hg], XT[:, g1])], "c_wt")
            for hg in range(2):
                pe.wait_ge(named("c_vn0"), hg + 1)
                quad(2 + hg, [(KD[:, hg], VN0[:, hg])], "c_s1m")
                quad(hg, [(ATT[:, 2 * hg], VN0[:, hg])], "c_o0")
            for hg in range(2):
                g1 = 2 * hg + 1
                pe.wait_ge(named("c_nw"), hg + 1)
                pe.wait_ge(named("c_s1"), hg + 1)
                quad(4 + hg, [(XT[:, g1], RV[:, g1]), (NW[:, hg], S1[:, hg])], "c_u1")
            for hg in range(2):
                pe.wait_ge(named("c_vn1"), hg + 1)
                quad(2 + hg, [(QD[:, hg], S1[:, hg]), (ATT[:, 2 * hg + 1], VN1[:, hg])], "c_o1")

        def c_act():
            def silu(u):
                act.wait_ge(named("c_conv"), u + 1)
                act.activation(QKV[:, 2 * u:2 * u + 2, :], CC[:, u % 4, :, :], ACT.Silu).then_inc(named("c_silu"), 1)

            for u in range(NCU):
                cols_done(act, "c_qkv", u)
                for f in range(2):
                    ins = act.activation(CC[:, u % 4, f, :], PS[:, G + u % 4, f * T:(f + 1) * T], ACT.Copy,
                                         scale=cconv_cols[:, 2 * u + f, 3:4])
                ins.then_inc(named("c_tap"), 1)
                if u:
                    silu(u - 1)
            silu(NCU - 1)
            for b in range(4):
                rows_done(act, "c_gate", b)
                act.activation(SGC[:, b // 2, (b % 2) * 512:(b % 2 + 1) * 512], PS[:, G + b, :],
                               ACT.Silu).then_inc(named("c_sg"), 1)
            R = lambda j: CR[:, j, :]
            act.wait_ge(named("c_za"), 1)
            act_then(act.activation(R(6), R(5), ACT.Exp))
            act.activation(R(6), R(6), ACT.Ln, bias=one_c[0:8, 0:1]).then_inc(named("c_la"), 1)
            act.activation(R(0), PS[0:8, A, 0:T], ACT.Exp, scale=-1.0).then_inc(named("c_eb"), 1)
            act.activation(NEA[:, :], gate_p[:, 3:4], ACT.Exp).then_inc(named("c_nea"), 1)
            for i in range(8):
                act.wait_ge(named("l2_ss"), i + 1)
                if i >= 2:
                    act.wait_ge(named("l2_done"), i - 1)
                q = i < 4
                act.activation(RSL[:, i % 2, :], PS[:, A + 2 + i % 2, :], ACT.Ln,
                               bias=(eps128_c if q else eps_c)[:, 0:1],
                               scale=(float(P) if q else 1.0)).then_inc(named("l2_ln"), 1)
                act.wait_ge(named("l2_ln"), i + 1)
                act.activation(RSL[:, i % 2, :], RSL[:, i % 2, :], ACT.Exp, scale=-0.5).then_inc(named("l2_rs"), 1)
            act.wait_ge(named("c_gcb"), 1)
            act.activation(GX[:, 0, :], GCB[:, 1, 0:8], ACT.Exp).then_inc(named("c_gx"), 1)
            act.activation(GX[:, 3, :], GX[:, 2, :], ACT.Exp).then_inc(named("c_gx"), 1)
            for gi in range(4):
                act.wait_ge(named("c_e"), gi + 1)
                if gi >= 2:
                    act.wait_ge(named("c_prep"), gi - 1)
                act.activation(DEC[:, gi % 2, :, :], TE[:, gi % 2, :, :], ACT.Exp).then_inc(named("c_dec"), 1)
                if gi % 2:
                    if gi == 3:
                        act.wait_ge(named("c_qd"), 1)
                    act.activation(TQ, PS[:, 4 * (gi % 2), :].rearrange("p (h n) -> p h n", h=4),
                                   ACT.Exp).then_inc(named("c_tq"), 1)
            for n in range(4 * (LEVELS - 1)):
                act.wait_ge(named("c_ym"), n + 1)
                act.activation(YI[:, n % 4, :, :], PS[:, (n % 4) % 2, :].rearrange("p (h n) -> p h n", h=4),
                               ACT.Copy).then_inc(named("c_y"), 1)
            for hg in range(2):
                act.wait_ge(named("c_wt"), hg + 1)
                act.activation(NW[:, hg, :, :], PS[:, 6 + hg, :].rearrange("p (h n) -> p h n", h=4), ACT.Copy,
                               scale=-1.0).then_inc(named("c_nw"), 1)
            for hg in range(2):
                act.wait_ge(named("c_s1m"), hg + 1)
                act.activation(S1[:, hg, :, :], PS[:, 2 + hg, :].rearrange("p (h n) -> p h n", h=4),
                               ACT.Copy).then_inc(named("c_s1"), 1)
            for hg in range(2):
                act.wait_ge(named("c_o0"), hg + 1)
                act.activation(OC[:, 0, 512 * hg:512 * (hg + 1)], PS[:, hg, :], ACT.Copy).then_inc(named("c_oc0"), 1)
            act.wait_ge(named("c_ssq"), 1)
            act_then(act.activation(CST[:, 1, :], CST[:, 0, :], ACT.Ln, bias=eps_c[:, 0:1], scale=1.0 / P))
            act.activation(CST[:, 2, :], CST[:, 1, :], ACT.Exp, scale=-0.5).then_inc(named("c_hrs"), 1)

        def c_pool():
            pool.wait_ge(named("c_silu"), 8)
            for i in range(8):
                if i >= 2:
                    pool.wait_ge(named("l2_ss"), i - 1)
                pool.tensor_tensor(SQL[:, i % 2, :].rearrange("p (c n) -> p c n", c=2), QKV[:, 2 * i:2 * i + 2, :],
                                   QKV[:, 2 * i:2 * i + 2, :], ALU.mult).then_inc(named("l2_sq"), 1)
            for hg in range(2):
                pool.wait_ge(named("c_tq"), hg + 1)
                pool.tensor_tensor(QD[:, hg, :, :], QKV[:, 4 * hg:4 * hg + 4, P:T], TQ, ALU.mult).then_inc(named("c_qd"), 1)
            for n in range(4 * LEVELS):
                lvl, gi = n // 4, n % 4
                if n == 0:
                    pool.wait_ge(named("c_prep"), 4)
                if lvl == 1:
                    pool.wait_ge(named("c_x"), gi + 1)
                elif lvl > 1:
                    pool.wait_ge(named("c_ym"), n - 7)
                pool.tensor_tensor(LT[:, gi, :, :], ATC[:, gi, :, :],
                                   LM[:, lvl, :].unsqueeze(1).to_broadcast([P, 4, P]), ALU.mult
                                   ).then_inc(named("c_lt"), 1)

        def c_dve():
            for u in range(NCU):
                dve.wait_ge(named("c_tap"), u + 1)
                for tap in (2, 1, 0):
                    lag = 3 - tap
                    for f in range(2):
                        ins = dve.scalar_tensor_tensor(
                            out=CC[:, u % 4, f, lag:T], in0=PS[:, G + u % 4, f * T:(f + 1) * T - lag],
                            scalar=cconv_cols[:, 2 * u + f, tap:tap + 1], in1=CC[:, u % 4, f, lag:T], op0=ALU.mult,
                            op1=ALU.add)
                    if tap:
                        dve_then(ins)
                ins.then_inc(named("c_conv"), 1)
            R = lambda j: CR[:, j, :]
            dve.wait_ge(named("c_gates"), 2)
            dve_then(dve.tensor_scalar(R(3), PS[0:8, A + 1, 0:T], gate_p[:, 4:5], None, ALU.add))
            dve_then(dve.tensor_scalar(R(4), R(3), 0.0, None, ALU.min))
            dve.scalar_tensor_tensor(out=R(5), in0=R(4), scalar=2.0, in1=R(3), op0=ALU.mult,
                                     op1=ALU.subtract).then_inc(named("c_za"), 1)
            dve.memset(GAB[:, :], 0.0)
            dve.wait_ge(named("c_eb"), 1)
            dve_then(dve.tensor_scalar(R(1), R(0), 1.0, None, ALU.add))
            dve_then(dve.reciprocal(R(2), R(1)))
            dve.wait_ge(named("c_la"), 1)
            dve.wait_ge(named("c_nea"), 1)
            dve_then(dve.tensor_tensor(R(3), R(3), R(6), ALU.add))
            dve_then(dve.tensor_tensor(R(3), R(3), R(4), ALU.subtract))
            dve_then(dve.tensor_scalar(R(5), R(3), NEA[:, 0:1], -1.0, ALU.mult, ALU.mult))
            for c in range(2):
                s_ = CR[:, 5, c * P:(c + 1) * P]
                ins = dve.tensor_tensor_scan(CR[:, 7, c * P:(c + 1) * P], s_, s_, 0.0, ALU.add, ALU.bypass)
            dve_then(ins)
            dve.tensor_scalar(DG[:, :], ident[0:8, 0:8], CR[:, 7, P - 1:P], None, ALU.mult)
            dve.tensor_copy(GAB[0:8, :], R(7))
            dve_then(dve.tensor_copy(GAB[32:40, :], R(2)))
            dve.sem_inc(named("c_rows"), 1)
            for i in range(8):
                dve.wait_ge(named("l2_rs"), i + 1)
                o = QKV[:, 2 * i:2 * i + 2, :]
                dve.tensor_tensor(o, o, RSL[:, i % 2, :].rearrange("p (c n) -> p c n", c=2),
                                  ALU.mult).then_inc(named("l2_done"), 1)
            dve.wait_ge(named("c_cols"), 1)
            dve_then(dve.tensor_copy(GCB[:, :, :], PS[:, A, 0:80].rearrange("p (t n) -> p t n", t=2)))
            dve_then(dve.tensor_tensor(GX[:, 2, :], PS[:, A, 128:136], GCB[:, 0, 0:8], ALU.subtract))
            dve.sem_inc(named("c_gcb"), 1)

            def bc(col):
                return col.unsqueeze(2).to_broadcast([P, 4, P])

            def quad(bank):
                return PS[:, bank, :].rearrange("p (h n) -> p h n", h=4)

            for gi in range(4):
                hg, c = gi // 2, gi % 2
                dve.wait_ge(named("c_vt"), gi + 1)
                dve.tensor_tensor(RV[:, gi, :, :], quad(gi), bc(GCB[:, c, 32 + 4 * hg:36 + 4 * hg]),
                                  ALU.mult).then_inc(named("c_rv"), 1)
            dve.wait_ge(named("c_gx"), 2)
            dve_then(dve.tensor_tensor(GX[:, 1, :], GX[:, 0, :], GCB[:, 1, 32:40], ALU.mult))
            for gi in range(4):
                hg, c = gi // 2, gi % 2
                dve.wait_ge(named("c_kt"), gi + 1)
                dst, col = (RK, 1) if c else (KD, 3)
                dve.tensor_tensor(dst[:, hg, :, :], quad(4 + gi), bc(GX[:, col, 4 * hg:4 * hg + 4]),
                                  ALU.mult).then_inc(named("c_rk"), 1)
            for gi in range(4):
                hg, c = gi // 2, gi % 2
                pb = 4 * (gi % 2)
                dve.wait_ge(named("c_p"), 4 * gi + 1)
                if gi >= 2:
                    dve.wait_ge(named("c_dec"), gi - 1)
                for j in range(4):
                    ins = dve.scalar_tensor_tensor(out=TE[:, gi % 2, j, :], in0=PS[:, pb, j * P:(j + 1) * P],
                                                   scalar=GCB[:, c, 4 * hg + j:4 * hg + j + 1], in1=neg_ge[:, 0, :],
                                                   op0=ALU.subtract, op1=ALU.add)
                ins.then_inc(named("c_e"), 1)
                dve.wait_ge(named("c_dec"), gi + 1)
                dve.wait_ge(named("c_p"), 4 * gi + 4)
                dec = DEC[:, gi % 2, :, :]
                dve_then(dve.tensor_tensor(ATC[:, gi, :, :], quad(pb + 2), dec, ALU.mult))
                dve.tensor_tensor(ATT[:, gi, :, :], quad(pb + 3), dec, ALU.mult)
                if c:
                    dve.wait_ge(named("c_tq"), hg + 1)
                dve_then(dve.tensor_tensor(ATC[:, gi, :, :], quad(pb + 1), ATC[:, gi, :, :], ALU.mult))
                dve.sem_inc(named("c_prep"), 1)
            idb = ident[:, :].unsqueeze(1).to_broadcast([P, 4, P])
            for gi in range(4):
                dve.wait_ge(named("c_l0"), gi + 1)
                dve.tensor_tensor(XT[:, gi, :, :], idb, LT[:, gi, :, :], ALU.subtract)
                dve_then(dve.scalar_tensor_tensor(out=XI[:, gi, :, :], in0=quad(6 + gi % 2), scalar=-1.0, in1=idb,
                                                  op0=ALU.mult, op1=ALU.add))
                dve.sem_inc(named("c_x"), 1)
            NL = 4 * (LEVELS - 1)
            for n in range(NL):
                gi = n % 4
                dve.wait_ge(named("c_pq"), n + 1)
                if n < NL - 4:
                    dve.tensor_tensor(XI[:, gi, :, :], XI[:, gi, :, :], quad(2 + gi % 2), ALU.subtract)
                dve_then(dve.tensor_tensor(XT[:, gi, :, :], XT[:, gi, :, :], quad(4 + gi % 2), ALU.subtract))
                dve.sem_inc(named("c_x"), 1)
            for hg in range(2):
                dve.wait_ge(named("c_u0"), hg + 1)
                dve.tensor_copy(VN0[:, hg, :, :], quad(hg)).then_inc(named("c_vn0"), 1)
            for hg in range(2):
                dve.wait_ge(named("c_u1"), hg + 1)
                dve.tensor_copy(VN1[:, hg, :, :], quad(4 + hg)).then_inc(named("c_vn1"), 1)
            for hg in range(2):
                dve.wait_ge(named("c_o1"), hg + 1)
                dve_then(dve.tensor_copy(OC[:, 1, 512 * hg:512 * (hg + 1)], PS[:, 2 + hg, :]))
            dve.wait_ge(named("c_oc0"), 2)
            head_norm_dve(OC, OSQ, CST, 8, "c_ssq", "c_hrs",
                          row[:, ROW_CHEAD:ROW_CHEAD + P].unsqueeze(1).to_broadcast([P, 8, P]), SGC, "c_om")

        def final_act():
            resid(9)(act)
            act.activation(HN[:, 1, :], X[:, 1, :], ACT.Square, accum_out=stat[:, 1:2]).then_inc(s_stat, 1)
            act.wait_ge(s_stat, 2 * 11)
            act_then(act.activation(lnv[:, :], stat[:, :], ACT.Ln, bias=eps_c[:, 0:1], scale=1.0 / D))
            act.activation(rstd[:, :], lnv[:, :], ACT.Exp, scale=-0.5).then_inc(s_rstd, 1)

        def final_dve():
            resid(9)(dve)
            dve.tensor_tensor_reduce(out=HN[:, 0, :], in0=X[:, 0, :], in1=X[:, 0, :], scale=1.0, scalar=0.0,
                                     op0=ALU.mult, op1=ALU.add, accum_out=stat[:, 0:1]).then_inc(s_stat, 1)
            dve.wait_ge(s_stat, 2 * 11)
            dve.wait_ge(s_rstd, 11)
            for t in range(TT):
                dve.scalar_tensor_tensor(out=HN[:, t, :], in0=X[:, t, :], scalar=rstd[:, t:t + 1],
                                         in1=row[:, ROW_FINAL:ROW_FINAL + D], op0=ALU.mult,
                                         op1=ALU.mult).then_inc(named("final"), 1)

        def final_sp(sp):
            for t in range(TT):
                sp.wait_ge(named("final"), t + 1)
                sp.dma_start(out[t * P:(t + 1) * P, :], HN[:, t, :]).then_inc(s_out, 16)
            sp.wait_ge(s_out, 16 * TT)

        from_stage = {"mix": "up", "ffn": "ple_gate", "ple": "ab_qk", "mixer0": "xk0", "xa0": "m10", "mlp0": "c_qkv",
                      "mixer1": "xk1", "xa1": "m11"}
        stop_unit = first_unit[from_stage[stop]] if stop in from_stage else len(plan)
        STAGES = ["mix", "ffn", "ple", "mixer0", "xa0", "mlp0", "mixer1", "xa1", "mlp1"]
        upto = STAGES.index(stop) if stop in STAGES else 99

        block = ctx.enter_context(nc.Block())

        @block.sync
        def _(sp):
            small_sp(sp)
            weights_sp(sp)
            if stop:
                sp.wait_ge(s_x, 4 * (upto + 1))
                sp.dma_start(out.rearrange("(t p) d -> p t d", p=P), X[:, :, :]).then_inc(s_out, 16)
                sp.wait_ge(s_out, 16)
            else:
                final_sp(sp)

        @block.gpsimd
        def _(p_):
            consts_pool()
            c_consts_pool()
            if upto >= 1:
                up_pool()
            if upto >= 6:
                c_pool()

        @block.tensor
        def _(p_):
            pe.wait_ge(s_const, 1)
            turn_pe(0, HN, norm_ready_pe(0))
            turn_pe(1, HN, norm_ready_pe(1), free=lambda: (pe.wait_ge(s_tpd, 2), pe.wait_ge(s_tpa, 2)))
            qk_pe()
            v_pe()
            attn_pe()
            turn_pe(2, OM, lambda t: pe.wait_ge(named("mix_out"), t + 1))
            rows_product("w_out", HT, DC, ready=turned(2, pe), free=lambda: pe.wait_ge(named("v1_ready"), 4))
            if upto >= 1:
                turn_pe(3, HN, norm_ready_pe(2))
                up_pe()
                down_pe()
            if upto >= 2:
                turn_pe(4, HN, norm_ready_pe(3))
                ple_pe()
            if upto >= 3:
                turn_pe(5, HN, norm_ready_pe(4))
                ab_pe()
                turn_pe(6, OM2, lambda t: (pe.wait_ge(named("ab_om"), t + 1), pe.wait_ge(named("ab_o"), 8)))
                rows_product("ab_out", HT, DC, ready=turned(6, pe))
            for l in range(2):
                if l and upto >= 6:
                    turn_pe(9, HN, norm_ready_pe(7))
                    c_pe()
                    turn_pe(10, OC, lambda t: pe.wait_ge(named("c_om"), t + 1))
                    rows_product("c_out", HT, DC, ready=turned(10, pe))
                if upto >= 4 + 3 * l:
                    xa_kv_pe(l)
                    turn_pe(7 + 4 * l, HN, norm_ready_pe(5 + 3 * l))
                    xa_pe(l, 7 + 4 * l)
                if upto >= 5 + 3 * l:
                    turn_pe(8 + 4 * l, HN, norm_ready_pe(6 + 3 * l))
                    mlp_pe(l, 8 + 4 * l)

        @block.scalar
        def _(p_):
            act.wait_ge(s_const, 1)
            norm_act(0, MEM, lambda e: e.wait_ge(s_mem, 16))
            act.wait_ge(s_small, 16 * N_SMALL)
            turn_act(0, MEMT, LN_MEM)
            norm_act(1, X, lambda e: (e.wait_ge(s_x_in, 16), e.wait_ge(s_tp, 4)))
            turn_act(1, HT, LN_MIX)
            lam_act()
            qk_act()
            v_act()
            attn_act()
            subln_act()
            turn_act(2, HT)
            if upto >= 1:
                norm_act(2, X, resid(1))
                turn_act(3, HT, LN_FFN)
                up_act()
            if upto >= 2:
                norm_act(3, X, resid(2))
                turn_act(4, HT, LN_PLE)
                ple_act()
            if upto >= 3:
                norm_act(4, X, resid(3))
                turn_act(5, HT, LN_MIX0)
                ab_act()
                turn_act(6, HT)
            for l in range(2):
                if l and upto >= 6:
                    norm_act(7, X, resid(6))
                    turn_act(9, HT, LN_MIX1)
                    c_act()
                    turn_act(10, HT)
                if upto >= 4 + 3 * l:
                    xa_kv_evac(l, act)
                    norm_act(5 + 3 * l, X, resid(4 + 3 * l))
                    turn_act(7 + 4 * l, HT, LN_XA0 + 3 * l)
                    xa_act(l)
                if upto >= 5 + 3 * l:
                    norm_act(6 + 3 * l, X, resid(5 + 3 * l))
                    turn_act(8 + 4 * l, HT, LN_MLP0 + 3 * l)
                    mlp_act(l)
            if not stop:
                final_act()

        @block.vector
        def _(p_):
            dve.wait_ge(s_const, 1)
            norm_dve(0, MEM, lambda e: e.wait_ge(s_mem, 16))
            dve.wait_ge(s_small, 16 * N_SMALL)
            turn_dve(0, MEMT, LN_MEM)
            norm_dve(1, X, lambda e: (e.wait_ge(s_x_in, 16), e.wait_ge(s_tp, 4)))
            turn_dve(1, HT, LN_MIX)
            biases_dve()
            qk_dve()
            fg_dve()
            attn_dve()
            turn_dve(2, HT)
            resid_add_dve("w_out")
            if upto >= 1:
                norm_dve(2, X, resid(1))
                turn_dve(3, HT, LN_FFN)
                up_dve()
                resid_add_dve("down")
            if upto >= 2:
                norm_dve(3, X, resid(2))
                turn_dve(4, HT, LN_PLE)
                ple_dve()
            if upto >= 3:
                norm_dve(4, X, resid(3))
                turn_dve(5, HT, LN_MIX0)
                ab_dve()
                turn_dve(6, HT)
                resid_add_dve("ab_out")
            for l in range(2):
                if l and upto >= 6:
                    norm_dve(7, X, resid(6))
                    turn_dve(9, HT, LN_MIX1)
                    c_dve()
                    turn_dve(10, HT)
                    resid_add_dve("c_out")
                if upto >= 4 + 3 * l:
                    xa_kv_evac(l, dve)
                    norm_dve(5 + 3 * l, X, resid(4 + 3 * l))
                    turn_dve(7 + 4 * l, HT, LN_XA0 + 3 * l)
                    xa_dve(l)
                    resid_add_dve(f"xo{l}")
                if upto >= 5 + 3 * l:
                    norm_dve(6 + 3 * l, X, resid(5 + 3 * l))
                    turn_dve(8 + 4 * l, HT, LN_MLP0 + 3 * l)
                    mlp_dve(l)
                    resid_add_dve(f"m2{l}")
            if not stop:
                final_dve()


def laid_out(v):
    import numpy as np

    f = {k: np.asarray(a) for k, a in v.items()}
    wi, ab, cw = f["w_in"][0], f["ab_w_in_2"][0], f["c_w_in_2"][0]
    a = {"x": f["x"][0], "mem": f["mem_2"][0], "p": f["p"][0, 0]}
    a["w_in"] = np.concatenate([wi[:, 0:1024], wi[:, 1280:2048], wi[:, 2438:3206], wi[:, 1024:1280],
                                wi[:, 2048:2432], wi[:, 3206:3590]], axis=1)
    a["w_out"], a["w_up"], a["w_down"] = f["w_out"][0], f["w_up"][0], f["w_down"][0]
    a["w_ple_gate"], a["w_ple_proj"] = f["w_ple_gate"][0], f["w_ple_proj"][0]
    a["ab_w_in"] = np.concatenate([ab[:, 1544:2568], ab[:, 0:512], ab[:, 512:1536], ab[:, 2568:3080]], axis=1)
    a["ab_w_out"], a["c_w_out"] = f["ab_w_out_2"][0], f["c_w_out_2"][0]
    a["c_w_in"] = cw[:, 0:4096]
    for l in range(2):
        for n in ("xa_wq", "xa_wk", "xa_wv", "xa_wo", "mlp_w1", "mlp_w2"):
            a[f"{n}{l}"] = f[f"{n}_2"][l]
    a["gate_w"] = np.concatenate([wi[:, 2432:2438], ab[:, 1536:1544], cw[:, 4096:4112]], axis=1)
    lns = np.stack([f["ln_mix"][0], f["ln_ffn"][0], f["ln_ple"][0], f["mem_norm_2"], f["mix_norm_2"][0],
                    f["xa_norm_2"][0], f["mlp_norm_2"][0], f["mix_norm_2"][1], f["xa_norm_2"][1], f["mlp_norm_2"][1]])
    a["ln_cols"] = lns.reshape(10, 8, 128).transpose(2, 0, 1).reshape(128, 80)
    a["qk_cols"] = np.concatenate([f["qk_gain"][0].T, f["qk_gain"][0].T], axis=0)
    a["row"] = np.concatenate([f["subln_gain"][0], f["ab_head_gain_2"][0].reshape(-1), f["c_head_gain_2"][0],
                               f["lam_params"][0].reshape(-1), f["final_norm_2"]])[None, :]
    cc = np.concatenate([f["conv_w"][0], f["conv_b"]], axis=0)
    a["conv_cols"] = cc.reshape(4, 44, 128).transpose(2, 1, 0).reshape(128, 176)
    a["cconv_cols"] = f["c_conv_w_2"][0].reshape(4, 24, 128).transpose(2, 1, 0).reshape(128, 96)
    gp = np.zeros((8, 5), np.float32)
    gp[0:6, 0], gp[0:4, 1], gp[0:4, 2] = f["fgate_bias"][0], f["ab_b_i_2"][0], f["ab_b_f_2"][0]
    gp[:, 3], gp[:, 4] = f["c_a_log_2"][0], f["c_dt_bias_2"][0]
    a["gate_p"] = gp
    a["rel_rev"] = f["rel_bias"][0][:, ::-1]
    return {k: np.ascontiguousarray(x) for k, x in a.items()}


STOP = None


def kernel(**inputs):
    import numpy as _np
    import concourse.bacc as _bacc
    from concourse import mybir as _mybir
    from concourse.bass_utils import run_bass_kernel_spmd as _run

    nc = _bacc.Bacc("TRN2", target_bir_lowering=False, num_devices=1)
    arrays = laid_out(inputs)
    I = {n: nc.dram_tensor(f"in_{n}", a.shape, _mybir.dt.from_np(a.dtype), kind="ExternalInput").ap()
         for n, a in arrays.items()}
    out = nc.dram_tensor("out_0", (T, D), _mybir.dt.float32, kind="ExternalOutput").ap()
    scratch = nc.dram_tensor("rel_rows", (6, P, 511), _mybir.dt.float32).ap()
    build_two_blocks(nc, I, out, scratch, STOP)
    r = _run(nc, [{f"in_{n}": a for n, a in arrays.items()}], core_ids=[0])
    return _np.asarray(r.results[0]["out_0"]).reshape(1, T, D)
```

```python
from contextlib import ExitStack

import concourse.bass as bass
from concourse import mybir

P = 128
T = 256
TT = T // P
D = 1024
DC = D // P
EPS = 1e-6
BIG = 1e30
RING = 4
UNIT = 2048
PART = UNIT // 2
PARTS = 4

F32 = mybir.dt.float32
F32R = mybir.dt.float32r
ALU = mybir.AluOpType
ACT = mybir.ActivationFunctionType
AX = mybir.AxisListType

LN_MIX, LN_FFN, LN_PLE, LN_MEM, LN_MIX0, LN_XA0, LN_MLP0, LN_MIX1, LN_XA1, LN_MLP1 = range(10)
EXP_LN = "natural_log_exp_and_others"
ROW_SUBLN, ROW_ABHEAD, ROW_CHEAD, ROW_LAM, ROW_FINAL, ROW_LEN = 0, 64, 576, 704, 960, 1984

D_FF = 2816
FF_TILES = D_FF // P
D_FF_2 = 4096
FF2_TILES = D_FF_2 // P
LAM_INIT = 0.2


def weight_plan():
    plan = []

    def cols(stage, w, starts):
        plan.extend((stage, w, "cols", c) for c in starts)

    def rows(stage, w, chunks, c0=0, width=D):
        per = UNIT // width
        for k in range(0, chunks, per):
            plan.append((stage, w, "rows", (k, min(per, chunks - k), c0, width)))

    cols("qk", "w_in", range(0, 2560, 256))
    rows("v", "w_in", DC, 2560)
    cols("fg", "gates", [0])
    rows("w_out", "w_out", DC)
    for j in range(D_FF // 256):
        cols("up", "w_up", (256 * j, D_FF + 256 * j))
    rows("down", "w_down", FF_TILES)
    rows("ple_gate", "w_ple_gate", DC)
    rows("ple_proj", "w_ple_proj", 2)
    cols("ab_qk", "ab_w_in", range(0, 1536, 256))
    cols("ab_g", "gates", [256])
    rows("ab_vo", "ab_w_in", DC, 1536)
    rows("ab_sv", "ab_w_in", DC, 2560, 512)
    rows("ab_out", "ab_w_out", DC)
    for l in range(2):
        if l:
            cols("c_qkv", "c_w_in", range(0, 3072, 256))
            rows("c_gate", "c_w_in", DC, 3072)
            cols("c_g", "gates", [512])
            rows("c_out", "c_w_out", DC)
        cols(f"xk{l}", f"xa_wk{l}", range(0, D, 256))
        rows(f"xv{l}", f"xa_wv{l}", DC)
        cols(f"xq{l}", f"xa_wq{l}", range(0, D, 256))
        rows(f"xo{l}", f"xa_wo{l}", DC)
        cols(f"m1{l}", f"mlp_w1{l}", range(0, D_FF_2, 256))
        rows(f"m2{l}", f"mlp_w2{l}", FF2_TILES)
    return plan


def build_two_blocks(nc, I, out, scratch, stop=None):
    plan = weight_plan()
    first_unit = {}
    for n, (stage, *_r) in enumerate(plan):
        first_unit.setdefault(stage, n)

    if True:
        from_stage = {"mix": "up", "ffn": "ple_gate", "ple": "ab_qk", "mixer0": "xk0", "xa0": "m10", "mlp0": "c_qkv",
                      "mixer1": "xk1", "xa1": "m11"}
        stop_unit = first_unit[from_stage[stop]] if stop in from_stage else len(plan)
        STAGES = ["mix", "ffn", "ple", "mixer0", "xa0", "mlp0", "mixer1", "xa1", "mlp1"]
        upto = STAGES.index(stop) if stop in STAGES else 99

    with ExitStack() as ctx:
        def sb(name, shape, dtype=F32):
            return ctx.enter_context(nc.sbuf_tensor(name, shape, dtype))

        def sem(name):
            return ctx.enter_context(nc.semaphore(name))

        X = sb("resid", [P, TT, D])
        HN = sb("normed", [P, TT, D])
        MEMT = [sb(f"mem_t_{x}", [P, DC, T], F32R) for x in ("hi", "lo")]
        raw = sb("weights", [P, RING, UNIT])
        WH = sb("weights_hi", [P, PARTS, PART], F32R)
        WL = sb("weights_lo", [P, PARTS, PART], F32R)
        ARENA = 84 * 256
        with nc.sbuf_tensor("split_arena", [P, ARENA], F32R) as split_arena:
            pass
        arena = sb("arena", [P, ARENA])
        ident = sb("ident", [P, P])
        ones = sb("ones", [P, P])
        halves = sb("halves", [P, P])
        tri = sb("tri", [P, P])
        sel = sb("sel", [8, 8, P])
        neg_ge = sb("neg_ge", [P, 3, P])
        neg_gt = sb("neg_gt", [P, 3, P])
        ln_cols = sb("ln_cols", [P, 10, DC])
        qk_cols = sb("qk_cols", [P, 6])
        qk_fold = sb("qk_fold", [P, 6])
        row = sb("row", [P, ROW_LEN])
        conv_cols = sb("conv_cols", [P, 2 * FF_TILES, 4])
        cconv_cols = sb("cconv_cols", [P, 24, 4])
        gate_p = sb("gate_p", [8, 5])
        stat = sb("stat", [P, 2])
        lnv = sb("lnv", [P, 2])
        rstd = sb("rstd", [P, 2])
        eps_c = sb("eps_c", [P, 1])
        eps64_c = sb("eps64_c", [P, 1])
        one_c = sb("one_c", [P, 1])
        lam = sb("lam", [P, 8])
        PS = ctx.enter_context(nc.psum_tensor("ps", [P, 8, 512], F32))
        G, A = 0, 4

        def view(first, shape, parts=P, of=None):
            n = 1
            for s in shape:
                n *= s
            v = (arena if of is None else of)[0:parts, first:first + n]
            if len(shape) == 1:
                return v
            names = "abcd"[:len(shape)]
            spec = {c: s for c, s in zip(names, shape)}
            return v.rearrange(f"p ({' '.join(names)}) -> p {' '.join(names)}", **spec)

        def pair(first, chunks):
            return [view(first + i * chunks * T, (chunks, T), of=split_arena) for i in range(2)]

        HT = pair(0, DC)

        s_x_in = sem("x_loaded")
        s_small = sem("small_loaded")
        s_const = sem("constants_built")
        s_pool_chain = sem("pool_chain")
        s_act_chain = sem("act_chain")
        s_dve_chain = sem("dve_chain")
        s_unit = [sem(f"unit_landed_{i}") for i in range(RING)]
        s_hi = sem("weights_hi_ready")
        s_lo = sem("weights_lo_ready")
        s_used = sem("part_used")
        s_x = sem("resid_ready")
        s_stat = sem("norm_squares")
        s_rstd = sem("norm_rstd")
        s_hn0 = sem("normed_tile0")
        s_hn1 = sem("normed_tile1")
        s_tp = sem("transposed")
        s_th = sem("turned_hi")
        s_tl = sem("turned_lo")
        s_acc = sem("rows_product_done")
        s_out = sem("out_stored")

        S = {}

        def named(name):
            if name not in S:
                S[name] = sem(name)
            return S[name]

        chain_n = {"act": 0, "dve": 0, "pool": 0}

        def act_then(ins):
            chain_n["act"] += 1
            ins.then_inc(s_act_chain, 1)
            nc.scalar.wait_ge(s_act_chain, chain_n["act"])

        def dve_then(ins):
            chain_n["dve"] += 1
            ins.then_inc(s_dve_chain, 1)
            nc.vector.wait_ge(s_dve_chain, chain_n["dve"])

        def pool_then(ins):
            chain_n["pool"] += 1
            ins.then_inc(s_pool_chain, 1)
            nc.gpsimd.wait_ge(s_pool_chain, chain_n["pool"])

        dve, act, pool, pe = nc.vector, nc.scalar, nc.gpsimd, nc.tensor

        def weights_sp(sp):
            for n, (stage, w, kind, at) in enumerate(plan):
                if n >= stop_unit:
                    break
                slot = n % RING
                if n >= RING:
                    sp.wait_ge(s_lo, 2 * (n - RING) + 2)
                W = I[w]
                if kind == "cols":
                    dst = raw[:, slot, :].rearrange("p (c n) -> p c n", c=DC)
                    src = W[:, at:at + 256].rearrange("(c p) n -> p c n", p=P)
                else:
                    k, per, c0, width = at
                    dst = raw[:, slot, 0:per * width].rearrange("p (c n) -> p c n", c=per)
                    src = W[k * P:(k + per) * P, c0:c0 + width].rearrange("(c p) n -> p c n", p=P)
                sp.dma_start(dst, src).then_inc(s_unit[slot], 16)

        def part_views(p):
            r, h, l = raw[:, (p // 2) % RING, :], WH[:, p % PARTS, :], WL[:, p % PARTS, :]
            if plan[p // 2][2] == "cols":
                r = r.rearrange("p (c n) -> p c n", c=DC)[:, :, (p % 2) * P:(p % 2 + 1) * P]
                return r, h.rearrange("p (c n) -> p c n", c=DC), l.rearrange("p (c n) -> p c n", c=DC)
            return r[:, (p % 2) * PART:(p % 2 + 1) * PART], h, l

        split_n = {"act": 0, "dve": 0}

        def split(eng, upto):
            who = "act" if eng is act else "dve"
            for p in range(split_n[who], min(upto + 1, 2 * stop_unit)):
                r, h, l = part_views(p)
                n = p // 2
                if eng is act:
                    act.wait_ge(s_unit[n % RING], 16 * (n // RING + 1))
                    if p >= PARTS:
                        act.wait_ge(s_used, p - PARTS + 1)
                    act.activation(h, r, ACT.Copy).then_inc(s_hi, 1)
                else:
                    dve.wait_ge(s_hi, p + 1)
                    dve.tensor_tensor(l, r, h.bitcast(F32), ALU.subtract).then_inc(s_lo, 1)
                split_n[who] = p + 1

        def last_part(stage):
            return 2 * max(n for n, x in enumerate(plan) if x[0] == stage) + 1

        def split_through(eng, stage, more):
            split(eng, last_part(stage) + more)

        def cols_unit(stage, u, rhs, banks, free=None, ready=None):
            n = first_unit[stage] + u
            if free:
                free(u)
            for f in range(2):
                p = 2 * n + f
                pe.wait_ge(s_lo, p + 1)
                _r, wh, wl = part_views(p)
                o = PS[:, banks, f * T:(f + 1) * T] if isinstance(banks, int) else PS[:, banks[f], 0:T]
                for k in range(DC):
                    if ready and u == 0 and f == 0:
                        ready(k)
                    for i, (w, x) in enumerate(((wh, rhs[0]), (wh, rhs[1]), (wl, rhs[0]))):
                        mm = pe.matmul(o, w[:, k, :], x[:, k, :], start=(k == 0 and i == 0),
                                       stop=(k == DC - 1 and i == 2))
                mm.then_inc(s_used, 1)

        def cols_done(eng, stage, u):
            last = 2 * (first_unit[stage] + u) + 1
            if eng is act or eng is dve:
                split(eng, last + 3)
            eng.wait_ge(s_used, last + 1)

        ROWS = {}
        acc = 0
        for stage, width in (("v", D), ("w_out", D), ("down", D), ("ple_gate", D), ("ple_proj", D), ("ab_vo", D),
                             ("ab_sv", 512), ("ab_out", D), ("xv0", D), ("xo0", D), ("m20", D), ("c_gate", D),
                             ("c_out", D), ("xv1", D), ("xo1", D), ("m21", D)):
            banks = TT * width // 512
            ROWS[stage] = (banks, acc)
            acc += banks - 1

        def rows_done(eng, stage, b, more=2):
            banks, before = ROWS[stage]
            split_through(eng, stage, more)
            if b < banks - 1:
                eng.wait_ge(s_acc, before + b + 1)
            else:
                eng.wait_ge(s_used, last_part(stage) + 1)

        def rows_product(stage, lhs, chunks, width=D, base=G, ready=None, free=None):
            per = PART // width
            nb = width // 512
            p = 2 * first_unit[stage]
            for k0 in range(0, chunks, per):
                pe.wait_ge(s_lo, p + 1)
                _r, wh, wl = part_views(p)
                for k in range(k0, k0 + per):
                    if ready:
                        ready(k)
                    if k == 0 and free:
                        free()
                    for t in range(TT):
                        for i, (x, w) in enumerate(((lhs[0], wh), (lhs[0], wl), (lhs[1], wh))):
                            for b in range(nb):
                                c = (k - k0) * width + b * 512
                                mm = pe.matmul(PS[:, base + nb * t + b, :], x[:, k, t * P:(t + 1) * P],
                                               w[:, c:c + 512], start=(k == 0 and i == 0),
                                               stop=(k == chunks - 1 and i == 2))
                                if k == chunks - 1 and i == 2 and not (t == TT - 1 and b == nb - 1):
                                    mm.then_inc(s_acc, 1)
                mm.then_inc(s_used, 1)
                p += 1

        def norm_dve(i, src, ready):
            ready(dve)
            dve.tensor_tensor_reduce(out=HN[:, 0, :], in0=src[:, 0, :], in1=src[:, 0, :], scale=1.0, scalar=0.0,
                                     op0=ALU.mult, op1=ALU.add, accum_out=stat[:, 0:1]).then_inc(s_stat, 1)
            dve.wait_ge(s_rstd, i + 1)
            dve.tensor_scalar(HN[:, 0, :], src[:, 0, :], rstd[:, 0:1], None, ALU.mult).then_inc(s_hn0, 1)

        def norm_act(i, src, ready):
            ready(act)
            act.activation(HN[:, 1, :], src[:, 1, :], ACT.Square, accum_out=stat[:, 1:2]).then_inc(s_stat, 1)
            act.wait_ge(s_stat, 2 * (i + 1))
            act_then(act.activation(lnv[:, :], stat[:, :], ACT.Ln, bias=eps_c[:, 0:1], scale=1.0 / D))
            act.activation(rstd[:, :], lnv[:, :], ACT.Exp, scale=-0.5).then_inc(s_rstd, 1)
            act.wait_ge(s_rstd, i + 1)
            act.activation(HN[:, 1, :], src[:, 1, :], ACT.Copy, scale=rstd[:, 1:2]).then_inc(s_hn1, 1)

        def turn_pe(m, src, ready, free=None):
            if free:
                free()
            for c2 in range(4):
                for c in (2 * c2, 2 * c2 + 1):
                    for t in range(TT):
                        if c2 == 0:
                            ready(t)
                        mm = pe.transpose(PS[:, A + c2, (c % 2) * T + t * P:(c % 2) * T + (t + 1) * P],
                                          src[:, t, c * P:(c + 1) * P], ident[:, :])
                mm.then_inc(s_tp, 1)

        def turn_act(m, dst, gain=None):
            for c2 in range(4):
                act.wait_ge(s_tp, 4 * m + c2 + 1)
                if gain is None:
                    act.activation(dst[0][:, 2 * c2:2 * c2 + 2, :],
                                   PS[:, A + c2, :].rearrange("p (c n) -> p c n", c=2), ACT.Copy).then_inc(s_th, 1)
                else:
                    for c in (0, 1):
                        ins = act.activation(dst[0][:, 2 * c2 + c, :], PS[:, A + c2, c * T:(c + 1) * T], ACT.Copy,
                                             scale=ln_cols[:, gain, 2 * c2 + c:2 * c2 + c + 1])
                    ins.then_inc(s_th, 1)

        def turn_dve(m, dst, gain=None):
            for c2 in range(4):
                dve.wait_ge(s_th, 4 * m + c2 + 1)
                if gain is None:
                    cc = slice(2 * c2, 2 * c2 + 2)
                    dve.tensor_tensor(dst[1][:, cc, :], PS[:, A + c2, :].rearrange("p (c n) -> p c n", c=2),
                                      dst[0][:, cc, :].bitcast(F32), ALU.subtract).then_inc(s_tl, 1)
                else:
                    for c in (0, 1):
                        k = 2 * c2 + c
                        ins = dve.scalar_tensor_tensor(
                            out=dst[1][:, k, :], in0=PS[:, A + c2, c * T:(c + 1) * T],
                            scalar=ln_cols[:, gain, k:k + 1], in1=dst[0][:, k, :].bitcast(F32), op0=ALU.mult,
                            op1=ALU.subtract)
                    ins.then_inc(s_tl, 1)

        def turned(m, eng):
            def ready(k):
                if k % 2 == 0:
                    eng.wait_ge(s_tl, 4 * m + k // 2 + 1)
            return ready

        def norm_ready_pe(i):
            def ready(t):
                pe.wait_ge((s_hn0, s_hn1)[t], i + 1)
            return ready

        SUMMED = ["w_out", "down", "ple_proj", "ab_out", "xo0", "m20", "c_out", "xo1", "m21"]

        def resid(r):
            def ready(eng):
                if r:
                    split_through(eng, SUMMED[r - 1], 2)
                    eng.wait_ge(s_x, 4 * r)
                else:
                    eng.wait_ge(s_x_in, 16)
            return ready

        def resid_add_dve(stage):
            for b in range(4):
                rows_done(dve, stage, b)
                x = X[:, b // 2, (b % 2) * 512:(b % 2 + 1) * 512]
                dve.tensor_tensor(x, PS[:, G + b, :], x, ALU.add).then_inc(s_x, 1)

        MEM = view(36 * 256, (TT, D))
        relrow = view(80 * 256, (257,), 6)
        relext = view(82 * 256, (511,), 6)
        qkT = view(16 * 256, (20, T))
        V1 = view(36 * 256, (TT, D))
        OM = view(44 * 256, (TT, D))
        BT = view(52 * 256, (11, T))
        SQ = view(63 * 256, (2, 512))
        RS = view(67 * 256, (2, 512))
        FG = view(63 * 256, (8, T), 8)
        FL = view(71 * 256, (T,), 102)
        FR = view(72 * 256, (6, T), 102)
        SN = view(0, (3, T))
        PT = view(3 * 256, (3, T))
        MN = view(6 * 256, (40,))
        LS = view(6 * 256 + 40, (40,))
        RL = view(6 * 256 + 80, (40,))
        OD = view(7 * 256, (2, 64))
        DSQ = view(8 * 256, (8, 64))
        DST = view(10 * 256, (3, 8))

        def small_sp(sp):
            sp.dma_start(MEM, I["mem"].rearrange("(t p) d -> p t d", p=P)).then_inc(s_mem, 16)
            sp.dma_start(X[:, :, :], I["x"].rearrange("(t p) d -> p t d", p=P)).then_inc(s_x_in, 16)
            for dst, src in ((ln_cols[:, :, :], I["ln_cols"].rearrange("p (a b) -> p a b", a=10)),
                             (qk_cols[:, :], I["qk_cols"]),
                             (gate_p[:, :], I["gate_p"]),
                             (relrow[:, :], I["rel_rev"]),
                             (row[:, :], I["row"].to_broadcast([P, ROW_LEN])),
                             (conv_cols[:, :, :], I["conv_cols"].rearrange("p (a b) -> p a b", b=4)),
                             (cconv_cols[:, :, :], I["cconv_cols"].rearrange("p (a b) -> p a b", b=4)),
                             (PIN, I["p"].rearrange("(t p) d -> p t d", p=P))):
                sp.dma_start(dst, src).then_inc(s_small, 16)

        N_SMALL = 8
        PIN_t = sb("p_in", [P, TT, 256])
        PIN = PIN_t[:, :, :]
        s_mem = sem("mem_loaded")

        def consts_pool():
            sel_ge = ALU.is_ge
            pool_then(pool.memset(ident[:, :], 0.0))
            pool_then(pool.affine_select(out=ident[:, :], in_=ident[:, :], compare_op=ALU.not_equal, fill=1.0,
                                         base=0, pattern=[[-1, P]], channel_multiplier=1))
            pool.memset(ones[:, :], 1.0)
            pool.memset(eps_c[:, :], EPS)
            pool.memset(eps64_c[:, :], 64 * EPS)
            pool_then(pool.memset(one_c[:, :], 1.0))
            pool.sem_inc(s_const, 1)
            pool.memset(halves[:, :], 0.0)
            pool.memset(tri[:, :], 1.0)
            pool.memset(sel[:, :, :], 0.0)
            pool.memset(neg_ge[:, :, :], 0.0)
            pool_then(pool.memset(neg_gt[:, :, :], 0.0))
            pool_then(pool.memset(halves[0:64, 0:64], 1.0))
            pool_then(pool.memset(halves[64:128, 64:128], 1.0))
            pool.affine_select(out=tri[:, :], in_=tri[:, :], compare_op=sel_ge, fill=0.0, base=0,
                               pattern=[[-1, P]], channel_multiplier=1)
            pool.affine_select(out=sel[:, :, :], in_=sel[:, :, :], compare_op=ALU.not_equal, fill=1.0, base=0,
                               pattern=[[-1, 8], [0, P]], channel_multiplier=1)
            for b in (0, 2):
                pool.affine_select(out=neg_gt[:, b, :], in_=neg_gt[:, b, :], compare_op=sel_ge, fill=-BIG,
                                   base=-1, pattern=[[1, P]], channel_multiplier=-1)
                last = pool.affine_select(out=neg_ge[:, b, :], in_=neg_ge[:, b, :], compare_op=sel_ge, fill=-BIG,
                                          base=0, pattern=[[1, P]], channel_multiplier=-1)
            pool_then(last)
            pool.sem_inc(s_const, 1)
            pool.iota(BT[:, 0, :], pattern=[[-1, T]], base=P, channel_multiplier=1,
                      allow_small_or_imprecise_dtypes=True).then_inc(named("dist"), 1)
            pool_then(pool.memset(BT[:, 4, :], 0.0))
            pool.affine_select(out=BT[:, 4, :], in_=BT[:, 4, :], compare_op=sel_ge, fill=BIG, base=P,
                               pattern=[[-1, T]], channel_multiplier=1).then_inc(named("causal"), 1)
            pool.wait_ge(named("relext"), 1)
            pool.dma_start(scratch[:, :, :], relext[:, :].unsqueeze(1).to_broadcast([6, P, 511])
                           ).then_inc(named("rel_out"), 16)
            pool.wait_ge(named("rel_out"), 16)
            for h in range(6):
                src = bass.AP(scratch.tensor, h * P * 511 + 127, [[510, P], [1, T]])
                pool.dma_start(BT[:, 5 + h, :], src).then_inc(named("rel_in"), 16)

        def biases_dve():
            dve.wait_ge(s_small, 16 * N_SMALL)
            dve.tensor_copy(relext[:, 127:384], relrow[:, :])
            dve.tensor_copy(relext[:, 0:127], relrow[:, 0:1].to_broadcast([6, 127]))
            dve_then(dve.tensor_copy(relext[:, 384:511], relrow[:, 256:257].to_broadcast([6, 127])))
            dve.sem_inc(named("relext"), 1)
            r = row[:, ROW_LAM:ROW_LAM + 256].rearrange("p (a n) -> p a n", a=4)
            for j in range(2):
                dve.tensor_tensor_reduce(out=HN[:, 0, 64 * j:64 * j + 64], in0=r[:, 2 * j, :], in1=r[:, 2 * j + 1, :],
                                         scale=1.0, scalar=0.0, op0=ALU.mult, op1=ALU.add,
                                         accum_out=lam[:, j:j + 1]).then_inc(named("lam_dots"), 1)
            dve.wait_ge(named("lam_exp"), 1)
            dve_then(dve.tensor_tensor(lam[:, 4:5], lam[:, 3:4], lam[:, 2:3], ALU.subtract))
            dve_then(dve.tensor_scalar(lam[:, 5:6], lam[:, 4:5], -LAM_INIT, None, ALU.add))
            for j in range(6):
                dve.tensor_scalar(qk_fold[:, j:j + 1], qk_cols[:, j:j + 1], (-1.0, 8.0)[j % 2], None, ALU.mult)
            dve_then(dve.tensor_scalar(row[:, ROW_SUBLN:ROW_SUBLN + 64], row[:, ROW_SUBLN:ROW_SUBLN + 64],
                                       1.0 - LAM_INIT, None, ALU.mult))
            dve.wait_ge(named("dist"), 1)
            for h in (1, 2, 3, 0):
                slope = 2.0 ** (-2.0 * (h + 1))
                dve_then(dve.tensor_scalar(BT[:, h, :], BT[:, 0, :], slope, None, ALU.mult))
            dve_then(dve.scalar_tensor_tensor(out=BT[:, 0:4, :], in0=BT[:, 0:4, :], scalar=-1.0, in1=BT[:, 0:4, :],
                                              op0=ALU.mult, op1=ALU.max))
            dve.wait_ge(named("rel_in"), 16 * 6)
            dve_then(dve.tensor_scalar(BT[:, 5:11, :], BT[:, 5:11, :], -1.0, None, ALU.mult))
            dve.memset(BT[0:64, 0:4, 192:256], BIG)
            dve_then(dve.memset(BT[0:64, 5:11, 192:256], BIG))

        def lam_act():
            act.wait_ge(named("lam_dots"), 2)
            act.activation(lam[:, 2:4], lam[:, 0:2], ACT.Exp).then_inc(named("lam_exp"), 1)

        QGAIN = [0] * 4 + [1] * 4 + [2] * 3 + [3] * 3 + [4] * 3 + [5] * 3

        def qk_pe():
            def free(u):
                if u >= 4:
                    pe.wait_ge(named("qk_done"), 2 * (u - 3))

            def squares(u):
                pe.wait_ge(named("qk_sq"), u + 1)
                if u >= 2:
                    pe.wait_ge(named("qk_rs"), u - 1)
                elif u == 0:
                    pe.wait_ge(s_const, 2)
                    pe.wait_ge(s_tl, 4 * 2)
                pe.matmul(PS[:, A + u % 2, :], halves[:, :], SQ[:, u % 2, :], start=True,
                          stop=True).then_inc(named("qk_ss"), 1)

            for u in range(10):
                cols_unit("qk", u, HT, G + u % 4, free, turned(1, pe))
                if u >= 1:
                    squares(u - 1)
            squares(9)

        def qk_act():
            for u in range(11):
                if u < 10:
                    cols_done(act, "qk", u)
                    if u >= 2:
                        act.wait_ge(named("qk_ss"), u - 1)
                    act.activation(SQ[:, u % 2, :], PS[:, G + u % 4, :], ACT.Square).then_inc(named("qk_sq"), 1)
                if u >= 1:
                    v = u - 1
                    act.wait_ge(named("qk_ss"), v + 1)
                    if v >= 2:
                        act.wait_ge(named("qk_done"), 2 * (v - 1))
                    act.activation(RS[:, v % 2, :], PS[:, A + v % 2, :], ACT.Ln,
                                   bias=eps64_c[:, 0:1]).then_inc(named("qk_rs"), 1)
                    act.wait_ge(named("qk_rs"), v + 1)
                    act.activation(RS[:, v % 2, :], RS[:, v % 2, :], ACT.Exp, scale=-0.5).then_inc(named("qk_rsx"), 1)

        def qk_dve():
            for u in range(10):
                cols_done(dve, "qk", u)
                dve.wait_ge(named("qk_rsx"), u + 1)
                for f in range(2):
                    j = QGAIN[2 * u + f]
                    dve.scalar_tensor_tensor(out=qkT[:, 2 * u + f, :], in0=PS[:, G + u % 4, f * T:(f + 1) * T],
                                             scalar=qk_fold[:, j:j + 1], in1=RS[:, u % 2, f * T:(f + 1) * T],
                                             op0=ALU.mult, op1=ALU.mult).then_inc(named("qk_done"), 1)

        def v_pe():
            rows_product("v", HT, DC, free=lambda: pe.wait_ge(named("qk_done"), 20))
            cols_unit("fg", 0, HT, (A, A + 2), lambda u: pe.wait_ge(named("qk_rs"), 10))

        def v_act():
            for b in range(4):
                rows_done(act, "v", b)
                act.activation(V1[:, b // 2, (b % 2) * 512:(b % 2 + 1) * 512], PS[:, G + b, :],
                               ACT.Copy).then_inc(named("v1_ready"), 1)
            split_through(act, "fg", 4)
            act.wait_ge(named("fg_z"), 1)
            act_then(act.activation(FG[0:6, 3, :], FG[0:6, 2, :], ACT.Exp))
            act.activation(FG[0:6, 4, :], FG[0:6, 3, :], ACT.Ln, bias=one_c[0:6, 0:1]).then_inc(named("fg_ln"), 1)

        def fg_dve():
            cols_done(dve, "fg", 0)
            dve_then(dve.tensor_scalar(FG[0:6, 0, :], PS[0:6, A, 0:T], gate_p[0:6, 0:1], None, ALU.add))
            dve_then(dve.tensor_scalar(FG[0:6, 1, :], FG[0:6, 0, :], 0.0, None, ALU.min))
            dve.scalar_tensor_tensor(out=FG[0:6, 2, :], in0=FG[0:6, 1, :], scalar=2.0, in1=FG[0:6, 0, :],
                                     op0=ALU.mult, op1=ALU.subtract).then_inc(named("fg_z"), 1)
            dve.memset(FL[:, :], 0.0)
            dve.memset(FR[:, :, :], 0.0)
            dve.wait_ge(named("fg_ln"), 1)
            dve_then(dve.tensor_tensor(FG[0:6, 5, :], FG[0:6, 1, :], FG[0:6, 4, :], ALU.subtract))
            dve_then(dve.tensor_tensor_scan(FG[0:6, 6, :], FG[0:6, 5, :], FG[0:6, 5, :], 0.0, ALU.add, ALU.bypass))
            split_through(dve, "fg", 4)
            for lo in (0, 64):
                dve.tensor_copy(FL[lo:lo + 6, :], FG[0:6, 6, :])
                dve.memset(FL[lo + 32:lo + 38, :], 1.0)
            for h in range(6):
                lo = 64 * (h % 2)
                dve.tensor_scalar(FR[lo:lo + 6, h, 0:P], sel[0:6, h, :], -1.0, None, ALU.mult)
                dve.tensor_scalar(FR[lo:lo + 6, h, P:T], sel[0:6, h, :], -1.0, None, ALU.mult)
                ins = dve.tensor_scalar(FR[lo + 32:lo + 38, h, :], FG[0:6, 6, :], sel[0:6, h, 0:1], None, ALU.mult)
            dve_then(ins)
            dve.sem_inc(named("fg_ready"), 1)

        HEADS = []
        for h in range(4):
            for j in range(2):
                HEADS.append((2 * j + h // 2, 4 + 2 * j + h // 2, h % 2, h, 64 * h, "diff", h, j))
        for h in range(6):
            HEADS.append((8 + h // 2, 11 + h // 2, h % 2, 4, 256 + 64 * h, "fox", h, 0))
        for h in range(6):
            HEADS.append((14 + h // 2, 17 + h // 2, h % 2, 5 + h, 640 + 64 * h, "chunk", h, 0))
        NA = 2 * len(HEADS)

        def wide(v):
            return min(v, D - P)

        def attn_pe():
            def scores(n):
                qt, kt, half, _b, _v, kind, h, _j = HEADS[n // 2]
                t, nk = n % 2, P * (n % 2 + 1)
                lo = 64 * half
                if n == 0:
                    pe.wait_ge(named("qk_done"), 20)
                    pe.wait_ge(named("fg_ready"), 1)
                if n >= 2:
                    pe.wait_ge(named("at_max"), n - 1)
                mm = pe.matmul(PS[:, A + n % 2, 0:nk], qkT[lo:lo + 64, qt, t * P:(t + 1) * P],
                               qkT[lo:lo + 64, kt, 0:nk], start=True, stop=(kind != "fox"))
                if kind == "fox":
                    mm = pe.matmul(PS[:, A + n % 2, 0:nk], FL[lo:lo + 38, t * P:(t + 1) * P],
                                   FR[lo:lo + 38, h, 0:nk],
                                   start=False, stop=True)
                mm.then_inc(named("at_s"), 1)

            def turn(n):
                t = n % 2
                pe.wait_ge(named("at_exp"), n + 1)
                if n >= 2:
                    pe.wait_ge(named("at_pt"), n - 1)
                for b in range(t + 1):
                    mm = pe.transpose(PS[:, A + 2 + t, b * P:(b + 1) * P],
                                      SN[:, n % 3, b * P:(b + 1) * P], ident[:, :])
                mm.then_inc(named("at_tp"), 1)

            def weigh(n):
                v = HEADS[n // 2][4]
                t = n % 2
                pe.wait_ge(named("at_pt"), n + 1)
                if n == 0:
                    pe.wait_ge(named("v1_ready"), 4)
                if n >= 2:
                    pe.wait_ge(named("at_o"), n - 1)
                for b in range(t + 1):
                    mm = pe.matmul(PS[:, G + n % 2, 0:P], PT[:, n % 3, b * P:(b + 1) * P],
                                   V1[:, b, wide(v):wide(v) + P], start=(b == 0), stop=(b == t))
                mm.then_inc(named("at_pv"), 1)

            for n in range(NA + 2):
                if n < NA:
                    scores(n)
                if 1 <= n <= NA:
                    turn(n - 1)
                if n >= 2:
                    weigh(n - 2)

        def attn_act():
            for n in range(NA + 1):
                if n < NA:
                    nk = P * (n % 2 + 1)
                    act.wait_ge(named("at_max"), n + 1)
                    act.activation(SN[:, n % 3, 0:nk], SN[:, n % 3, 0:nk], ACT.Exp, bias=MN[:, n:n + 1], scale=-1.0,
                                   accum_out=LS[:, n:n + 1]).then_inc(named("at_exp"), 1)
                if n >= 1:
                    m = n - 1
                    nk = P * (m % 2 + 1)
                    act.wait_ge(named("at_tp"), m + 1)
                    if m >= 3:
                        act.wait_ge(named("at_pv"), m - 2)
                    act.activation(PT[:, m % 3, 0:nk], PS[:, A + 2 + m % 2, 0:nk],
                                   ACT.Copy).then_inc(named("at_pt"), 1)

        def attn_dve():
            def low(n):
                bias = HEADS[n // 2][3]
                t, nk = n % 2, P * (n % 2 + 1)
                dve.wait_ge(named("at_s"), n + 1)
                if n == 8 * 2:
                    dve.wait_ge(named("causal"), 1)
                if n >= 3:
                    dve.wait_ge(named("at_tp"), n - 2)
                dve.tensor_tensor_reduce(out=SN[:, n % 3, 0:nk], in0=PS[:, A + n % 2, 0:nk],
                                         in1=BT[:, bias, T - nk:T], scale=1.0, scalar=3.0e38, op0=ALU.add,
                                         op1=ALU.min, accum_out=MN[:, n:n + 1]).then_inc(named("at_max"), 1)

            def finish(n):
                _q, _k, _half, _b, v, kind, h, j = HEADS[n // 2]
                t = n % 2
                dve.wait_ge(named("at_exp"), n + 1)
                dve_then(dve.reciprocal(RL[:, n:n + 1], LS[:, n:n + 1]))
                o = PS[:, G + n % 2, v - wide(v):v - wide(v) + 64]
                if kind == "diff" and j == 0:
                    dve.wait_ge(named("at_pv"), n + 1)
                    dve_then(dve.tensor_scalar(OD[:, t, :], o, RL[:, n:n + 1], None, ALU.mult))
                    dve.sem_inc(named("at_o"), 1)
                elif kind == "diff":
                    dve_then(dve.tensor_tensor(RL[:, n:n + 1], RL[:, n:n + 1], lam[:, 5:6], ALU.mult))
                    dve.wait_ge(named("at_pv"), n + 1)
                    dve.scalar_tensor_tensor(out=OM[:, t, v:v + 64], in0=o, scalar=RL[:, n:n + 1], in1=OD[:, t, :],
                                             op0=ALU.mult, op1=ALU.add).then_inc(named("at_o"), 1)
                else:
                    dve.wait_ge(named("at_pv"), n + 1)
                    dve.tensor_scalar(OM[:, t, v:v + 64], o, RL[:, n:n + 1], None, ALU.mult).then_inc(named("at_o"), 1)

            for n in range(NA + 2):
                if n < NA:
                    low(n)
                if n >= 2:
                    finish(n - 2)
            dve.wait_ge(named("at_o"), NA)
            for t in range(TT):
                o = OM[:, t, 0:256].rearrange("p (h d) -> p h d", h=4)
                dve_then(dve.tensor_tensor(DSQ[:, 4 * t:4 * t + 4, :], o, o, ALU.mult))
            dve.tensor_reduce(DST[:, 0, :], DSQ[:, :, :], AX.X, ALU.add).then_inc(named("sub_sum"), 1)
            dve.wait_ge(named("sub_rs"), 1)
            for t in range(TT):
                o = OM[:, t, 0:256].rearrange("p (h d) -> p h d", h=4)
                dve_then(dve.tensor_tensor(o, o, DST[:, 2, 4 * t:4 * t + 4].unsqueeze(2).to_broadcast([P, 4, 64]), ALU.mult))
                dve.tensor_tensor(o, o, row[:, ROW_SUBLN:ROW_SUBLN + 64].unsqueeze(1).to_broadcast([P, 4, 64]),
                                  ALU.mult).then_inc(named("mix_out"), 1)

        def subln_act():
            act.wait_ge(named("sub_sum"), 1)
            act_then(act.activation(DST[:, 1, :], DST[:, 0, :], ACT.Ln, bias=eps_c[:, 0:1], scale=1.0 / 64))
            act.activation(DST[:, 2, :], DST[:, 1, :], ACT.Exp, scale=-0.5).then_inc(named("sub_rs"), 1)

        GT = pair(16 * 256, FF_TILES)
        CS = view(60 * 256, (4, 2, T))
        SLU = view(68 * 256, (2, 2, T))
        GF = view(72 * 256, (2, 2, T))
        NUP = 2 * (D_FF // 256)

        def up_pe():
            def free(u):
                if u >= 4:
                    pe.wait_ge(named("up_conv"), u - 3)
                elif u == 0:
                    pe.wait_ge(s_x, 4)

            for u in range(NUP):
                cols_unit("up", u, HT, G + u % 4, free, turned(3, pe))

        def up_tile(u, f):
            return (u % 2) * FF_TILES + 2 * (u // 2) + f

        def up_act():
            def silu(j):
                act.wait_ge(named("up_conv"), 2 * j + 1)
                if j >= 2:
                    act.wait_ge(named("up_g"), j - 1)
                act.activation(SLU[:, j % 2, :, :], CS[:, (2 * j) % 4, :, :], ACT.Silu).then_inc(named("up_silu"), 1)

            def high(j):
                act.wait_ge(named("up_g"), j + 1)
                act.activation(GT[0][:, 2 * j:2 * j + 2, :], GF[:, j % 2, :, :], ACT.Copy).then_inc(named("up_gh"), 1)

            for u in range(NUP):
                cols_done(act, "up", u)
                if u >= 4:
                    act.wait_ge(named("up_g"), (u - 4) // 2 + 1)
                for f in range(2):
                    c = conv_cols[:, up_tile(u, f), :]
                    ins = act.activation(CS[:, u % 4, f, :], PS[:, G + u % 4, f * T:(f + 1) * T], ACT.Identity,
                                         bias=c[:, 3:4], scale=c[:, 2:3])
                ins.then_inc(named("up_tap"), 1)
                if u % 2:
                    silu(u // 2)
                elif u >= 2:
                    high(u // 2 - 1)
            high(NUP // 2 - 1)

        def up_dve():
            def low(j):
                dve.wait_ge(named("up_gh"), j + 1)
                dve.tensor_tensor(GT[1][:, 2 * j:2 * j + 2, :], GF[:, j % 2, :, :],
                                  GT[0][:, 2 * j:2 * j + 2, :].bitcast(F32), ALU.subtract).then_inc(named("up_gl"), 1)

            for u in range(NUP):
                cols_done(dve, "up", u)
                if u % 2 == 1 and u >= 3:
                    low((u - 3) // 2)
                dve.wait_ge(named("up_tap"), u + 1)
                for tap in (1, 0):
                    lag = 2 - tap
                    for f in range(2):
                        c = conv_cols[:, up_tile(u, f), :]
                        ins = dve.scalar_tensor_tensor(
                            out=CS[:, u % 4, f, lag:T], in0=PS[:, G + u % 4, f * T:(f + 1) * T - lag],
                            scalar=c[:, tap:tap + 1], in1=CS[:, u % 4, f, lag:T], op0=ALU.mult, op1=ALU.add)
                        if not (tap == 0 and f == 1):
                            if tap == 1 and f == 1:
                                dve_then(ins)
                ins.then_inc(named("up_conv"), 1)
            low(NUP // 2 - 1)

        def up_pool():
            for j in range(NUP // 2):
                pool.wait_ge(named("up_silu"), j + 1)
                pool.wait_ge(named("up_conv"), 2 * j + 2)
                if j >= 2:
                    pool.wait_ge(named("up_gl"), j - 1)
                pool.tensor_tensor(GF[:, j % 2, :, :], SLU[:, j % 2, :, :], CS[:, (2 * j + 1) % 4, :, :],
                                   ALU.mult).then_inc(named("up_g"), 1)

        def down_pe():
            rows_product("down", GT, FF_TILES, ready=lambda k: pe.wait_ge(named("up_gl"), k // 2 + 1),
                         free=lambda: pe.wait_ge(named("up_conv"), NUP))

        PTT = pair(16 * 256, 2)
        SG = view(20 * 256, (TT, D))
        PG = view(28 * 256, (2, 512))

        def ple_pe():
            rows_product("ple_gate", HT, DC, ready=turned(4, pe))
            pe.wait_ge(s_tl, 4 * 5)
            pe.wait_ge(s_small, 16 * N_SMALL)
            for c in range(2):
                for t in range(TT):
                    mm = pe.transpose(PS[:, A, c * T + t * P:c * T + (t + 1) * P], PIN[:, t, c * P:(c + 1) * P],
                                      ident[:, :])
            mm.then_inc(named("p_turned"), 1)

            rows_product("ple_proj", PTT, 2, base=A, free=lambda: pe.wait_ge(named("p_l"), 1))

        def ple_act():
            split_through(act, "ple_gate", 2)
            act.wait_ge(named("p_turned"), 1)
            act.activation(PTT[0], PS[:, A, :].rearrange("p (c n) -> p c n", c=2), ACT.Copy).then_inc(named("p_t"), 1)
            for b in range(4):
                rows_done(act, "ple_gate", b)
                act.activation(SG[:, b // 2, (b % 2) * 512:(b % 2 + 1) * 512], PS[:, G + b, :],
                               ACT.Sigmoid).then_inc(named("ple_sg"), 1)

        def ple_dve():
            split_through(dve, "ple_gate", 2)
            dve.wait_ge(named("p_t"), 1)
            dve.tensor_tensor(PTT[1], PS[:, A, :].rearrange("p (c n) -> p c n", c=2), PTT[0].bitcast(F32),
                              ALU.subtract).then_inc(named("p_l"), 1)
            for b in range(4):
                rows_done(dve, "ple_proj", b)
                dve.wait_ge(named("ple_sg"), b + 1)
                dve_then(dve.tensor_tensor(PG[:, b % 2, :], PS[:, A + b, :],
                                           SG[:, b // 2, (b % 2) * 512:(b % 2 + 1) * 512], ALU.mult))
                x = X[:, b // 2, (b % 2) * 512:(b % 2 + 1) * 512]
                dve.tensor_tensor(x, x, PG[:, b % 2, :], ALU.add).then_inc(s_x, 1)

        ABT = view(16 * 256, (12, T))
        VA = view(28 * 256, (TT, 4, 129))
        SGM = view(33 * 256, (TT, 512))
        SV = view(37 * 256, (TT, 512))
        OM2 = view(41 * 256, (TT, D))
        ROWSG = view(49 * 256, (12, T), 8)
        GA = view(61 * 256, (T,), 36)
        U3 = view(0, (2, 384))
        L3 = view(3 * 256, (2, 384))
        SP3 = view(6 * 256, (2, 384))
        W3 = view(9 * 256, (2, 384))
        HSQ = view(65 * 256, (TT, 4, P))
        HST = view(69 * 256, (4, 8))
        GC = view(62 * 256, (TT, 36))
        DN = view(63 * 256, (4, 2, 2))

        def ab_pe():
            def free(u):
                if u >= 4:
                    pe.wait_ge(named(("ab_ca", "ab_cd")[u % 2]), (u - 4) // 2 + 1)
            for u in range(6):
                cols_unit("ab_qk", u, HT, G + u % 4, free, turned(5, pe))
            cols_unit("ab_g", 0, HT, (A + 2, A + 3), lambda u: pe.wait_ge(s_tl, 4 * 6))

            def free2():
                pe.wait_ge(named("ab_ca"), 3)
                pe.wait_ge(named("ab_cd"), 3)
            rows_product("ab_vo", HT, DC, free=free2)
            rows_product("ab_sv", HT, DC, width=512, base=A)
            pe.wait_ge(named("ab_rows"), 1)
            for t in range(TT):
                mm = pe.transpose(PS[:, A + 2, 36 * t:36 * t + 36], GA[:, t * P:(t + 1) * P], ident[0:36, 0:36])
            mm.then_inc(named("ab_cols"), 1)

            def first(n):
                if n == 0:
                    pe.wait_ge(named("ab_va"), 2)
                    pe.wait_ge(named("ab_sgm"), 2)
                    pe.wait_ge(named("ab_svr"), 2)
                    pe.wait_ge(named("ab_gc"), 1)
                if n >= 2:
                    pe.wait_ge(named("ab_u"), n - 1)
                b = n % 2
                if n < 4:
                    m = ROWSG[0:4, 8, :]
                    pe.matmul(PS[:, b, 0:T], sel[0:4, n, :], m, start=True, stop=True)
                    mm = pe.matmul(PS[:, b, T:384], sel[0:4, n, :], ROWSG[0:4, 8, P:T], start=True, stop=True)
                else:
                    h = n - 4
                    pe.matmul(PS[:, b, 0:T], ABT[:, 4 + h, 0:P], ABT[:, h, :], start=True, stop=True)
                    mm = pe.matmul(PS[:, b, T:384], ABT[:, 4 + h, P:T], ABT[:, h, P:T], start=True, stop=True)
                mm.then_inc(named("ab_first"), 1)

            def second(n):
                b = 2 + n % 2
                if n >= 2:
                    pe.wait_ge(named("ab_sec_read"), n - 1)
                if n < 4:
                    lo = 64 * (n % 2)
                    q, k = ABT[lo:lo + 64, 8 + n // 2, :], ABT[lo:lo + 64, 10 + n // 2, :]
                    pe.matmul(PS[:, b, 0:T], k[:, 0:P], q, start=True, stop=True)
                    mm = pe.matmul(PS[:, b, T:384], k[:, P:T], q[:, P:T], start=True, stop=True)
                else:
                    pe.wait_ge(named("ab_sp"), n - 3)
                    sp3 = SP3[:, n % 2, :]
                    pe.matmul(PS[:, b, 0:384], tri[:, :], sp3, start=True, stop=False)
                    mm = pe.matmul(PS[:, b, P:T], ones[:, :], sp3[:, T:384], start=False, stop=True)
                mm.then_inc(named("ab_second"), 1)

            def weigh(n):
                b = 4 + n % 2
                pe.wait_ge(named("ab_w"), n + 1)
                if n >= 2:
                    pe.wait_ge(named("ab_o"), n - 1)
                w = W3[:, n % 2, :]
                nv = 129 if n < 4 else P
                v = [VA[:, t, n, :] if n < 4 else SV[:, t, (n - 4) * P:(n - 3) * P] for t in range(TT)]
                pe.matmul(PS[:, b, 0:nv], w[:, 0:P], v[0], start=True, stop=True)
                pe.matmul(PS[:, b, nv:2 * nv], w[:, P:T], v[0], start=True, stop=False)
                mm = pe.matmul(PS[:, b, nv:2 * nv], w[:, T:384], v[1], start=False, stop=True)
                mm.then_inc(named("ab_pv"), 1)

            for n in range(10):
                if n < 8:
                    first(n)
                if 1 <= n <= 8:
                    second(n - 1)
                if n >= 2:
                    weigh(n - 2)

        def ab_act():
            for u in range(0, 6, 2):
                cols_done(act, "ab_qk", u)
                act.activation(ABT[:, 2 * u:2 * u + 2, :], PS[:, G + u % 4, :].rearrange("p (c n) -> p c n", c=2),
                               ACT.Copy, scale=(P ** -0.5 if u < 2 else 1.0)).then_inc(named("ab_ca"), 1)
            split_through(act, "ab_g", 3)
            act.wait_ge(named("ab_zi"), 1)
            act.activation(ROWSG[0:4, 1, :], ROWSG[0:4, 0, :], ACT.Tanh, scale=1.0 / 15).then_inc(named("ab_li"), 1)
            for t in range(TT):
                rows_done(act, "ab_vo", 2 * t + 1)
                act.activation(SGM[:, t, :], PS[:, G + 2 * t + 1, :], ACT.Sigmoid).then_inc(named("ab_sgm"), 1)
            act.preload_act_table_set(EXP_LN)
            act.wait_ge(named("ab_zf"), 1)
            act_then(act.activation(ROWSG[0:4, 4, :], ROWSG[0:4, 3, :], ACT.Exp))
            act.activation(ROWSG[0:4, 5, :], ROWSG[0:4, 4, :], ACT.Ln, bias=one_c[0:4, 0:1]).then_inc(named("ab_lf"), 1)
            for t in range(TT):
                rows_done(act, "ab_sv", t)
                act.activation(SV[:, t, :], PS[:, A + t, :], ACT.Copy).then_inc(named("ab_svr"), 1)
            split_through(act, "ab_sv", 4)
            act.wait_ge(named("ab_m"), 1)
            act.activation(GA[32:36, :], ROWSG[0:4, 9, :], ACT.Exp, scale=-1.0).then_inc(named("ab_enm"), 1)
            for n in range(9):
                if n < 8:
                    act.wait_ge(named("ab_u"), n + 1)
                    if n < 4:
                        act.activation(L3[:, n % 2, :], U3[:, n % 2, :], ACT.Exp).then_inc(named("ab_l"), 1)
                    else:
                        if n >= 6:
                            act.wait_ge(named("ab_sp"), n - 5)
                        act_then(act.activation(L3[:, n % 2, :], U3[:, n % 2, :], ACT.Abs))
                        act_then(act.activation(L3[:, n % 2, :], L3[:, n % 2, :], ACT.Exp, scale=-1.0))
                        act.activation(L3[:, n % 2, :], L3[:, n % 2, :], ACT.Ln,
                                       bias=one_c[:, 0:1]).then_inc(named("ab_l"), 1)
                if n >= 5:
                    m = n - 1
                    act.wait_ge(named("ab_sec_read"), m + 1)
                    act.wait_ge(named("ab_pv"), m - 1)
                    act.activation(W3[:, m % 2, :], U3[:, m % 2, :], ACT.Exp).then_inc(named("ab_w"), 1)
            act.wait_ge(named("ab_ssq"), 1)
            act_then(act.activation(HST[:, 1, :], HST[:, 0, :], ACT.Ln, bias=eps_c[:, 0:1], scale=1.0 / P))
            act.activation(HST[:, 2, :], HST[:, 1, :], ACT.Exp, scale=-0.5).then_inc(named("ab_hrs"), 1)

        def ab_dve():
            for u in range(1, 6, 2):
                cols_done(dve, "ab_qk", u)
                dve.tensor_scalar(ABT[:, 2 * u:2 * u + 2, :], PS[:, G + u % 4, :].rearrange("p (c n) -> p c n", c=2),
                                  {1: P ** -0.5, 3: 1.0, 5: 64 ** -0.5}[u], None, ALU.mult).then_inc(named("ab_cd"), 1)
            R = lambda j: ROWSG[0:4, j, :]
            cols_done(dve, "ab_g", 0)
            dve.tensor_scalar(R(0), PS[0:4, A + 2, 0:T], gate_p[0:4, 1:2], None, ALU.add).then_inc(named("ab_zi"), 1)
            dve_then(dve.tensor_scalar(R(6), PS[0:4, A + 3, 0:T], gate_p[0:4, 2:3], None, ALU.add))
            dve_then(dve.tensor_scalar(R(2), R(6), 0.0, None, ALU.min))
            dve.scalar_tensor_tensor(out=R(3), in0=R(2), scalar=2.0, in1=R(6), op0=ALU.mult,
                                     op1=ALU.subtract).then_inc(named("ab_zf"), 1)
            dve.memset(GA[:, :], 0.0)
            dve.memset(VA[:, :, :, 128:129], 1.0)
            for t in range(TT):
                rows_done(dve, "ab_vo", 2 * t)
                dve.tensor_copy(VA[:, t, :, 0:P], PS[:, G + 2 * t, :].rearrange("p (h d) -> p h d", h=4)
                                ).then_inc(named("ab_va"), 1)
            split_through(dve, "ab_vo", 4)
            dve.wait_ge(named("ab_lf"), 1)
            dve.wait_ge(named("ab_li"), 1)
            dve_then(dve.tensor_tensor(R(6), R(2), R(5), ALU.subtract))
            dve_then(dve.tensor_tensor_scan(R(7), R(6), R(6), 0.0, ALU.add, ALU.bypass))
            dve_then(dve.scalar_tensor_tensor(out=R(10), in0=R(1), scalar=15.0, in1=R(7), op0=ALU.mult,
                                              op1=ALU.subtract))
            dve_then(dve.tensor_tensor_scan(R(11), R(10), R(10), 0.0, ALU.max, ALU.max))
            dve_then(dve.tensor_scalar(R(8), R(11), -1.0, None, ALU.mult))
            dve.tensor_copy(GA[0:4, :], R(10))
            dve_then(dve.tensor_tensor(R(9), R(7), R(11), ALU.add))
            dve.sem_inc(named("ab_m"), 1)
            split_through(dve, "ab_sv", 4)
            dve.wait_ge(named("ab_enm"), 1)
            dve.sem_inc(named("ab_rows"), 1)
            dve.wait_ge(named("ab_cols"), 1)
            dve_then(dve.tensor_copy(GC[:, :, :], PS[:, A + 2, 0:72].rearrange("p (t n) -> p t n", t=2)))
            dve.sem_inc(named("ab_gc"), 1)

            def after_first(n):
                dve.wait_ge(named("ab_first"), n + 1)
                u, z = U3[:, n % 2, :], PS[:, n % 2, 0:384]
                if 2 <= n < 6:
                    dve.wait_ge(named("ab_l"), n - 1)
                if n >= 6:
                    dve.wait_ge(named("ab_w"), n - 1)
                if n < 4:
                    dve.scalar_tensor_tensor(out=u[:, 0:T], in0=z[:, 0:T], scalar=GC[:, 0, n:n + 1],
                                             in1=neg_ge[:, 0:2, :], op0=ALU.add, op1=ALU.add)
                    dve.scalar_tensor_tensor(out=u[:, T:384], in0=z[:, T:384], scalar=GC[:, 1, n:n + 1],
                                             in1=neg_ge[:, 2, :], op0=ALU.add, op1=ALU.add).then_inc(named("ab_u"), 1)
                else:
                    dve.tensor_tensor(u, z, neg_gt[:, :, :].rearrange("p a b -> p (a b)"),
                                      ALU.add).then_inc(named("ab_u"), 1)

            def after_l(n):
                if n < 4:
                    dve.wait_ge(named("ab_l"), n + 1)
                    dve.wait_ge(named("ab_second"), n + 1)
                    if n >= 2:
                        dve.wait_ge(named("ab_pv"), n - 1)
                    dve_then(dve.tensor_tensor(W3[:, n % 2, :], PS[:, 2 + n % 2, 0:384], L3[:, n % 2, :], ALU.mult))
                    dve.sem_inc(named("ab_w"), 1)
                    dve.sem_inc(named("ab_sec_read"), 1)
                else:
                    dve.wait_ge(named("ab_l"), n + 1)
                    if n >= 6:
                        dve.wait_ge(named("ab_second"), n - 1)
                    dve_then(dve.scalar_tensor_tensor(out=SP3[:, n % 2, :], in0=U3[:, n % 2, :], scalar=0.0,
                                                      in1=L3[:, n % 2, :], op0=ALU.max, op1=ALU.add))
                    dve.sem_inc(named("ab_sp"), 1)
                    dve.wait_ge(named("ab_second"), n + 1)
                    dve.scalar_tensor_tensor(out=U3[:, n % 2, :], in0=PS[:, 2 + n % 2, 0:384], scalar=-1.0,
                                             in1=U3[:, n % 2, :], op0=ALU.mult,
                                             op1=ALU.add).then_inc(named("ab_sec_read"), 1)

            def finish(n):
                dve.wait_ge(named("ab_pv"), n + 1)
                b = 4 + n % 2
                if n < 4:
                    o = PS[:, b, 0:258].rearrange("p (t n) -> p t n", t=2)
                    dn = DN[:, n, :, :]
                    dve_then(dve.scalar_tensor_tensor(out=dn[:, 0, :], in0=o[:, :, 128], scalar=-1.0,
                                                      in1=GC[:, :, 32 + n], op0=ALU.mult, op1=ALU.max))
                    dve_then(dve.tensor_tensor(dn[:, 0, :], o[:, :, 128], dn[:, 0, :], ALU.max))
                    dve_then(dve.reciprocal(dn[:, 1, :], dn[:, 0, :]))
                    for t in range(TT):
                        ins = dve.tensor_scalar(OM2[:, t, n * P:(n + 1) * P], o[:, t, 0:P], dn[:, 1, t:t + 1], None,
                                                ALU.mult)
                    ins.then_inc(named("ab_o"), 1)
                else:
                    dve.tensor_copy(OM2[:, :, n * P:(n + 1) * P],
                                    PS[:, b, 0:T].rearrange("p (t n) -> p t n", t=2)).then_inc(named("ab_o"), 1)

            for n in range(10):
                if n < 8:
                    after_first(n)
                if 1 <= n <= 8:
                    after_l(n - 1)
                if n >= 2:
                    finish(n - 2)
            dve.wait_ge(named("ab_o"), 8)
            head_norm_dve(OM2[:, :, 0:512], HSQ, HST, 4, "ab_ssq", "ab_hrs",
                          row[:, ROW_ABHEAD:ROW_ABHEAD + 512].rearrange("p (h d) -> p h d", h=4), SGM, "ab_om")

        def head_norm_dve(o_all, sq, st, heads, told, asked, gain, gate, done):
            for t in range(TT):
                o = o_all[:, t, :].rearrange("p (h d) -> p h d", h=heads)
                q = sq[:, t, :, :] if len(sq.shape) == 4 else sq
                dve_then(dve.tensor_tensor(q, o, o, ALU.mult))
                dve_then(dve.tensor_reduce(st[:, 0, heads * t:heads * (t + 1)], q, AX.X, ALU.add))
            dve.sem_inc(named(told), 1)
            dve.wait_ge(named(asked), 1)
            for t in range(TT):
                o = o_all[:, t, :].rearrange("p (h d) -> p h d", h=heads)
                r = st[:, 2, heads * t:heads * (t + 1)].unsqueeze(2).to_broadcast([P, heads, P])
                dve_then(dve.tensor_tensor(o, o, r, ALU.mult))
                dve_then(dve.tensor_tensor(o, o, gain, ALU.mult))
                dve.tensor_tensor(o, o, gate[:, t, :].rearrange("p (h d) -> p h d", h=heads),
                                  ALU.mult).then_inc(named(done), 1)

        XQ = view(16 * 256, (8, T))
        XK = view(24 * 256, (8, T))
        XV = view(32 * 256, (TT, D))
        XP = view(40 * 256, (3, T))
        XPT = view(43 * 256, (2, 2, T))
        XMN = view(47 * 256, (3, 8))
        XO = pair(48 * 256, 8)
        NX = 8

        def xa_kv_pe(l):
            s0 = NX * l

            def free(u):
                if u == 0:
                    pe.wait_ge(s_x, 4 * (4 + 3 * l))
            for u in range(4):
                cols_unit(f"xk{l}", u, MEMT, G + u, free)
            rows_product(f"xv{l}", MEMT, DC, free=lambda: (pe.wait_ge(named("xk_a"), 2 * l + 2),
                                                           pe.wait_ge(named("xk_d"), 2 * l + 2)))

        def xa_kv_evac(l, eng):
            k = 0 if eng is act else 1
            for u in (k, k + 2):
                cols_done(eng, f"xk{l}", u)
                src = PS[:, G + u, :].rearrange("p (c n) -> p c n", c=2)
                if k:
                    dve.tensor_copy(XK[:, 2 * u:2 * u + 2, :], src).then_inc(named("xk_d"), 1)
                else:
                    act.activation(XK[:, 2 * u:2 * u + 2, :], src, ACT.Copy).then_inc(named("xk_a"), 1)
            for b in (k, k + 2):
                rows_done(eng, f"xv{l}", b)
                dst = XV[:, b // 2, (b % 2) * 512:(b % 2 + 1) * 512]
                if k:
                    dve.tensor_copy(dst, PS[:, G + b, :]).then_inc(named("xv_d"), 1)
                else:
                    act.activation(dst, PS[:, G + b, :], ACT.Copy).then_inc(named("xv_a"), 1)

        def xa_pe(l, turn):
            c0 = NX * l

            def free(u):
                if u == 0:
                    pe.wait_ge(named("xv_a"), 2 * l + 2)
                    pe.wait_ge(named("xv_d"), 2 * l + 2)
            for u in range(4):
                cols_unit(f"xq{l}", u, HT, G + u, free, turned(turn, pe))

            def scores(n):
                h, t = n // 2, n % 2
                if n == 0:
                    pe.wait_ge(s_tl, 4 * (turn + 1))
                pe.wait_ge(named(("xq_a", "xq_d")[h % 2]), 2 * l + h // 2 + 1)
                if n >= 2:
                    pe.wait_ge(named("xa_exp"), c0 + n - 1)
                for c in range(2):
                    mm = pe.matmul(PS[:, A + n % 2, 0:T], XQ[:, 2 * h + c, t * P:(t + 1) * P], XK[:, 2 * h + c, :],
                                   start=(c == 0), stop=(c == 1))
                mm.then_inc(named("xa_s"), 1)

            def turn_p(n):
                pe.wait_ge(named("xa_norm"), c0 + n + 1)
                if n >= 2:
                    pe.wait_ge(named("xa_pt"), c0 + n - 1)
                for b in range(2):
                    mm = pe.transpose(PS[:, A + 2 + n % 2, b * P:(b + 1) * P], XP[:, n % 3, b * P:(b + 1) * P],
                                      ident[:, :])
                mm.then_inc(named("xa_tp"), 1)

            def weigh(h):
                pe.wait_ge(named("xa_pt"), c0 + 2 * h + 2)
                if h >= 2:
                    pe.wait_ge(named("xa_o"), 4 * l + h - 1)
                elif h == 0:
                    pe.wait_ge(named("xq_a"), 2 * l + 2)
                    pe.wait_ge(named("xq_d"), 2 * l + 2)
                for c in range(2):
                    for m in range(2):
                        mm = pe.matmul(PS[:, G + h % 2, c * T:(c + 1) * T],
                                       XV[:, m, h * T + c * P:h * T + (c + 1) * P], XPT[:, h % 2, m, :],
                                       start=(m == 0), stop=(m == 1))
                mm.then_inc(named("xa_pv"), 1)

            for n in range(NX + 2):
                if n < NX:
                    scores(n)
                if 1 <= n <= NX:
                    turn_p(n - 1)
                if n >= 2 and n % 2:
                    weigh((n - 2) // 2)
            rows_product(f"xo{l}", XO, DC, ready=lambda k: pe.wait_ge(named("xa_o"), 4 * l + k // 2 + 1),
                         free=lambda: pe.wait_ge(named("xa_o"), 4 * l + 4))

        def xa_act(l):
            c0 = NX * l
            for u in (0, 2):
                cols_done(act, f"xq{l}", u)
                act.activation(XQ[:, 2 * u:2 * u + 2, :], PS[:, G + u, :].rearrange("p (c n) -> p c n", c=2),
                               ACT.Copy, scale=-1.0 / 16).then_inc(named("xq_a"), 1)
            split_through(act, f"xq{l}", 4)
            for n in range(NX + 3):
                if n < NX:
                    act.wait_ge(named("xa_min"), c0 + n + 1)
                    if n >= 3:
                        act.wait_ge(named("xa_tp"), c0 + n - 2)
                    act.activation(XP[:, n % 3, :], PS[:, A + n % 2, 0:T], ACT.Exp, bias=XMN[:, 0, n:n + 1],
                                   scale=-1.0, accum_out=XMN[:, 1, n:n + 1]).then_inc(named("xa_exp"), 1)
                if n >= 3 and n % 2:
                    h = (n - 3) // 2
                    act.wait_ge(named("xa_pv"), 4 * l + h + 1)
                    act.activation(XO[0][:, 2 * h:2 * h + 2, :], PS[:, G + h % 2, :].rearrange("p (c n) -> p c n", c=2),
                                   ACT.Copy).then_inc(named("xa_oh"), 1)
                if 1 <= n <= NX:
                    m = n - 1
                    h, t = m // 2, m % 2
                    act.wait_ge(named("xa_tp"), c0 + m + 1)
                    if h >= 2:
                        act.wait_ge(named("xa_pv"), 4 * l + h - 1)
                    act.activation(XPT[:, h % 2, :, t * P:(t + 1) * P],
                                   PS[:, A + 2 + m % 2, 0:T].rearrange("p (m n) -> p m n", m=2),
                                   ACT.Copy).then_inc(named("xa_pt"), 1)

        def xa_dve(l):
            c0 = NX * l
            for u in (1, 3):
                cols_done(dve, f"xq{l}", u)
                dve.tensor_scalar(XQ[:, 2 * u:2 * u + 2, :], PS[:, G + u, :].rearrange("p (c n) -> p c n", c=2),
                                  -1.0 / 16, None, ALU.mult).then_inc(named("xq_d"), 1)
            split_through(dve, f"xq{l}", 4)
            for n in range(NX + 3):
                if n < NX:
                    dve.wait_ge(named("xa_s"), c0 + n + 1)
                    dve.tensor_reduce(XMN[:, 0, n:n + 1], PS[:, A + n % 2, 0:T], AX.X,
                                      ALU.min).then_inc(named("xa_min"), 1)
                if 1 <= n <= NX:
                    m = n - 1
                    dve.wait_ge(named("xa_exp"), c0 + m + 1)
                    dve_then(dve.reciprocal(XMN[:, 2, m:m + 1], XMN[:, 1, m:m + 1]))
                    dve.tensor_scalar(XP[:, m % 3, :], XP[:, m % 3, :], XMN[:, 2, m:m + 1], None,
                                      ALU.mult).then_inc(named("xa_norm"), 1)
                if n >= 3 and n % 2:
                    h = (n - 3) // 2
                    if h < 4:
                        xo_out(l, h)

        def xo_out(l, h):
            dve.wait_ge(named("xa_oh"), 4 * l + h + 1)
            dve.tensor_tensor(XO[1][:, 2 * h:2 * h + 2, :], PS[:, G + h % 2, :].rearrange("p (c n) -> p c n", c=2),
                              XO[0][:, 2 * h:2 * h + 2, :].bitcast(F32), ALU.subtract).then_inc(named("xa_o"), 1)

        HID = pair(16 * 256, FF2_TILES)
        RLU = HN[:, 0, :].rearrange("p (a c n) -> p a c n", a=2, c=2)
        RSQ = HN[:, 1, :].rearrange("p (a c n) -> p a c n", a=2, c=2)
        NM1 = D_FF_2 // 256

        def mlp_pe(l, turn):
            def free(u):
                if u == 0:
                    pe.wait_ge(s_x, 4 * (5 + 3 * l))
                if u >= 4:
                    pe.wait_ge(named("m1_relu"), NM1 * l + u - 3)
            for u in range(NM1):
                cols_unit(f"m1{l}", u, HT, G + u % 4, free, turned(turn, pe))
            rows_product(f"m2{l}", HID, FF2_TILES, ready=lambda k: pe.wait_ge(named("m1_sq"), NM1 * l + k // 2 + 1),
                         free=lambda: pe.wait_ge(named("m1_relu"), NM1 * (l + 1)))

        def mlp_act(l):
            for u in range(NM1):
                cols_done(act, f"m1{l}", u)
                if u >= 2:
                    act.wait_ge(named("m1_f"), NM1 * l + u - 1)
                    act.wait_ge(named("m1_h"), NM1 * l + u - 1)
                act_then(act.activation(RLU[:, u % 2, :, :], PS[:, G + u % 4, :].rearrange("p (c n) -> p c n", c=2),
                                        ACT.Relu))
                act.sem_inc(named("m1_relu"), 1)
                act.activation(HID[0][:, 2 * u:2 * u + 2, :], RLU[:, u % 2, :, :], ACT.Square).then_inc(named("m1_h"), 1)

        def mlp_pool(l):
            for u in range(NM1):
                pool.wait_ge(named("m1_relu"), NM1 * l + u + 1)
                if u >= 2:
                    pool.wait_ge(named("m1_sq"), NM1 * l + u - 1)
                pool.tensor_tensor(RSQ[:, u % 2, :, :], RLU[:, u % 2, :, :], RLU[:, u % 2, :, :],
                                   ALU.mult).then_inc(named("m1_f"), 1)

        def mlp_dve(l):
            for u in range(NM1):
                cols_done(dve, f"m1{l}", u)
                dve.wait_ge(named("m1_h"), NM1 * l + u + 1)
                dve.wait_ge(named("m1_f"), NM1 * l + u + 1)
                dve.tensor_tensor(HID[1][:, 2 * u:2 * u + 2, :], RSQ[:, u % 2, :, :],
                                  HID[0][:, 2 * u:2 * u + 2, :].bitcast(F32), ALU.subtract
                                  ).then_inc(named("m1_sq"), 1)

        NCU = 12
        QKV = view(16 * 256, (24, T))
        CC = view(48 * 256, (4, 2, T))
        SGC = view(40 * 256, (TT, D))
        SQL = view(56 * 256, (2, 512))
        RSL = view(60 * 256, (2, 512))
        DEC = view(0, (2, 4, P))
        ATC = view(56 * 256, (4, 4, P))
        ATT = view(64 * 256, (4, 4, P))
        RV = view(48 * 256, (4, 4, P))
        RK = view(72 * 256, (2, 4, P))
        KD = view(76 * 256, (2, 4, P))
        QD = view(80 * 256, (2, 4, P))
        GAB = view(5 * 256, (T,), 40)
        CR = view(8 * 256, (8, T), 8)
        LT = view(0, (4, 4, P))
        XI = view(8 * 256, (4, 4, P))
        XT = view(16 * 256, (4, 4, P))
        YI = view(24 * 256, (4, 4, P))
        VN0 = view(24 * 256, (2, 4, P))
        S1 = view(28 * 256, (2, 4, P))
        NW = view(8 * 256, (2, 4, P))
        VN1 = view(12 * 256, (2, 4, P))
        OC = view(32 * 256, (TT, D))
        OSQ = view(56 * 256, (8, P))
        TE = HN[:, 0, :].rearrange("p (a h n) -> p a h n", a=2, h=4)
        TQ = HN[:, 1, 0:512].rearrange("p (h n) -> p h n", h=4)
        LM = sb("level_masks", [P, 7, P])
        GCB = sb("gate_cols", [P, TT, 40])
        GX = sb("gate_col_exps", [P, 4, 8])
        CST = sb("c_stats", [P, 3, 16])
        DG = sb("g_last_diag", [8, 8])
        NEA = sb("a_exp", [8, 1])
        eps128_c = sb("eps128_c", [P, 1])
        LEVELS = 7

        def c_consts_pool():
            pool.memset(eps128_c[:, :], P * EPS)
            pool_then(pool.memset(LM[:, :, :], 0.0))
            for i in range(LEVELS):
                b = 1 << i
                m = LM[:, i, :].rearrange("p (n h b) -> p n h b", h=2, b=b)[:, :, 1, :]
                n = P // (2 * b)
                pool_then(pool.memset(m, 1.0))
                pool_then(pool.affine_select(out=m, in_=m, compare_op=ALU.is_ge, fill=0.0, base=0,
                                             pattern=[[-2 * b, n], [0, b]], channel_multiplier=1))
                pool_then(pool.affine_select(out=m, in_=m, compare_op=ALU.is_ge, fill=0.0, base=b - 1,
                                             pattern=[[2 * b, n], [0, b]], channel_multiplier=-1))
            pool.sem_inc(named("c_consts"), 1)

        def c_pe():
            def free(u):
                if u == 0:
                    pe.wait_ge(s_x, 4 * 6)
                if u >= 4:
                    pe.wait_ge(named("c_conv"), u - 3)
            for u in range(NCU):
                cols_unit("c_qkv", u, HT, G + u % 4, free, turned(9, pe))
            rows_product("c_gate", HT, DC, free=lambda: pe.wait_ge(named("c_conv"), NCU))
            cols_unit("c_g", 0, HT, (A, A + 1), lambda u: pe.wait_ge(s_tl, 4 * 10))
            for i in range(8):
                pe.wait_ge(named("l2_sq"), i + 1)
                if i >= 2:
                    pe.wait_ge(named("l2_ln"), i - 1)
                pe.matmul(PS[:, A + 2 + i % 2, :], ones[:, :], SQL[:, i % 2, :], start=True,
                          stop=True).then_inc(named("l2_ss"), 1)
            pe.wait_ge(named("c_rows"), 1)
            for t in range(TT):
                pe.transpose(PS[:, A, 40 * t:40 * t + 40], GAB[:, t * P:(t + 1) * P], ident[0:40, 0:40])
            pe.matmul(PS[:, A, 128:136], ones[0:8, :], DG[:, :], start=True, stop=True).then_inc(named("c_cols"), 1)
            for gi in range(4):
                hg, c = gi // 2, gi % 2
                pe.wait_ge(named("c_sg"), gi + 1)
                if gi == 0:
                    pe.wait_ge(named("c_silu"), NCU)
                for j in range(4):
                    mm = pe.transpose(PS[:, gi, j * P:(j + 1) * P], QKV[:, 16 + 4 * hg + j, c * P:(c + 1) * P],
                                      ident[:, :])
                mm.then_inc(named("c_vt"), 1)
            for gi in range(4):
                hg, c = gi // 2, gi % 2
                if gi == 0:
                    pe.wait_ge(named("l2_done"), 8)
                    pe.wait_ge(named("c_gcb"), 1)
                for j in range(4):
                    mm = pe.transpose(PS[:, 4 + gi, j * P:(j + 1) * P], QKV[:, 8 + 4 * hg + j, c * P:(c + 1) * P],
                                      ident[:, :])
                mm.then_inc(named("c_kt"), 1)
            for gi in range(4):
                hg, c = gi // 2, gi % 2
                pb = 4 * (gi % 2)
                tok = slice(c * P, (c + 1) * P)
                if gi < 2:
                    pe.wait_ge(named("c_rv" if gi == 0 else "c_rk"), 4)
                else:
                    pe.wait_ge(named("c_prep"), gi - 1)
                for i, r in ((0, 7), (1, 2)):
                    for j in range(4):
                        mm = pe.matmul(PS[:, pb + i, j * P:(j + 1) * P], sel[:, 4 * hg + j, :], CR[:, r, tok],
                                       start=True, stop=True)
                    mm.then_inc(named("c_p"), 1)
                for i, q0 in ((2, 8), (3, 0)):
                    for j in range(4):
                        mm = pe.matmul(PS[:, pb + i, j * P:(j + 1) * P], QKV[:, 8 + 4 * hg + j, tok],
                                       QKV[:, q0 + 4 * hg + j, tok], start=True, stop=True)
                    mm.then_inc(named("c_p"), 1)
            for gi in range(4):
                pe.wait_ge(named("c_lt"), gi + 1)
                if gi == 0:
                    pe.wait_ge(named("c_prep"), 4)
                if gi >= 2:
                    pe.wait_ge(named("c_x"), gi - 1)
                for j in range(4):
                    mm = pe.transpose(PS[:, 6 + gi % 2, j * P:(j + 1) * P], LT[:, gi, j, :], ident[:, :])
                mm.then_inc(named("c_l0"), 1)

            NL = 4 * (LEVELS - 1)

            def y(n):
                gi = n % 4
                pe.wait_ge(named("c_x"), n + 1)
                pe.wait_ge(named("c_lt"), n + 5)
                if n >= 2:
                    pe.wait_ge(named("c_y"), n - 1)
                for j in range(4):
                    mm = pe.matmul(PS[:, gi % 2, j * P:(j + 1) * P], LT[:, gi, j, :], XI[:, gi, j, :], start=True,
                                   stop=True)
                mm.then_inc(named("c_ym"), 1)

            def pq(n):
                gi = n % 4
                pe.wait_ge(named("c_y"), n + 1)
                if n >= 2:
                    pe.wait_ge(named("c_x"), n + 3)
                if n < NL - 4:
                    for j in range(4):
                        pe.matmul(PS[:, 2 + gi % 2, j * P:(j + 1) * P], XT[:, gi, j, :], YI[:, gi, j, :], start=True,
                                  stop=True)
                for j in range(4):
                    mm = pe.matmul(PS[:, 4 + gi % 2, j * P:(j + 1) * P], YI[:, gi, j, :], XT[:, gi, j, :], start=True,
                                   stop=True)
                mm.then_inc(named("c_pq"), 1)

            for n in range(NL + 1):
                if n < NL:
                    y(n)
                if n >= 1:
                    pq(n - 1)

            def quad(bank, terms, told):
                for j in range(4):
                    for i, (l, r) in enumerate(terms):
                        mm = pe.matmul(PS[:, bank, j * P:(j + 1) * P], l[:, j, :], r[:, j, :], start=(i == 0),
                                       stop=(i == len(terms) - 1))
                mm.then_inc(named(told), 1)

            for hg in range(2):
                g0, g1 = 2 * hg, 2 * hg + 1
                pe.wait_ge(named("c_x"), 4 * LEVELS if hg else 4 * LEVELS - 2)
                if hg == 0:
                    pe.wait_ge(named("c_y"), NL)
                quad(hg, [(XT[:, g0], RV[:, g0])], "c_u0")
                quad(6 + hg, [(RK[:, hg], XT[:, g1])], "c_wt")
            for hg in range(2):
                pe.wait_ge(named("c_vn0"), hg + 1)
                quad(2 + hg, [(KD[:, hg], VN0[:, hg])], "c_s1m")
                quad(hg, [(ATT[:, 2 * hg], VN0[:, hg])], "c_o0")
            for hg in range(2):
                g1 = 2 * hg + 1
                pe.wait_ge(named("c_nw"), hg + 1)
                pe.wait_ge(named("c_s1"), hg + 1)
                quad(4 + hg, [(XT[:, g1], RV[:, g1]), (NW[:, hg], S1[:, hg])], "c_u1")
            for hg in range(2):
                pe.wait_ge(named("c_vn1"), hg + 1)
                quad(2 + hg, [(QD[:, hg], S1[:, hg]), (ATT[:, 2 * hg + 1], VN1[:, hg])], "c_o1")

        def c_act():
            def silu(u):
                act.wait_ge(named("c_conv"), u + 1)
                act.activation(QKV[:, 2 * u:2 * u + 2, :], CC[:, u % 4, :, :], ACT.Silu).then_inc(named("c_silu"), 1)

            for u in range(NCU):
                cols_done(act, "c_qkv", u)
                for f in range(2):
                    ins = act.activation(CC[:, u % 4, f, :], PS[:, G + u % 4, f * T:(f + 1) * T], ACT.Copy,
                                         scale=cconv_cols[:, 2 * u + f, 3:4])
                ins.then_inc(named("c_tap"), 1)
                if u:
                    silu(u - 1)
            silu(NCU - 1)
            for b in range(4):
                rows_done(act, "c_gate", b)
                act.activation(SGC[:, b // 2, (b % 2) * 512:(b % 2 + 1) * 512], PS[:, G + b, :],
                               ACT.Silu).then_inc(named("c_sg"), 1)
            split_through(act, "c_g", 4)
            act.preload_act_table_set(EXP_LN)
            R = lambda j: CR[:, j, :]
            act.wait_ge(named("c_za"), 1)
            act_then(act.activation(R(6), R(5), ACT.Exp))
            act.activation(R(6), R(6), ACT.Ln, bias=one_c[0:8, 0:1]).then_inc(named("c_la"), 1)
            act.activation(R(0), PS[0:8, A, 0:T], ACT.Exp, scale=-1.0).then_inc(named("c_eb"), 1)
            act.activation(NEA[:, :], gate_p[:, 3:4], ACT.Exp).then_inc(named("c_nea"), 1)
            for i in range(8):
                act.wait_ge(named("l2_ss"), i + 1)
                if i >= 2:
                    act.wait_ge(named("l2_done"), i - 1)
                q = i < 4
                act.activation(RSL[:, i % 2, :], PS[:, A + 2 + i % 2, :], ACT.Ln,
                               bias=(eps128_c if q else eps_c)[:, 0:1],
                               scale=(float(P) if q else 1.0)).then_inc(named("l2_ln"), 1)
                act.wait_ge(named("l2_ln"), i + 1)
                act.activation(RSL[:, i % 2, :], RSL[:, i % 2, :], ACT.Exp, scale=-0.5).then_inc(named("l2_rs"), 1)
            act.wait_ge(named("c_gcb"), 1)
            act.activation(GX[:, 0, :], GCB[:, 1, 0:8], ACT.Exp).then_inc(named("c_gx"), 1)
            act.activation(GX[:, 3, :], GX[:, 2, :], ACT.Exp).then_inc(named("c_gx"), 1)
            for gi in range(4):
                act.wait_ge(named("c_e"), gi + 1)
                if gi >= 2:
                    act.wait_ge(named("c_prep"), gi - 1)
                act.activation(DEC[:, gi % 2, :, :], TE[:, gi % 2, :, :], ACT.Exp).then_inc(named("c_dec"), 1)
                if gi % 2:
                    if gi == 3:
                        act.wait_ge(named("c_qd"), 1)
                    act.activation(TQ, PS[:, 4 * (gi % 2), :].rearrange("p (h n) -> p h n", h=4),
                                   ACT.Exp).then_inc(named("c_tq"), 1)
            for n in range(4 * (LEVELS - 1)):
                act.wait_ge(named("c_ym"), n + 1)
                act.activation(YI[:, n % 4, :, :], PS[:, (n % 4) % 2, :].rearrange("p (h n) -> p h n", h=4),
                               ACT.Copy).then_inc(named("c_y"), 1)
            for hg in range(2):
                act.wait_ge(named("c_wt"), hg + 1)
                act.activation(NW[:, hg, :, :], PS[:, 6 + hg, :].rearrange("p (h n) -> p h n", h=4), ACT.Copy,
                               scale=-1.0).then_inc(named("c_nw"), 1)
            for hg in range(2):
                act.wait_ge(named("c_s1m"), hg + 1)
                act.activation(S1[:, hg, :, :], PS[:, 2 + hg, :].rearrange("p (h n) -> p h n", h=4),
                               ACT.Copy).then_inc(named("c_s1"), 1)
            for hg in range(2):
                act.wait_ge(named("c_o0"), hg + 1)
                act.activation(OC[:, 0, 512 * hg:512 * (hg + 1)], PS[:, hg, :], ACT.Copy).then_inc(named("c_oc0"), 1)
            act.wait_ge(named("c_ssq"), 1)
            act_then(act.activation(CST[:, 1, :], CST[:, 0, :], ACT.Ln, bias=eps_c[:, 0:1], scale=1.0 / P))
            act.activation(CST[:, 2, :], CST[:, 1, :], ACT.Exp, scale=-0.5).then_inc(named("c_hrs"), 1)

        def c_pool():
            pool.wait_ge(named("c_silu"), 8)
            for i in range(8):
                if i >= 2:
                    pool.wait_ge(named("l2_ss"), i - 1)
                pool.tensor_tensor(SQL[:, i % 2, :].rearrange("p (c n) -> p c n", c=2), QKV[:, 2 * i:2 * i + 2, :],
                                   QKV[:, 2 * i:2 * i + 2, :], ALU.mult).then_inc(named("l2_sq"), 1)
            for hg in range(2):
                pool.wait_ge(named("c_tq"), hg + 1)
                pool.tensor_tensor(QD[:, hg, :, :], QKV[:, 4 * hg:4 * hg + 4, P:T], TQ, ALU.mult).then_inc(named("c_qd"), 1)
            for n in range(4 * LEVELS):
                lvl, gi = n // 4, n % 4
                if n == 0:
                    pool.wait_ge(named("c_prep"), 4)
                if lvl == 1:
                    pool.wait_ge(named("c_x"), gi + 1)
                elif lvl > 1:
                    pool.wait_ge(named("c_ym"), n - 7)
                pool.tensor_tensor(LT[:, gi, :, :], ATC[:, gi, :, :],
                                   LM[:, lvl, :].unsqueeze(1).to_broadcast([P, 4, P]), ALU.mult
                                   ).then_inc(named("c_lt"), 1)

        def c_dve():
            for u in range(NCU):
                cols_done(dve, "c_qkv", u)
                dve.wait_ge(named("c_tap"), u + 1)
                for tap in (2, 1, 0):
                    lag = 3 - tap
                    for f in range(2):
                        ins = dve.scalar_tensor_tensor(
                            out=CC[:, u % 4, f, lag:T], in0=PS[:, G + u % 4, f * T:(f + 1) * T - lag],
                            scalar=cconv_cols[:, 2 * u + f, tap:tap + 1], in1=CC[:, u % 4, f, lag:T], op0=ALU.mult,
                            op1=ALU.add)
                    if tap:
                        dve_then(ins)
                ins.then_inc(named("c_conv"), 1)
            R = lambda j: CR[:, j, :]
            cols_done(dve, "c_g", 0)
            split_through(dve, "c_g", 4)
            dve_then(dve.tensor_scalar(R(3), PS[0:8, A + 1, 0:T], gate_p[:, 4:5], None, ALU.add))
            dve_then(dve.tensor_scalar(R(4), R(3), 0.0, None, ALU.min))
            dve.scalar_tensor_tensor(out=R(5), in0=R(4), scalar=2.0, in1=R(3), op0=ALU.mult,
                                     op1=ALU.subtract).then_inc(named("c_za"), 1)
            dve.memset(GAB[:, :], 0.0)
            dve.wait_ge(named("c_eb"), 1)
            dve_then(dve.tensor_scalar(R(1), R(0), 1.0, None, ALU.add))
            dve_then(dve.reciprocal(R(2), R(1)))
            dve.wait_ge(named("c_la"), 1)
            dve.wait_ge(named("c_nea"), 1)
            dve_then(dve.tensor_tensor(R(3), R(3), R(6), ALU.add))
            dve_then(dve.tensor_tensor(R(3), R(3), R(4), ALU.subtract))
            dve_then(dve.tensor_scalar(R(5), R(3), NEA[:, 0:1], -1.0, ALU.mult, ALU.mult))
            for c in range(2):
                s_ = CR[:, 5, c * P:(c + 1) * P]
                ins = dve.tensor_tensor_scan(CR[:, 7, c * P:(c + 1) * P], s_, s_, 0.0, ALU.add, ALU.bypass)
            dve_then(ins)
            dve.tensor_scalar(DG[:, :], ident[0:8, 0:8], CR[:, 7, P - 1:P], None, ALU.mult)
            dve.tensor_copy(GAB[0:8, :], R(7))
            dve_then(dve.tensor_copy(GAB[32:40, :], R(2)))
            dve.sem_inc(named("c_rows"), 1)
            for i in range(8):
                dve.wait_ge(named("l2_rs"), i + 1)
                o = QKV[:, 2 * i:2 * i + 2, :]
                dve.tensor_tensor(o, o, RSL[:, i % 2, :].rearrange("p (c n) -> p c n", c=2),
                                  ALU.mult).then_inc(named("l2_done"), 1)
            dve.wait_ge(named("c_cols"), 1)
            dve_then(dve.tensor_copy(GCB[:, :, :], PS[:, A, 0:80].rearrange("p (t n) -> p t n", t=2)))
            dve_then(dve.tensor_tensor(GX[:, 2, :], PS[:, A, 128:136], GCB[:, 0, 0:8], ALU.subtract))
            dve.sem_inc(named("c_gcb"), 1)

            def bc(col):
                return col.unsqueeze(2).to_broadcast([P, 4, P])

            def quad(bank):
                return PS[:, bank, :].rearrange("p (h n) -> p h n", h=4)

            for gi in range(4):
                hg, c = gi // 2, gi % 2
                dve.wait_ge(named("c_vt"), gi + 1)
                dve.tensor_tensor(RV[:, gi, :, :], quad(gi), bc(GCB[:, c, 32 + 4 * hg:36 + 4 * hg]),
                                  ALU.mult).then_inc(named("c_rv"), 1)
            dve.wait_ge(named("c_gx"), 2)
            dve_then(dve.tensor_tensor(GX[:, 1, :], GX[:, 0, :], GCB[:, 1, 32:40], ALU.mult))
            for gi in range(4):
                hg, c = gi // 2, gi % 2
                dve.wait_ge(named("c_kt"), gi + 1)
                dst, col = (RK, 1) if c else (KD, 3)
                dve.tensor_tensor(dst[:, hg, :, :], quad(4 + gi), bc(GX[:, col, 4 * hg:4 * hg + 4]),
                                  ALU.mult).then_inc(named("c_rk"), 1)
            for gi in range(4):
                hg, c = gi // 2, gi % 2
                pb = 4 * (gi % 2)
                dve.wait_ge(named("c_p"), 4 * gi + 1)
                if gi >= 2:
                    dve.wait_ge(named("c_dec"), gi - 1)
                for j in range(4):
                    ins = dve.scalar_tensor_tensor(out=TE[:, gi % 2, j, :], in0=PS[:, pb, j * P:(j + 1) * P],
                                                   scalar=GCB[:, c, 4 * hg + j:4 * hg + j + 1], in1=neg_ge[:, 0, :],
                                                   op0=ALU.subtract, op1=ALU.add)
                ins.then_inc(named("c_e"), 1)
                dve.wait_ge(named("c_dec"), gi + 1)
                dve.wait_ge(named("c_p"), 4 * gi + 4)
                dec = DEC[:, gi % 2, :, :]
                dve_then(dve.tensor_tensor(ATC[:, gi, :, :], quad(pb + 2), dec, ALU.mult))
                dve.tensor_tensor(ATT[:, gi, :, :], quad(pb + 3), dec, ALU.mult)
                if c:
                    dve.wait_ge(named("c_tq"), hg + 1)
                dve_then(dve.tensor_tensor(ATC[:, gi, :, :], quad(pb + 1), ATC[:, gi, :, :], ALU.mult))
                dve.sem_inc(named("c_prep"), 1)
            idb = ident[:, :].unsqueeze(1).to_broadcast([P, 4, P])
            for gi in range(4):
                dve.wait_ge(named("c_l0"), gi + 1)
                dve.tensor_tensor(XT[:, gi, :, :], idb, LT[:, gi, :, :], ALU.subtract)
                dve_then(dve.scalar_tensor_tensor(out=XI[:, gi, :, :], in0=quad(6 + gi % 2), scalar=-1.0, in1=idb,
                                                  op0=ALU.mult, op1=ALU.add))
                dve.sem_inc(named("c_x"), 1)
            NL = 4 * (LEVELS - 1)
            for n in range(NL):
                gi = n % 4
                dve.wait_ge(named("c_pq"), n + 1)
                if n < NL - 4:
                    dve.tensor_tensor(XI[:, gi, :, :], XI[:, gi, :, :], quad(2 + gi % 2), ALU.subtract)
                dve_then(dve.tensor_tensor(XT[:, gi, :, :], XT[:, gi, :, :], quad(4 + gi % 2), ALU.subtract))
                dve.sem_inc(named("c_x"), 1)
            for hg in range(2):
                dve.wait_ge(named("c_u0"), hg + 1)
                dve.tensor_copy(VN0[:, hg, :, :], quad(hg)).then_inc(named("c_vn0"), 1)
            for hg in range(2):
                dve.wait_ge(named("c_u1"), hg + 1)
                dve.tensor_copy(VN1[:, hg, :, :], quad(4 + hg)).then_inc(named("c_vn1"), 1)
            for hg in range(2):
                dve.wait_ge(named("c_o1"), hg + 1)
                dve_then(dve.tensor_copy(OC[:, 1, 512 * hg:512 * (hg + 1)], PS[:, 2 + hg, :]))
            dve.wait_ge(named("c_oc0"), 2)
            head_norm_dve(OC, OSQ, CST, 8, "c_ssq", "c_hrs",
                          row[:, ROW_CHEAD:ROW_CHEAD + P].unsqueeze(1).to_broadcast([P, 8, P]), SGC, "c_om")

        def final_act():
            resid(9)(act)
            act.activation(HN[:, 1, :], X[:, 1, :], ACT.Square, accum_out=stat[:, 1:2]).then_inc(s_stat, 1)
            act.wait_ge(s_stat, 2 * 11)
            act_then(act.activation(lnv[:, :], stat[:, :], ACT.Ln, bias=eps_c[:, 0:1], scale=1.0 / D))
            act.activation(rstd[:, :], lnv[:, :], ACT.Exp, scale=-0.5).then_inc(s_rstd, 1)

        def final_dve():
            resid(9)(dve)
            dve.tensor_tensor_reduce(out=HN[:, 0, :], in0=X[:, 0, :], in1=X[:, 0, :], scale=1.0, scalar=0.0,
                                     op0=ALU.mult, op1=ALU.add, accum_out=stat[:, 0:1]).then_inc(s_stat, 1)
            dve.wait_ge(s_stat, 2 * 11)
            dve.wait_ge(s_rstd, 11)
            for t in range(TT):
                dve.scalar_tensor_tensor(out=HN[:, t, :], in0=X[:, t, :], scalar=rstd[:, t:t + 1],
                                         in1=row[:, ROW_FINAL:ROW_FINAL + D], op0=ALU.mult,
                                         op1=ALU.mult).then_inc(named("final"), 1)

        def final_sp(sp):
            for t in range(TT):
                sp.wait_ge(named("final"), t + 1)
                sp.dma_start(out[t * P:(t + 1) * P, :], HN[:, t, :]).then_inc(s_out, 16)
            sp.wait_ge(s_out, 16 * TT)

        block = ctx.enter_context(nc.Block())

        @block.sync
        def _(sp):
            small_sp(sp)
            weights_sp(sp)
            if stop:
                sp.wait_ge(s_x, 4 * (upto + 1))
                sp.dma_start(out.rearrange("(t p) d -> p t d", p=P), X[:, :, :]).then_inc(s_out, 16)
                sp.wait_ge(s_out, 16)
            else:
                final_sp(sp)

        @block.gpsimd
        def _(p_):
            consts_pool()
            c_consts_pool()
            if upto >= 1:
                up_pool()
            for l in range(2):
                if l and upto >= 6:
                    c_pool()
                if upto >= 5 + 3 * l:
                    mlp_pool(l)

        @block.tensor
        def _(p_):
            pe.wait_ge(s_const, 1)
            turn_pe(0, HN, norm_ready_pe(0))
            turn_pe(1, HN, norm_ready_pe(1), free=lambda: pe.wait_ge(s_tl, 4))
            qk_pe()
            v_pe()
            attn_pe()
            turn_pe(2, OM, lambda t: pe.wait_ge(named("mix_out"), t + 1))
            rows_product("w_out", HT, DC, ready=turned(2, pe), free=lambda: pe.wait_ge(named("v1_ready"), 4))
            if upto >= 1:
                turn_pe(3, HN, norm_ready_pe(2))
                up_pe()
                down_pe()
            if upto >= 2:
                turn_pe(4, HN, norm_ready_pe(3))
                ple_pe()
            if upto >= 3:
                turn_pe(5, HN, norm_ready_pe(4))
                ab_pe()
                turn_pe(6, OM2, lambda t: (pe.wait_ge(named("ab_om"), t + 1), pe.wait_ge(named("ab_o"), 8)))
                rows_product("ab_out", HT, DC, ready=turned(6, pe))
            for l in range(2):
                if l and upto >= 6:
                    turn_pe(9, HN, norm_ready_pe(7))
                    c_pe()
                    turn_pe(10, OC, lambda t: pe.wait_ge(named("c_om"), t + 1))
                    rows_product("c_out", HT, DC, ready=turned(10, pe))
                if upto >= 4 + 3 * l:
                    xa_kv_pe(l)
                    turn_pe(7 + 4 * l, HN, norm_ready_pe(5 + 3 * l))
                    xa_pe(l, 7 + 4 * l)
                if upto >= 5 + 3 * l:
                    turn_pe(8 + 4 * l, HN, norm_ready_pe(6 + 3 * l))
                    mlp_pe(l, 8 + 4 * l)

        @block.scalar
        def _(p_):
            act.preload_act_table_set(EXP_LN)
            act.wait_ge(s_const, 1)
            norm_act(0, MEM, lambda e: e.wait_ge(s_mem, 16))
            act.wait_ge(s_small, 16 * N_SMALL)
            turn_act(0, MEMT, LN_MEM)
            norm_act(1, X, lambda e: (e.wait_ge(s_x_in, 16), e.wait_ge(s_tp, 4)))
            turn_act(1, HT, LN_MIX)
            lam_act()
            qk_act()
            v_act()
            attn_act()
            subln_act()
            turn_act(2, HT)
            if upto >= 1:
                norm_act(2, X, resid(1))
                turn_act(3, HT, LN_FFN)
                up_act()
                act.preload_act_table_set(EXP_LN)
            if upto >= 2:
                norm_act(3, X, resid(2))
                turn_act(4, HT, LN_PLE)
                ple_act()
                act.preload_act_table_set(EXP_LN)
            if upto >= 3:
                norm_act(4, X, resid(3))
                turn_act(5, HT, LN_MIX0)
                ab_act()
                turn_act(6, HT)
            for l in range(2):
                if l and upto >= 6:
                    norm_act(7, X, resid(6))
                    turn_act(9, HT, LN_MIX1)
                    c_act()
                    turn_act(10, HT)
                if upto >= 4 + 3 * l:
                    xa_kv_evac(l, act)
                    norm_act(5 + 3 * l, X, resid(4 + 3 * l))
                    turn_act(7 + 4 * l, HT, LN_XA0 + 3 * l)
                    xa_act(l)
                if upto >= 5 + 3 * l:
                    norm_act(6 + 3 * l, X, resid(5 + 3 * l))
                    turn_act(8 + 4 * l, HT, LN_MLP0 + 3 * l)
                    mlp_act(l)
            if not stop:
                final_act()
            else:
                split(act, 2 * stop_unit)

        @block.vector
        def _(p_):
            dve.wait_ge(s_const, 1)
            norm_dve(0, MEM, lambda e: e.wait_ge(s_mem, 16))
            dve.wait_ge(s_small, 16 * N_SMALL)
            turn_dve(0, MEMT, LN_MEM)
            norm_dve(1, X, lambda e: (e.wait_ge(s_x_in, 16), e.wait_ge(s_tp, 4)))
            turn_dve(1, HT, LN_MIX)
            biases_dve()
            qk_dve()
            fg_dve()
            attn_dve()
            turn_dve(2, HT)
            resid_add_dve("w_out")
            if upto >= 1:
                norm_dve(2, X, resid(1))
                turn_dve(3, HT, LN_FFN)
                up_dve()
                resid_add_dve("down")
            if upto >= 2:
                norm_dve(3, X, resid(2))
                turn_dve(4, HT, LN_PLE)
                ple_dve()
            if upto >= 3:
                norm_dve(4, X, resid(3))
                turn_dve(5, HT, LN_MIX0)
                ab_dve()
                turn_dve(6, HT)
                resid_add_dve("ab_out")
            for l in range(2):
                if l and upto >= 6:
                    norm_dve(7, X, resid(6))
                    turn_dve(9, HT, LN_MIX1)
                    c_dve()
                    turn_dve(10, HT)
                    resid_add_dve("c_out")
                if upto >= 4 + 3 * l:
                    xa_kv_evac(l, dve)
                    norm_dve(5 + 3 * l, X, resid(4 + 3 * l))
                    turn_dve(7 + 4 * l, HT, LN_XA0 + 3 * l)
                    xa_dve(l)
                    resid_add_dve(f"xo{l}")
                if upto >= 5 + 3 * l:
                    norm_dve(6 + 3 * l, X, resid(5 + 3 * l))
                    turn_dve(8 + 4 * l, HT, LN_MLP0 + 3 * l)
                    mlp_dve(l)
                    resid_add_dve(f"m2{l}")
            if not stop:
                final_dve()


def laid_out(v):
    import numpy as np

    f = {k: np.asarray(a) for k, a in v.items()}
    wi, ab, cw = f["w_in"][0], f["ab_w_in_2"][0], f["c_w_in_2"][0]
    a = {"x": f["x"][0], "mem": f["mem_2"][0], "p": f["p"][0, 0]}
    a["w_in"] = np.concatenate([wi[:, 0:1024], wi[:, 1280:2048], wi[:, 2438:3206], wi[:, 1024:1280],
                                wi[:, 2048:2432], wi[:, 3206:3590]], axis=1)
    a["w_out"], a["w_up"], a["w_down"] = f["w_out"][0], f["w_up"][0], f["w_down"][0]
    a["w_ple_gate"], a["w_ple_proj"] = f["w_ple_gate"][0], f["w_ple_proj"][0]
    a["ab_w_in"] = np.concatenate([ab[:, 1544:2568], ab[:, 0:512], ab[:, 512:1536], ab[:, 2568:3080]], axis=1)
    a["ab_w_out"], a["c_w_out"] = f["ab_w_out_2"][0], f["c_w_out_2"][0]
    a["c_w_in"] = cw[:, 0:4096]
    for l in range(2):
        for n in ("xa_wq", "xa_wk", "xa_wv", "xa_wo", "mlp_w1", "mlp_w2"):
            a[f"{n}{l}"] = f[f"{n}_2"][l]
    g = np.zeros((1024, 768), np.float32)
    for at, cols in ((0, wi[:, 2432:2438]), (256, ab[:, 1536:1540]), (384, ab[:, 1540:1544]),
                     (512, cw[:, 4096:4104]), (640, cw[:, 4104:4112])):
        g[:, at:at + cols.shape[1]] = cols
    a["gates"] = g
    lns = np.stack([f["ln_mix"][0], f["ln_ffn"][0], f["ln_ple"][0], f["mem_norm_2"], f["mix_norm_2"][0],
                    f["xa_norm_2"][0], f["mlp_norm_2"][0], f["mix_norm_2"][1], f["xa_norm_2"][1], f["mlp_norm_2"][1]])
    a["ln_cols"] = lns.reshape(10, 8, 128).transpose(2, 0, 1).reshape(128, 80)
    a["qk_cols"] = np.concatenate([f["qk_gain"][0].T, f["qk_gain"][0].T], axis=0)
    a["row"] = np.concatenate([f["subln_gain"][0], f["ab_head_gain_2"][0].reshape(-1), f["c_head_gain_2"][0],
                               f["lam_params"][0].reshape(-1), f["final_norm_2"]])[None, :]
    cc = np.concatenate([f["conv_w"][0], f["conv_b"]], axis=0)
    a["conv_cols"] = cc.reshape(4, 44, 128).transpose(2, 1, 0).reshape(128, 176)
    a["cconv_cols"] = f["c_conv_w_2"][0].reshape(4, 24, 128).transpose(2, 1, 0).reshape(128, 96)
    gp = np.zeros((8, 5), np.float32)
    gp[0:6, 0], gp[0:4, 1], gp[0:4, 2] = f["fgate_bias"][0], f["ab_b_i_2"][0], f["ab_b_f_2"][0]
    gp[:, 3], gp[:, 4] = f["c_a_log_2"][0], f["c_dt_bias_2"][0]
    a["gate_p"] = gp
    a["rel_rev"] = f["rel_bias"][0][:, ::-1]
    return {k: np.ascontiguousarray(x) for k, x in a.items()}


STOP = None


def kernel(**inputs):
    import numpy as _np
    import concourse.bacc as _bacc
    from concourse import mybir as _mybir
    from concourse.bass_utils import run_bass_kernel_spmd as _run

    nc = _bacc.Bacc("TRN2", target_bir_lowering=False, num_devices=1)
    arrays = laid_out(inputs)
    I = {n: nc.dram_tensor(f"in_{n}", a.shape, _mybir.dt.from_np(a.dtype), kind="ExternalInput").ap()
         for n, a in arrays.items()}
    out = nc.dram_tensor("out_0", (T, D), _mybir.dt.float32, kind="ExternalOutput").ap()
    scratch = nc.dram_tensor("rel_rows", (6, P, 511), _mybir.dt.float32).ap()
    build_two_blocks(nc, I, out, scratch, STOP)
    r = _run(nc, [{f"in_{n}": a for n, a in arrays.items()}], core_ids=[0])
    return _np.asarray(r.results[0]["out_0"]).reshape(1, T, D)
```

```python
from contextlib import ExitStack

import concourse.bass as bass
from concourse import mybir

P = 128
T = 256
TT = T // P
D = 1024
DC = D // P
EPS = 1e-6
BIG = 1e30
RING = 4
UNIT = 2048
PART = UNIT // 2
PARTS = 4

F32 = mybir.dt.float32
F32R = mybir.dt.float32r
ALU = mybir.AluOpType
ACT = mybir.ActivationFunctionType
AX = mybir.AxisListType

LN_MIX, LN_FFN, LN_PLE, LN_MEM, LN_MIX0, LN_XA0, LN_MLP0, LN_MIX1, LN_XA1, LN_MLP1 = range(10)
EXP_LN = "natural_log_exp_and_others"
ROW_SUBLN, ROW_ABHEAD, ROW_CHEAD, ROW_LAM, ROW_FINAL, ROW_LEN = 0, 64, 576, 704, 960, 1984

D_FF = 2816
FF_TILES = D_FF // P
D_FF_2 = 4096
FF2_TILES = D_FF_2 // P
LAM_INIT = 0.2


def weight_plan():
    plan = []

    def cols(stage, w, starts):
        plan.extend((stage, w, "cols", c) for c in starts)

    def rows(stage, w, chunks, c0=0, width=D):
        per = UNIT // width
        for k in range(0, chunks, per):
            plan.append((stage, w, "rows", (k, min(per, chunks - k), c0, width)))

    cols("qk", "w_in", range(0, 2560, 256))
    cols("fg", "gates", [0])
    rows("v", "w_in", DC, 2560)
    rows("w_out", "w_out", DC)
    for j in range(D_FF // 256):
        cols("up", "w_up", (256 * j, D_FF + 256 * j))
    rows("down", "w_down", FF_TILES)
    rows("ple_proj", "w_ple_proj", 2)
    rows("ple_gate", "w_ple_gate", DC)
    cols("xk0", "xa_wk0", range(0, D, 256))
    cols("ab_qk", "ab_w_in", range(0, 1536, 256))
    cols("ab_g", "gates", [256])
    rows("ab_vo", "ab_w_in", DC, 1536)
    rows("ab_sv", "ab_w_in", DC, 2560, 512)
    rows("ab_out", "ab_w_out", DC)
    for l in range(2):
        if l:
            cols("c_qkv", "c_w_in", range(0, 3072, 256))
            cols("c_g", "gates", [512])
            rows("c_gate", "c_w_in", DC, 3072)
            rows("c_out", "c_w_out", DC)
        if l:
            cols("xk1", "xa_wk1", range(0, D, 256))
        rows(f"xv{l}", f"xa_wv{l}", DC)
        cols(f"xq{l}", f"xa_wq{l}", range(0, D, 256))
        rows(f"xo{l}", f"xa_wo{l}", DC)
        cols(f"m1{l}", f"mlp_w1{l}", range(0, D_FF_2, 256))
        rows(f"m2{l}", f"mlp_w2{l}", FF2_TILES)
    return plan


def build_two_blocks(nc, I, out, scratch):
    plan = weight_plan()
    first_unit = {}
    for n, (stage, *_r) in enumerate(plan):
        first_unit.setdefault(stage, n)

    with ExitStack() as ctx:
        def sb(name, shape, dtype=F32):
            return ctx.enter_context(nc.sbuf_tensor(name, shape, dtype))

        def sem(name):
            return ctx.enter_context(nc.semaphore(name))

        X = sb("resid", [P, TT, D])
        HN = sb("normed", [P, TT, D])
        MEMT = [sb(f"mem_t_{x}", [P, DC, T], F32R) for x in ("hi", "lo")]
        raw = sb("weights", [P, RING, UNIT])
        WH = sb("weights_hi", [P, PARTS, PART], F32R)
        WL = sb("weights_lo", [P, PARTS, PART], F32R)
        ARENA = 84 * 256
        with nc.sbuf_tensor("split_arena", [P, ARENA], F32R) as split_arena:
            pass
        arena = sb("arena", [P, ARENA])
        ident = sb("ident", [P, P])
        ones = sb("ones", [P, P])
        halves = sb("halves", [P, P])
        tri = sb("tri", [P, P])
        sel = sb("sel", [8, 8, P])
        neg_ge = sb("neg_ge", [P, 3, P])
        neg_gt = sb("neg_gt", [P, 3, P])
        ln_cols = sb("ln_cols", [P, 10, DC])
        qk_cols = sb("qk_cols", [P, 6])
        qk_fold = sb("qk_fold", [P, 6])
        row = sb("row", [P, ROW_LEN])
        conv_cols = sb("conv_cols", [P, 2 * FF_TILES, 4])
        cconv_cols = sb("cconv_cols", [P, 24, 4])
        gate_p = sb("gate_p", [8, 5])
        stat = sb("stat", [P, 4])
        mean0 = sb("mean0", [P, 2])
        lnv = sb("lnv", [P, 2])
        rstd = sb("rstd", [P, 2])
        eps_c = sb("eps_c", [P, 1])
        eps64_c = sb("eps64_c", [P, 1])
        one_c = sb("one_c", [P, 1])
        lam = sb("lam", [P, 8])
        PS = ctx.enter_context(nc.psum_tensor("ps", [P, 8, 512], F32))
        G, A = 0, 4

        def view(first, shape, parts=P, of=None):
            n = 1
            for s in shape:
                n *= s
            v = (arena if of is None else of)[0:parts, first:first + n]
            if len(shape) == 1:
                return v
            names = "abcd"[:len(shape)]
            spec = {c: s for c, s in zip(names, shape)}
            return v.rearrange(f"p ({' '.join(names)}) -> p {' '.join(names)}", **spec)

        def pair(first, chunks):
            return [view(first + i * chunks * T, (chunks, T), of=split_arena) for i in range(2)]

        HT = pair(0, DC)

        s_x_in = [sem(f"x_loaded_{t}") for t in range(TT)]
        s_early = sem("early_loaded")
        s_small = sem("small_loaded")
        s_const = sem("constants_built")
        s_pool_chain = sem("pool_chain")
        s_act_chain = sem("act_chain")
        s_dve_chain = sem("dve_chain")
        s_unit = [sem(f"unit_landed_{i}") for i in range(RING)]
        s_hi = sem("weights_hi_ready")
        s_lo = sem("weights_lo_ready")
        s_used = sem("part_used")
        s_x = sem("resid_ready")
        s_stat = sem("norm_squares")
        s_rstd = sem("norm_rstd")
        s_mean0 = sem("first_half_mean")
        s_hn_act = sem("normed_first_half")
        s_hn_dve = sem("normed_second_half")
        s_tp = sem("transposed")
        s_th = sem("turned_hi")
        s_tl = sem("turned_lo")
        s_acc = sem("rows_product_done")
        s_out = sem("out_stored")

        S = {}

        def named(name):
            if name not in S:
                S[name] = sem(name)
            return S[name]

        chain_n = {"act": 0, "dve": 0, "pool": 0}

        def act_then(ins):
            chain_n["act"] += 1
            ins.then_inc(s_act_chain, 1)
            nc.scalar.wait_ge(s_act_chain, chain_n["act"])

        def dve_then(ins):
            chain_n["dve"] += 1
            ins.then_inc(s_dve_chain, 1)
            nc.vector.wait_ge(s_dve_chain, chain_n["dve"])

        def pool_then(ins):
            chain_n["pool"] += 1
            ins.then_inc(s_pool_chain, 1)
            nc.gpsimd.wait_ge(s_pool_chain, chain_n["pool"])

        dve, act, pool, pe = nc.vector, nc.scalar, nc.gpsimd, nc.tensor

        def weights_sp(sp, start, end):
            for n, (stage, w, kind, at) in enumerate(plan[start:end], start):
                slot = n % RING
                if n >= RING:
                    sp.wait_ge(s_lo, 2 * (n - RING) + 2)
                W = I[w]
                if kind == "cols":
                    dst = raw[:, slot, :].rearrange("p (c n) -> p c n", c=DC)
                    src = W[:, at:at + 256].rearrange("(c p) n -> p c n", p=P)
                else:
                    k, per, c0, width = at
                    dst = raw[:, slot, 0:per * width].rearrange("p (c n) -> p c n", c=per)
                    src = W[k * P:(k + per) * P, c0:c0 + width].rearrange("(c p) n -> p c n", p=P)
                sp.dma_start(dst, src).then_inc(s_unit[slot], 16)

        def part_views(p):
            r, h, l = raw[:, (p // 2) % RING, :], WH[:, p % PARTS, :], WL[:, p % PARTS, :]
            if plan[p // 2][2] == "cols":
                r = r.rearrange("p (c n) -> p c n", c=DC)[:, :, (p % 2) * P:(p % 2 + 1) * P]
                return r, h.rearrange("p (c n) -> p c n", c=DC), l.rearrange("p (c n) -> p c n", c=DC)
            return r[:, (p % 2) * PART:(p % 2 + 1) * PART], h, l

        split_n = {"act": 0, "dve": 0}

        def split(eng, upto):
            who = "act" if eng is act else "dve"
            for p in range(split_n[who], min(upto + 1, 2 * len(plan))):
                r, h, l = part_views(p)
                n = p // 2
                if eng is act:
                    act.wait_ge(s_unit[n % RING], 16 * (n // RING + 1))
                    if p >= PARTS:
                        act.wait_ge(s_used, p - PARTS + 1)
                    act.activation(h, r, ACT.Copy).then_inc(s_hi, 1)
                else:
                    dve.wait_ge(s_hi, p + 1)
                    dve.tensor_tensor(l, r, h.bitcast(F32), ALU.subtract).then_inc(s_lo, 1)
                split_n[who] = p + 1

        def last_part(stage):
            return 2 * max(n for n, x in enumerate(plan) if x[0] == stage) + 1

        def split_through(eng, stage, more):
            split(eng, last_part(stage) + more)

        def cols_unit(stage, u, rhs, banks, free=None, ready=None):
            n = first_unit[stage] + u
            if free:
                free(u)
            for f in range(2):
                p = 2 * n + f
                pe.wait_ge(s_lo, p + 1)
                _r, wh, wl = part_views(p)
                o = PS[:, banks, f * T:(f + 1) * T] if isinstance(banks, int) else PS[:, banks[f], 0:T]
                for k in range(DC):
                    if ready and u == 0 and f == 0:
                        ready(k)
                    for i, (w, x) in enumerate(((wh, rhs[0]), (wh, rhs[1]), (wl, rhs[0]))):
                        mm = pe.matmul(o, w[:, k, :], x[:, k, :], start=(k == 0 and i == 0),
                                       stop=(k == DC - 1 and i == 2))
                mm.then_inc(s_used, 1)

        def cols_done(eng, stage, u, more=3):
            last = 2 * (first_unit[stage] + u) + 1
            if eng is act or eng is dve:
                split(eng, last + more)
            eng.wait_ge(s_used, last + 1)

        ROWS = {}
        acc = 0
        for stage, width in (("v", D), ("w_out", D), ("down", D), ("ple_proj", D), ("ple_gate", D), ("ab_vo", D),
                             ("ab_sv", 512), ("ab_out", D), ("xv0", D), ("xo0", D), ("m20", D), ("c_gate", D),
                             ("c_out", D), ("xv1", D), ("xo1", D), ("m21", D)):
            banks = TT * width // 512
            ROWS[stage] = (banks, acc)
            acc += banks - 1

        def rows_done(eng, stage, b, more=2):
            banks, before = ROWS[stage]
            split_through(eng, stage, more)
            if b < banks - 1:
                eng.wait_ge(s_acc, before + b + 1)
            else:
                eng.wait_ge(s_used, last_part(stage) + 1)

        def rows_product(stage, lhs, chunks, width=D, base=G, ready=None, free=None, free_tile=None):
            per = PART // width
            nb = width // 512
            p = 2 * first_unit[stage]
            for k0 in range(0, chunks - 2 * per, per):
                pe.wait_ge(s_lo, p + 1)
                _r, wh, wl = part_views(p)
                for k in range(k0, k0 + per):
                    if ready:
                        ready(k)
                    if k == 0 and free:
                        free()
                    for t in range(TT):
                        if k == 0 and free_tile:
                            free_tile(t)
                        for i, (x, w) in enumerate(((lhs[0], wh), (lhs[0], wl), (lhs[1], wh))):
                            for b in range(nb):
                                c = (k - k0) * width + b * 512
                                mm = pe.matmul(PS[:, base + nb * t + b, :], x[:, k, t * P:(t + 1) * P],
                                               w[:, c:c + 512], start=(k == 0 and i == 0), stop=False)
                mm.then_inc(s_used, 1)
                p += 1
            pe.wait_ge(s_lo, p + 2)
            last = range(chunks - 2 * per, chunks)
            for k in last:
                if ready:
                    ready(k)
            if last[0] == 0 and free:
                free()
            for t in range(TT):
                for b in range(nb):
                    for k in last:
                        _r, wh, wl = part_views(p + (k - last[0]) // per)
                        c = (k - last[0]) % per * width + b * 512
                        for i, (x, w) in enumerate(((lhs[0], wh), (lhs[0], wl), (lhs[1], wh))):
                            mm = pe.matmul(PS[:, base + nb * t + b, :], x[:, k, t * P:(t + 1) * P], w[:, c:c + 512],
                                           start=(k == 0 and i == 0), stop=(k == chunks - 1 and i == 2))
                        if t == TT - 1 and b == nb - 1 and (k - last[0]) % per == per - 1:
                            mm.then_inc(s_used, 1)
                    if not (t == TT - 1 and b == nb - 1):
                        mm.then_inc(s_acc, 1)

        def half(h):
            return slice(512 * h, 512 * (h + 1))

        def first_half_dve(i, t):
            dve.wait_ge(s_stat, 4 * i + 2 * t + 1)
            dve.tensor_scalar(mean0[:, t:t + 1], stat[:, 2 * t:2 * t + 1], 1.0 / D, EPS, ALU.mult,
                              ALU.add).then_inc(s_mean0, 1)

        def norm_stats_act(i, src, ready, scaled=None):
            for t in range(TT):
                for h in range(2):
                    ready(act, 2 * t + h)
                    act.activation(HN[:, t, half(h)], src[:, t, half(h)], ACT.Square,
                                   accum_out=stat[:, 2 * t + h:2 * t + h + 1]).then_inc(s_stat, 1)
                    if t == 1 and h == 0 and scaled:
                        scaled(0)
                act.wait_ge(s_stat, 4 * i + 2 * t + 2)
                act.wait_ge(s_mean0, 2 * i + t + 1)
                act_then(act.activation(lnv[:, t:t + 1], stat[:, 2 * t + 1:2 * t + 2], ACT.Ln,
                                        bias=mean0[:, t:t + 1], scale=1.0 / D))
                act.activation(rstd[:, t:t + 1], lnv[:, t:t + 1], ACT.Exp, scale=-0.5).then_inc(s_rstd, 1)
            if scaled:
                scaled(1)

        def norm_act(i, src, ready):
            def scaled(t):
                act.wait_ge(s_rstd, 2 * i + t + 1)
                act.activation(HN[:, t, half(0)], src[:, t, half(0)], ACT.Copy,
                               scale=rstd[:, t:t + 1]).then_inc(s_hn_act, 1)
            norm_stats_act(i, src, ready, scaled)

        def norm_dve(i, src, ready=None):
            if ready:
                ready(dve, 1)
                first_half_dve(i, 0)
                ready(dve, 3)
            for t in range(TT):
                if t:
                    first_half_dve(i, 1)
                dve.wait_ge(s_rstd, 2 * i + t + 1)
                dve.tensor_scalar(HN[:, t, half(1)], src[:, t, half(1)], rstd[:, t:t + 1], None,
                                  ALU.mult).then_inc(s_hn_dve, 1)

        def turn_pe(m, src, ready, free=None):
            if free:
                free()
            for t in range(TT):
                for c in range(DC):
                    if c % 4 == 0:
                        ready(t, c // 4)
                    mm = pe.transpose(PS[:, A + c // 2, (c % 2) * T + t * P:(c % 2) * T + (t + 1) * P],
                                      src[:, t, c * P:(c + 1) * P], ident[:, :])
                    if t == TT - 1 and c % 2:
                        mm.then_inc(s_tp, 1)

        def turn_act(m, dst, gain=None):
            for c2 in range(4):
                act.wait_ge(s_tp, 4 * m + c2 + 1)
                if gain is None:
                    act.activation(dst[0][:, 2 * c2:2 * c2 + 2, :],
                                   PS[:, A + c2, :].rearrange("p (c n) -> p c n", c=2), ACT.Copy).then_inc(s_th, 1)
                else:
                    for c in (0, 1):
                        ins = act.activation(dst[0][:, 2 * c2 + c, :], PS[:, A + c2, c * T:(c + 1) * T], ACT.Copy,
                                             scale=ln_cols[:, gain, 2 * c2 + c:2 * c2 + c + 1])
                    ins.then_inc(s_th, 1)

        def turn_dve(m, dst, gain=None):
            for c2 in range(4):
                dve.wait_ge(s_th, 4 * m + c2 + 1)
                if gain is None:
                    cc = slice(2 * c2, 2 * c2 + 2)
                    dve.tensor_tensor(dst[1][:, cc, :], PS[:, A + c2, :].rearrange("p (c n) -> p c n", c=2),
                                      dst[0][:, cc, :].bitcast(F32), ALU.subtract).then_inc(s_tl, 1)
                else:
                    for c in (0, 1):
                        k = 2 * c2 + c
                        ins = dve.scalar_tensor_tensor(
                            out=dst[1][:, k, :], in0=PS[:, A + c2, c * T:(c + 1) * T],
                            scalar=ln_cols[:, gain, k:k + 1], in1=dst[0][:, k, :].bitcast(F32), op0=ALU.mult,
                            op1=ALU.subtract)
                    ins.then_inc(s_tl, 1)

        def turned(m, eng):
            def ready(k):
                if k % 2 == 0:
                    eng.wait_ge(s_tl, 4 * m + k // 2 + 1)
            return ready

        def norm_ready_pe(i):
            def ready(t, h):
                pe.wait_ge((s_hn_act, s_hn_dve)[h], 2 * i + t + 1)
            return ready

        SUMMED = ["w_out", "down", "ple_gate", "ab_out", "xo0", "m20", "c_out", "xo1", "m21"]

        def resid(r):
            def ready(eng, b):
                if b == 0:
                    split_through(eng, SUMMED[r - 1], 2)
                eng.wait_ge(s_x, 4 * (r - 1) + b + 1)
            return ready

        def resid_add_dve(stage, i, base=G):
            for b in range(4):
                rows_done(dve, stage, b)
                x = X[:, b // 2, half(b % 2)]
                dve.tensor_tensor(x, PS[:, base + b, :], x, ALU.add).then_inc(s_x, 1)
                if b == 1:
                    first_half_dve(i, 0)

        MEM = view(44 * 256, (TT, D))
        relrow = view(80 * 256, (257,), 6)
        relext = view(82 * 256, (511,), 6)
        qkT = view(16 * 256, (20, T))
        V1 = view(36 * 256, (TT, D))
        OM = view(44 * 256, (TT, D))
        BT = view(52 * 256, (11, T))
        SQ = view(63 * 256, (2, 512))
        RS = view(67 * 256, (2, 512))
        FG = view(63 * 256, (8, T), 8)
        FL = view(71 * 256, (T,), 102)
        FR = view(72 * 256, (6, T), 102)
        SN = view(0, (3, T))
        PT = view(3 * 256, (3, T))
        MN = view(6 * 256, (40,))
        LS = view(6 * 256 + 40, (40,))
        RL = view(6 * 256 + 80, (40,))
        OD = view(7 * 256, (2, 64))
        DSQ = view(8 * 256, (8, 64))
        DST = view(10 * 256, (3, 8))

        def early_sp(sp):
            for t in range(TT):
                sp.dma_start(X[:, t, :], I["x"][t * P:(t + 1) * P, :]).then_inc(s_x_in[t], 16)
            for dst, src in ((ln_cols[:, :, :], I["ln_cols"].rearrange("p (a b) -> p a b", a=10)),
                             (qk_cols[:, :], I["qk_cols"]),
                             (relrow[:, :], I["rel_rev"])):
                sp.dma_start(dst, src).then_inc(s_early, 16)

        def small_sp(sp):
            sp.dma_start(MEM, I["mem"].rearrange("(t p) d -> p t d", p=P)).then_inc(s_mem, 16)
            for dst, src in ((gate_p[:, :], I["gate_p"]),
                             (row[:, :], I["row"].to_broadcast([P, ROW_LEN])),
                             (conv_cols[:, :, :], I["conv_cols"].rearrange("p (a b) -> p a b", b=4)),
                             (cconv_cols[:, :, :], I["cconv_cols"].rearrange("p (a b) -> p a b", b=4)),
                             (PIN, I["p"].rearrange("(t p) d -> p t d", p=P))):
                sp.dma_start(dst, src).then_inc(s_small, 16)

        N_SMALL = 5
        PIN_t = sb("p_in", [P, TT, 256])
        PIN = PIN_t[:, :, :]
        s_mem = sem("mem_loaded")

        def consts_pool():
            sel_ge = ALU.is_ge
            pool_then(pool.memset(ident[:, :], 0.0))
            pool_then(pool.affine_select(out=ident[:, :], in_=ident[:, :], compare_op=ALU.not_equal, fill=1.0,
                                         base=0, pattern=[[-1, P]], channel_multiplier=1))
            pool.memset(ones[:, :], 1.0)
            pool.memset(eps_c[:, :], EPS)
            pool.memset(eps64_c[:, :], 64 * EPS)
            pool_then(pool.memset(one_c[:, :], 1.0))
            pool.sem_inc(s_const, 1)
            pool.memset(halves[:, :], 0.0)
            pool.memset(tri[:, :], 1.0)
            pool.memset(sel[:, :, :], 0.0)
            pool.memset(neg_ge[:, :, :], 0.0)
            pool_then(pool.memset(neg_gt[:, :, :], 0.0))
            pool_then(pool.memset(halves[0:64, 0:64], 1.0))
            pool_then(pool.memset(halves[64:128, 64:128], 1.0))
            pool.affine_select(out=tri[:, :], in_=tri[:, :], compare_op=sel_ge, fill=0.0, base=0,
                               pattern=[[-1, P]], channel_multiplier=1)
            pool.affine_select(out=sel[:, :, :], in_=sel[:, :, :], compare_op=ALU.not_equal, fill=1.0, base=0,
                               pattern=[[-1, 8], [0, P]], channel_multiplier=1)
            for b in (0, 2):
                pool.affine_select(out=neg_gt[:, b, :], in_=neg_gt[:, b, :], compare_op=sel_ge, fill=-BIG,
                                   base=-1, pattern=[[1, P]], channel_multiplier=-1)
                last = pool.affine_select(out=neg_ge[:, b, :], in_=neg_ge[:, b, :], compare_op=sel_ge, fill=-BIG,
                                          base=0, pattern=[[1, P]], channel_multiplier=-1)
            pool_then(last)
            pool.sem_inc(s_const, 1)
            pool.iota(BT[:, 0, :], pattern=[[-1, T]], base=P, channel_multiplier=1,
                      allow_small_or_imprecise_dtypes=True).then_inc(named("tables"), 1)
            pool_then(pool.memset(BT[:, 4, :], 0.0))
            pool.affine_select(out=BT[:, 4, :], in_=BT[:, 4, :], compare_op=sel_ge, fill=BIG, base=P,
                               pattern=[[-1, T]], channel_multiplier=1).then_inc(named("tables"), 1)
            pool.memset(FR[:, :, :], 0.0)
            pool_then(pool.memset(FL[:, :], 0.0))
            pool_then(pool.memset(FL[32:38, :], 1.0))
            pool_then(pool.memset(FL[96:102, :], 1.0))
            pool.sem_inc(named("tables"), 1)
            pool.wait_ge(named("relext"), 1)
            pool.dma_start(scratch[:, :, :], relext[:, :].unsqueeze(1).to_broadcast([6, P, 511])
                           ).then_inc(named("rel_out"), 16)
            pool.wait_ge(named("rel_out"), 16)
            for h in range(6):
                src = bass.AP(scratch.tensor, h * P * 511 + 127, [[510, P], [1, T]])
                pool.dma_start(BT[:, 5 + h, :], src).then_inc(named("rel_in"), 16)

        def early_dve():
            for j in range(6):
                ins = dve.tensor_scalar(qk_fold[:, j:j + 1], qk_cols[:, j:j + 1], (-1.0, 8.0)[j % 2], None, ALU.mult)
            dve_then(ins)
            dve.tensor_copy(relext[:, 127:384], relrow[:, :])
            dve.tensor_copy(relext[:, 0:127], relrow[:, 0:1].to_broadcast([6, 127]))
            dve_then(dve.tensor_copy(relext[:, 384:511], relrow[:, 256:257].to_broadcast([6, 127])))
            dve.sem_inc(named("relext"), 1)

        def diff_biases_dve():
            dve.wait_ge(named("tables"), 1)
            for h in (1, 2, 3, 0):
                slope = 2.0 ** (-2.0 * (h + 1))
                dve_then(dve.tensor_scalar(BT[:, h, :], BT[:, 0, :], slope, None, ALU.mult))
            dve_then(dve.scalar_tensor_tensor(out=BT[:, 0:4, :], in0=BT[:, 0:4, :], scalar=-1.0, in1=BT[:, 0:4, :],
                                              op0=ALU.mult, op1=ALU.max))
            dve_then(dve.memset(BT[0:64, 0:4, 192:256], BIG))

        def rel_biases_dve():
            dve.wait_ge(named("rel_in"), 16 * 6)
            dve_then(dve.tensor_scalar(BT[:, 5:11, :], BT[:, 5:11, :], -1.0, None, ALU.mult))
            dve_then(dve.memset(BT[0:64, 5:11, 192:256], BIG))

        def lam_dots_dve():
            r = row[:, ROW_LAM:ROW_LAM + 256].rearrange("p (a n) -> p a n", a=4)
            for j in range(2):
                dve.tensor_tensor_reduce(out=HN[:, 0, 64 * j:64 * j + 64], in0=r[:, 2 * j, :], in1=r[:, 2 * j + 1, :],
                                         scale=1.0, scalar=0.0, op0=ALU.mult, op1=ALU.add,
                                         accum_out=lam[:, j:j + 1]).then_inc(named("lam_dots"), 1)

        def lam_dve():
            dve.wait_ge(named("lam_exp"), 1)
            dve_then(dve.tensor_tensor(lam[:, 4:5], lam[:, 3:4], lam[:, 2:3], ALU.subtract))
            dve_then(dve.tensor_scalar(lam[:, 5:6], lam[:, 4:5], -LAM_INIT, None, ALU.add))
            dve_then(dve.tensor_scalar(row[:, ROW_SUBLN:ROW_SUBLN + 64], row[:, ROW_SUBLN:ROW_SUBLN + 64],
                                       1.0 - LAM_INIT, None, ALU.mult))

        QGAIN = [0] * 4 + [1] * 4 + [2] * 3 + [3] * 3 + [4] * 3 + [5] * 3

        def qk_pe():
            def free(u):
                if u >= 4:
                    pe.wait_ge(named("qk_done"), 2 * (u - 3))

            def squares(u):
                pe.wait_ge(named("qk_sq"), u + 1)
                if u >= 2:
                    pe.wait_ge(named("qk_rs"), u - 1)
                elif u == 0:
                    pe.wait_ge(s_const, 2)
                    pe.wait_ge(s_tl, 4)
                pe.matmul(PS[:, A + u % 2, :], halves[:, :], SQ[:, u % 2, :], start=True,
                          stop=True).then_inc(named("qk_ss"), 1)

            for u in range(10):
                cols_unit("qk", u, HT, G + u % 4, free, turned(0, pe))
                if u >= 1:
                    squares(u - 1)
            squares(9)

        def qk_act():
            for u in range(11):
                if u < 10:
                    cols_done(act, "qk", u, 4)
                    if u >= 2:
                        act.wait_ge(named("qk_ss"), u - 1)
                    act.activation(SQ[:, u % 2, :], PS[:, G + u % 4, :], ACT.Square).then_inc(named("qk_sq"), 1)
                if u >= 1:
                    v = u - 1
                    act.wait_ge(named("qk_ss"), v + 1)
                    if v >= 2:
                        act.wait_ge(named("qk_done"), 2 * (v - 1))
                    act.activation(RS[:, v % 2, :], PS[:, A + v % 2, :], ACT.Ln,
                                   bias=eps64_c[:, 0:1]).then_inc(named("qk_rs"), 1)
                    act.wait_ge(named("qk_rs"), v + 1)
                    act.activation(RS[:, v % 2, :], RS[:, v % 2, :], ACT.Exp, scale=-0.5).then_inc(named("qk_rsx"), 1)

        def qk_dve():
            for u in range(10):
                cols_done(dve, "qk", u, 4)
                if u == 2:
                    diff_biases_dve()
                elif u == 5:
                    rel_biases_dve()
                dve.wait_ge(named("qk_rsx"), u + 1)
                for f in range(2):
                    j = QGAIN[2 * u + f]
                    dve.scalar_tensor_tensor(out=qkT[:, 2 * u + f, :], in0=PS[:, G + u % 4, f * T:(f + 1) * T],
                                             scalar=qk_fold[:, j:j + 1], in1=RS[:, u % 2, f * T:(f + 1) * T],
                                             op0=ALU.mult, op1=ALU.mult).then_inc(named("qk_done"), 1)

        def v_pe():
            cols_unit("fg", 0, HT, (A, A + 2), lambda u: pe.wait_ge(named("qk_rs"), 10))

            def turn_mem(k):
                if k == DC - 2:
                    turn_pe(1, HN, norm_ready_pe(1), free=lambda: pe.wait_ge(named("fg_z"), 1))
            rows_product("v", HT, DC, ready=turn_mem, free=lambda: pe.wait_ge(named("qk_done"), 20))

        def lam_act():
            act.wait_ge(named("lam_dots"), 2)
            act.activation(lam[:, 2:4], lam[:, 0:2], ACT.Exp).then_inc(named("lam_exp"), 1)

        def v_act():
            split_through(act, "fg", 4)
            act.wait_ge(named("fg_z"), 1)
            act_then(act.activation(FG[0:6, 3, :], FG[0:6, 2, :], ACT.Exp))
            act.activation(FG[0:6, 4, :], FG[0:6, 3, :], ACT.Ln, bias=one_c[0:6, 0:1]).then_inc(named("fg_ln"), 1)
            lam_act()
            split_through(act, "fg", 7)
            norm_act(1, MEM, lambda e, b: e.wait_ge(s_mem, 16))
            split_through(act, "v", 0)
            turn_act(1, MEMT, LN_MEM)
            for b in range(4):
                rows_done(act, "v", b)
                act.activation(V1[:, b // 2, half(b % 2)], PS[:, G + b, :], ACT.Copy).then_inc(named("v1_ready"), 1)

        def fg_dve():
            cols_done(dve, "fg", 0, 4)
            dve.wait_ge(s_small, 16 * N_SMALL)
            dve_then(dve.tensor_scalar(FG[0:6, 0, :], PS[0:6, A, 0:T], gate_p[0:6, 0:1], None, ALU.add))
            dve_then(dve.tensor_scalar(FG[0:6, 1, :], FG[0:6, 0, :], 0.0, None, ALU.min))
            dve.scalar_tensor_tensor(out=FG[0:6, 2, :], in0=FG[0:6, 1, :], scalar=2.0, in1=FG[0:6, 0, :],
                                     op0=ALU.mult, op1=ALU.subtract).then_inc(named("fg_z"), 1)
            lam_dots_dve()
            dve.wait_ge(named("tables"), 3)
            for h in range(6):
                lo = 64 * (h % 2)
                for q in (0, P):
                    dve.tensor_scalar(FR[lo:lo + 6, h, q:q + P], sel[0:6, h, :], -1.0, None, ALU.mult)
            dve.wait_ge(named("fg_ln"), 1)
            dve_then(dve.tensor_tensor(FG[0:6, 5, :], FG[0:6, 1, :], FG[0:6, 4, :], ALU.subtract))
            dve_then(dve.tensor_tensor_scan(FG[0:6, 6, :], FG[0:6, 5, :], FG[0:6, 5, :], 0.0, ALU.add, ALU.bypass))
            for lo in (0, 64):
                dve.tensor_copy(FL[lo:lo + 6, :], FG[0:6, 6, :])
            for h in range(6):
                lo = 64 * (h % 2)
                ins = dve.tensor_scalar(FR[lo + 32:lo + 38, h, :], FG[0:6, 6, :], sel[0:6, h, 0:1], None, ALU.mult)
            dve_then(ins)
            dve.sem_inc(named("fg_ready"), 1)

        def mem_dve():
            split_through(dve, "fg", 7)
            norm_dve(1, MEM, lambda e, b: e.wait_ge(s_mem, 16))
            split_through(dve, "v", 0)
            turn_dve(1, MEMT, LN_MEM)

        HEADS = []
        for h in range(4):
            for j in range(2):
                HEADS.append((2 * j + h // 2, 4 + 2 * j + h // 2, h % 2, h, 64 * h, "diff", h, j))
        for h in range(6):
            HEADS.append((8 + h // 2, 11 + h // 2, h % 2, 4, 256 + 64 * h, "fox", h, 0))
        for h in range(6):
            HEADS.append((14 + h // 2, 17 + h // 2, h % 2, 5 + h, 640 + 64 * h, "chunk", h, 0))
        NA = 2 * len(HEADS)

        def wide(v):
            return min(v, D - P)

        def attn_pe():
            def scores(n):
                qt, kt, half, _b, _v, kind, h, _j = HEADS[n // 2]
                t, nk = n % 2, P * (n % 2 + 1)
                lo = 64 * half
                if n == 0:
                    pe.wait_ge(named("qk_done"), 20)
                    pe.wait_ge(named("fg_ready"), 1)
                    pe.wait_ge(s_tl, 4 * 2)
                if n >= 2:
                    pe.wait_ge(named("at_max"), n - 1)
                mm = pe.matmul(PS[:, A + n % 2, 0:nk], qkT[lo:lo + 64, qt, t * P:(t + 1) * P],
                               qkT[lo:lo + 64, kt, 0:nk], start=True, stop=(kind != "fox"))
                if kind == "fox":
                    mm = pe.matmul(PS[:, A + n % 2, 0:nk], FL[lo:lo + 38, t * P:(t + 1) * P],
                                   FR[lo:lo + 38, h, 0:nk],
                                   start=False, stop=True)
                mm.then_inc(named("at_s"), 1)

            def turn(n):
                t = n % 2
                pe.wait_ge(named("at_exp"), n + 1)
                if n >= 2:
                    pe.wait_ge(named("at_pt"), n - 1)
                for b in range(t + 1):
                    mm = pe.transpose(PS[:, A + 2 + t, b * P:(b + 1) * P],
                                      SN[:, n % 3, b * P:(b + 1) * P], ident[:, :])
                mm.then_inc(named("at_tp"), 1)

            def weigh(n):
                v = HEADS[n // 2][4]
                t = n % 2
                pe.wait_ge(named("at_pt"), n + 1)
                if n == 0:
                    pe.wait_ge(named("v1_ready"), 4)
                if n >= 2:
                    pe.wait_ge(named("at_o"), n - 1)
                for b in range(t + 1):
                    mm = pe.matmul(PS[:, G + n % 2, 0:P], PT[:, n % 3, b * P:(b + 1) * P],
                                   V1[:, b, wide(v):wide(v) + P], start=(b == 0), stop=(b == t))
                mm.then_inc(named("at_pv"), 1)

            for n in range(NA + 2):
                if n < NA:
                    scores(n)
                if 1 <= n <= NA:
                    turn(n - 1)
                if n >= 2:
                    weigh(n - 2)

        def attn_act():
            for n in range(NA + 1):
                if n < NA:
                    nk = P * (n % 2 + 1)
                    act.wait_ge(named("at_max"), n + 1)
                    act.activation(SN[:, n % 3, 0:nk], SN[:, n % 3, 0:nk], ACT.Exp, bias=MN[:, n:n + 1], scale=-1.0,
                                   accum_out=LS[:, n:n + 1]).then_inc(named("at_exp"), 1)
                if n >= 1:
                    m = n - 1
                    nk = P * (m % 2 + 1)
                    act.wait_ge(named("at_tp"), m + 1)
                    if m >= 3:
                        act.wait_ge(named("at_pv"), m - 2)
                    act.activation(PT[:, m % 3, 0:nk], PS[:, A + 2 + m % 2, 0:nk],
                                   ACT.Copy).then_inc(named("at_pt"), 1)
                if n == 25:
                    subln_act()
                elif n in (33, 36):
                    split_through(act, "v", 3 + (n == 36))

        def attn_dve():
            def low(n):
                bias = HEADS[n // 2][3]
                t, nk = n % 2, P * (n % 2 + 1)
                dve.wait_ge(named("at_s"), n + 1)
                if n == 8 * 2:
                    dve.wait_ge(named("tables"), 2)
                if n >= 3:
                    dve.wait_ge(named("at_tp"), n - 2)
                dve.tensor_tensor_reduce(out=SN[:, n % 3, 0:nk], in0=PS[:, A + n % 2, 0:nk],
                                         in1=BT[:, bias, T - nk:T], scale=1.0, scalar=3.0e38, op0=ALU.add,
                                         op1=ALU.min, accum_out=MN[:, n:n + 1]).then_inc(named("at_max"), 1)

            def finish(n):
                _q, _k, _half, _b, v, kind, h, j = HEADS[n // 2]
                t = n % 2
                dve.wait_ge(named("at_exp"), n + 1)
                dve_then(dve.reciprocal(RL[:, n:n + 1], LS[:, n:n + 1]))
                o = PS[:, G + n % 2, v - wide(v):v - wide(v) + 64]
                if kind == "diff" and j == 0:
                    dve.wait_ge(named("at_pv"), n + 1)
                    dve_then(dve.tensor_scalar(OD[:, t, :], o, RL[:, n:n + 1], None, ALU.mult))
                    dve.sem_inc(named("at_o"), 1)
                elif kind == "diff":
                    dve_then(dve.tensor_tensor(RL[:, n:n + 1], RL[:, n:n + 1], lam[:, 5:6], ALU.mult))
                    dve.wait_ge(named("at_pv"), n + 1)
                    dve.scalar_tensor_tensor(out=OM[:, t, v:v + 64], in0=o, scalar=RL[:, n:n + 1], in1=OD[:, t, :],
                                             op0=ALU.mult, op1=ALU.add).then_inc(named("at_o"), 1)
                else:
                    dve.wait_ge(named("at_pv"), n + 1)
                    dve.tensor_scalar(OM[:, t, v:v + 64], o, RL[:, n:n + 1], None, ALU.mult).then_inc(named("at_o"), 1)

            for n in range(NA + 2):
                if n < NA:
                    low(n)
                if n >= 2:
                    finish(n - 2)
                if n in (19, 22):
                    subln_squares_dve((n - 19) // 3)
                elif n in (28, 31):
                    subln_scale_dve((n - 28) // 3)
                elif n in (34, 37):
                    split_through(dve, "v", 3 + (n == 37))
        def subln_squares_dve(t):
            dve.wait_ge(named("at_o"), 16)
            o = OM[:, t, 0:256].rearrange("p (h d) -> p h d", h=4)
            dve_then(dve.tensor_tensor(DSQ[:, 4 * t:4 * t + 4, :], o, o, ALU.mult))
            dve.tensor_reduce(DST[:, 0, 4 * t:4 * t + 4], DSQ[:, 4 * t:4 * t + 4, :], AX.X,
                              ALU.add).then_inc(named("sub_sum"), 1)

        def subln_scale_dve(t):
            dve.wait_ge(named("sub_rs"), 1)
            o = OM[:, t, 0:256].rearrange("p (h d) -> p h d", h=4)
            r = DST[:, 2, 4 * t:4 * t + 4].unsqueeze(2).to_broadcast([P, 4, 64])
            dve_then(dve.tensor_tensor(o, o, r, ALU.mult))
            dve.tensor_tensor(o, o, row[:, ROW_SUBLN:ROW_SUBLN + 64].unsqueeze(1).to_broadcast([P, 4, 64]),
                              ALU.mult).then_inc(named("mix_out"), 1)

        def subln_act():
            act.wait_ge(named("sub_sum"), 2)
            act_then(act.activation(DST[:, 1, :], DST[:, 0, :], ACT.Ln, bias=eps_c[:, 0:1], scale=1.0 / 64))
            act.activation(DST[:, 2, :], DST[:, 1, :], ACT.Exp, scale=-0.5).then_inc(named("sub_rs"), 1)

        GT = pair(16 * 256, FF_TILES)
        CS = view(60 * 256, (4, 2, T))
        SLU = view(68 * 256, (2, 2, T))
        GF = view(72 * 256, (2, 2, T))
        NUP = 2 * (D_FF // 256)

        def up_pe():
            def free(u):
                if u >= 4:
                    pe.wait_ge(named("up_conv"), u - 3)
                elif u == 0:
                    pe.wait_ge(s_x, 4)

            for u in range(NUP):
                cols_unit("up", u, HT, G + u % 4, free, turned(3, pe))

        def up_tile(u, f):
            return (u % 2) * FF_TILES + 2 * (u // 2) + f

        def up_act():
            def silu(j):
                act.wait_ge(named("up_conv"), 2 * j + 1)
                if j >= 2:
                    act.wait_ge(named("up_g"), j - 1)
                act.activation(SLU[:, j % 2, :, :], CS[:, (2 * j) % 4, :, :], ACT.Silu).then_inc(named("up_silu"), 1)

            def high(j):
                act.wait_ge(named("up_g"), j + 1)
                act.activation(GT[0][:, 2 * j:2 * j + 2, :], GF[:, j % 2, :, :], ACT.Copy).then_inc(named("up_gh"), 1)

            for u in range(NUP):
                cols_done(act, "up", u)
                if u >= 4:
                    act.wait_ge(named("up_g"), (u - 4) // 2 + 1)
                for f in range(2):
                    c = conv_cols[:, up_tile(u, f), :]
                    ins = act.activation(CS[:, u % 4, f, :], PS[:, G + u % 4, f * T:(f + 1) * T], ACT.Identity,
                                         bias=c[:, 3:4], scale=c[:, 2:3])
                ins.then_inc(named("up_tap"), 1)
                if u % 2:
                    silu(u // 2)
                elif u >= 2:
                    high(u // 2 - 1)
            high(NUP // 2 - 1)

        def up_dve():
            def low(j):
                dve.wait_ge(named("up_gh"), j + 1)
                dve.tensor_tensor(GT[1][:, 2 * j:2 * j + 2, :], GF[:, j % 2, :, :],
                                  GT[0][:, 2 * j:2 * j + 2, :].bitcast(F32), ALU.subtract).then_inc(named("up_gl"), 1)

            for u in range(NUP):
                cols_done(dve, "up", u)
                if u % 2 == 1 and u >= 3:
                    low((u - 3) // 2)
                dve.wait_ge(named("up_tap"), u + 1)
                for tap in (1, 0):
                    lag = 2 - tap
                    for f in range(2):
                        c = conv_cols[:, up_tile(u, f), :]
                        ins = dve.scalar_tensor_tensor(
                            out=CS[:, u % 4, f, lag:T], in0=PS[:, G + u % 4, f * T:(f + 1) * T - lag],
                            scalar=c[:, tap:tap + 1], in1=CS[:, u % 4, f, lag:T], op0=ALU.mult, op1=ALU.add)
                        if not (tap == 0 and f == 1):
                            if tap == 1 and f == 1:
                                dve_then(ins)
                ins.then_inc(named("up_conv"), 1)
            low(NUP // 2 - 1)

        def up_pool():
            for j in range(NUP // 2):
                pool.wait_ge(named("up_silu"), j + 1)
                pool.wait_ge(named("up_conv"), 2 * j + 2)
                if j >= 2:
                    pool.wait_ge(named("up_gl"), j - 1)
                pool.tensor_tensor(GF[:, j % 2, :, :], SLU[:, j % 2, :, :], CS[:, (2 * j + 1) % 4, :, :],
                                   ALU.mult).then_inc(named("up_g"), 1)

        def down_pe():
            rows_product("down", GT, FF_TILES, ready=lambda k: pe.wait_ge(named("up_gl"), k // 2 + 1),
                         free=lambda: pe.wait_ge(named("up_conv"), NUP))

        PTT = pair(76 * 256, 2)
        SG = view(20 * 256, (TT, D))
        PG = view(28 * 256, (2, 512))

        def ple_p_pe():
            pe.wait_ge(s_small, 16 * N_SMALL)
            for c in range(2):
                for t in range(TT):
                    mm = pe.transpose(PS[:, A, c * T + t * P:c * T + (t + 1) * P], PIN[:, t, c * P:(c + 1) * P],
                                      ident[:, :])
            mm.then_inc(named("p_turned"), 1)

        def ple_p_act():
            act.wait_ge(named("p_turned"), 1)
            act.activation(PTT[0], PS[:, A, :].rearrange("p (c n) -> p c n", c=2), ACT.Copy).then_inc(named("p_t"), 1)

        def ple_p_dve():
            dve.wait_ge(named("p_t"), 1)
            dve.tensor_tensor(PTT[1], PS[:, A, :].rearrange("p (c n) -> p c n", c=2), PTT[0].bitcast(F32),
                              ALU.subtract).then_inc(named("p_l"), 1)

        def ple_proj_pe():
            rows_product("ple_proj", PTT, 2, free=lambda: (pe.wait_ge(named("p_l"), 1), pe.wait_ge(s_x, 4 * 2)))

        def ple_gate_pe():
            rows_product("ple_gate", HT, DC, base=A, ready=turned(4, pe),
                         free_tile=lambda t: pe.wait_ge(s_tl, 4 * 4 + 2 * (t + 1)))

        def ple_act():
            for b in range(4):
                rows_done(act, "ple_gate", b)
                act.activation(SG[:, b // 2, half(b % 2)], PS[:, A + b, :], ACT.Sigmoid).then_inc(named("ple_sg"), 1)

        def ple_dve():
            for b in range(4):
                rows_done(dve, "ple_gate", b)
                dve.wait_ge(named("ple_sg"), b + 1)
                dve_then(dve.tensor_tensor(PG[:, b % 2, :], PS[:, G + b, :], SG[:, b // 2, half(b % 2)], ALU.mult))
                x = X[:, b // 2, half(b % 2)]
                dve.tensor_tensor(x, x, PG[:, b % 2, :], ALU.add).then_inc(s_x, 1)
                if b == 1:
                    first_half_dve(4, 0)

        ABT = view(16 * 256, (12, T))
        VA = view(28 * 256, (TT, 4, 129))
        SGM = view(33 * 256, (TT, 512))
        SV = view(37 * 256, (TT, 512))
        OM2 = view(41 * 256, (TT, D))
        ROWSG = view(49 * 256, (12, T), 8)
        GA = view(61 * 256, (T,), 36)
        U3 = view(0, (2, 384))
        L3 = view(3 * 256, (2, 384))
        SP3 = view(6 * 256, (2, 384))
        W3 = view(9 * 256, (2, 384))
        HSQ = view(65 * 256, (TT, 4, P))
        HST = view(69 * 256, (4, 8))
        GC = view(62 * 256, (TT, 36))
        DN = view(63 * 256, (4, 2, 2))

        def ab_pe():
            def free(u):
                if u == 0:
                    pe.wait_ge(named("xk_a"), 2)
                    pe.wait_ge(named("xk_d"), 2)
                if u >= 4:
                    pe.wait_ge(named(("ab_ca", "ab_cd")[u % 2]), (u - 4) // 2 + 1)
            for u in range(6):
                cols_unit("ab_qk", u, HT, G + u % 4, free, turned(5, pe))
            cols_unit("ab_g", 0, HT, (A + 2, A + 3), lambda u: pe.wait_ge(s_tl, 4 * 6))

            def free2():
                pe.wait_ge(named("ab_ca"), 3)
                pe.wait_ge(named("ab_cd"), 3)
            rows_product("ab_vo", HT, DC, free=free2)
            pe.wait_ge(named("ab_rows"), 1)
            for t in range(TT):
                mm = pe.transpose(PS[:, A + 2, 36 * t:36 * t + 36], GA[:, t * P:(t + 1) * P], ident[0:36, 0:36])
            mm.then_inc(named("ab_cols"), 1)
            rows_product("ab_sv", HT, DC, width=512, base=A)

            def first(n):
                if n == 0:
                    pe.wait_ge(named("ab_va"), 2)
                    pe.wait_ge(named("ab_sgm"), 2)
                    pe.wait_ge(named("ab_svr"), 2)
                    pe.wait_ge(named("ab_gc"), 1)
                if n >= 2:
                    pe.wait_ge(named("ab_u"), n - 1)
                b = n % 2
                if n < 4:
                    m = ROWSG[0:4, 8, :]
                    pe.matmul(PS[:, b, 0:T], sel[0:4, n, :], m, start=True, stop=True)
                    mm = pe.matmul(PS[:, b, T:384], sel[0:4, n, :], ROWSG[0:4, 8, P:T], start=True, stop=True)
                else:
                    h = n - 4
                    pe.matmul(PS[:, b, 0:T], ABT[:, 4 + h, 0:P], ABT[:, h, :], start=True, stop=True)
                    mm = pe.matmul(PS[:, b, T:384], ABT[:, 4 + h, P:T], ABT[:, h, P:T], start=True, stop=True)
                mm.then_inc(named("ab_first"), 1)

            def second(n):
                b = 2 + n % 2
                if n >= 2:
                    pe.wait_ge(named("ab_sec_read"), n - 1)
                if n < 4:
                    lo = 64 * (n % 2)
                    q, k = ABT[lo:lo + 64, 8 + n // 2, :], ABT[lo:lo + 64, 10 + n // 2, :]
                    pe.matmul(PS[:, b, 0:T], k[:, 0:P], q, start=True, stop=True)
                    mm = pe.matmul(PS[:, b, T:384], k[:, P:T], q[:, P:T], start=True, stop=True)
                else:
                    pe.wait_ge(named("ab_sp"), n - 3)
                    sp3 = SP3[:, n % 2, :]
                    pe.matmul(PS[:, b, 0:384], tri[:, :], sp3, start=True, stop=False)
                    mm = pe.matmul(PS[:, b, P:T], ones[:, :], sp3[:, T:384], start=False, stop=True)
                mm.then_inc(named("ab_second"), 1)

            def weigh(n):
                b = 4 + n % 2
                pe.wait_ge(named("ab_w"), n + 1)
                if n >= 2:
                    pe.wait_ge(named("ab_o"), n - 1)
                w = W3[:, n % 2, :]
                nv = 129 if n < 4 else P
                v = [VA[:, t, n, :] if n < 4 else SV[:, t, (n - 4) * P:(n - 3) * P] for t in range(TT)]
                pe.matmul(PS[:, b, 0:nv], w[:, 0:P], v[0], start=True, stop=True)
                pe.matmul(PS[:, b, nv:2 * nv], w[:, P:T], v[0], start=True, stop=False)
                mm = pe.matmul(PS[:, b, nv:2 * nv], w[:, T:384], v[1], start=False, stop=True)
                mm.then_inc(named("ab_pv"), 1)

            for n in range(10):
                if n < 8:
                    first(n)
                if 1 <= n <= 8:
                    second(n - 1)
                if n >= 2:
                    weigh(n - 2)

        def ab_act():
            for u in range(0, 6, 2):
                cols_done(act, "ab_qk", u)
                act.activation(ABT[:, 2 * u:2 * u + 2, :], PS[:, G + u % 4, :].rearrange("p (c n) -> p c n", c=2),
                               ACT.Copy, scale=(P ** -0.5 if u < 2 else 1.0)).then_inc(named("ab_ca"), 1)
            split_through(act, "ab_g", 3)
            act.wait_ge(named("ab_zi"), 1)
            act.activation(ROWSG[0:4, 1, :], ROWSG[0:4, 0, :], ACT.Tanh, scale=1.0 / 15).then_inc(named("ab_li"), 1)
            act.preload_act_table_set(EXP_LN)
            act.wait_ge(named("ab_zf"), 1)
            act_then(act.activation(ROWSG[0:4, 4, :], ROWSG[0:4, 3, :], ACT.Exp))
            act.activation(ROWSG[0:4, 5, :], ROWSG[0:4, 4, :], ACT.Ln, bias=one_c[0:4, 0:1]).then_inc(named("ab_lf"), 1)
            split_through(act, "ab_g", 4)
            act.wait_ge(named("ab_m"), 1)
            act.activation(GA[32:36, :], ROWSG[0:4, 9, :], ACT.Exp, scale=-1.0).then_inc(named("ab_enm"), 1)
            for t in range(TT):
                rows_done(act, "ab_vo", 2 * t + 1)
                act.activation(SGM[:, t, :], PS[:, G + 2 * t + 1, :], ACT.Sigmoid).then_inc(named("ab_sgm"), 1)
            act.preload_act_table_set(EXP_LN)
            for t in range(TT):
                rows_done(act, "ab_sv", t)
                act.activation(SV[:, t, :], PS[:, A + t, :], ACT.Copy).then_inc(named("ab_svr"), 1)
            split_through(act, "ab_sv", 4)
            for n in range(9):
                if n < 8:
                    act.wait_ge(named("ab_u"), n + 1)
                    if n < 4:
                        act.activation(L3[:, n % 2, :], U3[:, n % 2, :], ACT.Exp).then_inc(named("ab_l"), 1)
                    else:
                        if n >= 6:
                            act.wait_ge(named("ab_sp"), n - 5)
                        act_then(act.activation(L3[:, n % 2, :], U3[:, n % 2, :], ACT.Abs))
                        act_then(act.activation(L3[:, n % 2, :], L3[:, n % 2, :], ACT.Exp, scale=-1.0))
                        act.activation(L3[:, n % 2, :], L3[:, n % 2, :], ACT.Ln,
                                       bias=one_c[:, 0:1]).then_inc(named("ab_l"), 1)
                if n >= 5:
                    m = n - 1
                    act.wait_ge(named("ab_sec_read"), m + 1)
                    act.wait_ge(named("ab_pv"), m - 1)
                    act.activation(W3[:, m % 2, :], U3[:, m % 2, :], ACT.Exp).then_inc(named("ab_w"), 1)
                if n == 7:
                    act.wait_ge(named("ab_ssq"), 1)
                    act_then(act.activation(HST[:, 1, :], HST[:, 0, :], ACT.Ln, bias=eps_c[:, 0:1], scale=1.0 / P))
                    act.activation(HST[:, 2, :], HST[:, 1, :], ACT.Exp, scale=-0.5).then_inc(named("ab_hrs"), 1)

        def ab_dve():
            for u in range(1, 6, 2):
                cols_done(dve, "ab_qk", u)
                dve.tensor_scalar(ABT[:, 2 * u:2 * u + 2, :], PS[:, G + u % 4, :].rearrange("p (c n) -> p c n", c=2),
                                  {1: P ** -0.5, 3: 1.0, 5: 64 ** -0.5}[u], None, ALU.mult).then_inc(named("ab_cd"), 1)
            R = lambda j: ROWSG[0:4, j, :]
            cols_done(dve, "ab_g", 0)
            dve.tensor_scalar(R(0), PS[0:4, A + 2, 0:T], gate_p[0:4, 1:2], None, ALU.add).then_inc(named("ab_zi"), 1)
            dve_then(dve.tensor_scalar(R(6), PS[0:4, A + 3, 0:T], gate_p[0:4, 2:3], None, ALU.add))
            dve_then(dve.tensor_scalar(R(2), R(6), 0.0, None, ALU.min))
            dve.scalar_tensor_tensor(out=R(3), in0=R(2), scalar=2.0, in1=R(6), op0=ALU.mult,
                                     op1=ALU.subtract).then_inc(named("ab_zf"), 1)
            dve.memset(GA[:, :], 0.0)
            dve.memset(VA[:, :, :, 128:129], 1.0)
            dve.wait_ge(named("ab_lf"), 1)
            dve.wait_ge(named("ab_li"), 1)
            dve_then(dve.tensor_tensor(R(6), R(2), R(5), ALU.subtract))
            dve_then(dve.tensor_tensor_scan(R(7), R(6), R(6), 0.0, ALU.add, ALU.bypass))
            dve_then(dve.scalar_tensor_tensor(out=R(10), in0=R(1), scalar=15.0, in1=R(7), op0=ALU.mult,
                                              op1=ALU.subtract))
            dve_then(dve.tensor_tensor_scan(R(11), R(10), R(10), 0.0, ALU.max, ALU.max))
            dve_then(dve.tensor_scalar(R(8), R(11), -1.0, None, ALU.mult))
            dve.tensor_copy(GA[0:4, :], R(10))
            dve_then(dve.tensor_tensor(R(9), R(7), R(11), ALU.add))
            dve.sem_inc(named("ab_m"), 1)
            split_through(dve, "ab_g", 4)
            dve.wait_ge(named("ab_enm"), 1)
            dve.sem_inc(named("ab_rows"), 1)
            for t in range(TT):
                rows_done(dve, "ab_vo", 2 * t)
                dve.tensor_copy(VA[:, t, :, 0:P], PS[:, G + 2 * t, :].rearrange("p (h d) -> p h d", h=4)
                                ).then_inc(named("ab_va"), 1)
            split_through(dve, "ab_vo", 4)
            dve.wait_ge(named("ab_cols"), 1)
            dve_then(dve.tensor_copy(GC[:, :, :], PS[:, A + 2, 0:72].rearrange("p (t n) -> p t n", t=2)))
            dve.sem_inc(named("ab_gc"), 1)
            split_through(dve, "ab_sv", 4)

            def after_first(n):
                dve.wait_ge(named("ab_first"), n + 1)
                u, z = U3[:, n % 2, :], PS[:, n % 2, 0:384]
                if 2 <= n < 6:
                    dve.wait_ge(named("ab_l"), n - 1)
                if n >= 6:
                    dve.wait_ge(named("ab_w"), n - 1)
                if n < 4:
                    dve.scalar_tensor_tensor(out=u[:, 0:T], in0=z[:, 0:T], scalar=GC[:, 0, n:n + 1],
                                             in1=neg_ge[:, 0:2, :], op0=ALU.add, op1=ALU.add)
                    dve.scalar_tensor_tensor(out=u[:, T:384], in0=z[:, T:384], scalar=GC[:, 1, n:n + 1],
                                             in1=neg_ge[:, 2, :], op0=ALU.add, op1=ALU.add).then_inc(named("ab_u"), 1)
                else:
                    dve.tensor_tensor(u, z, neg_gt[:, :, :].rearrange("p a b -> p (a b)"),
                                      ALU.add).then_inc(named("ab_u"), 1)

            def after_l(n):
                if n < 4:
                    dve.wait_ge(named("ab_l"), n + 1)
                    dve.wait_ge(named("ab_second"), n + 1)
                    if n >= 2:
                        dve.wait_ge(named("ab_pv"), n - 1)
                    dve_then(dve.tensor_tensor(W3[:, n % 2, :], PS[:, 2 + n % 2, 0:384], L3[:, n % 2, :], ALU.mult))
                    dve.sem_inc(named("ab_w"), 1)
                    dve.sem_inc(named("ab_sec_read"), 1)
                else:
                    dve.wait_ge(named("ab_l"), n + 1)
                    if n >= 6:
                        dve.wait_ge(named("ab_second"), n - 1)
                    dve_then(dve.scalar_tensor_tensor(out=SP3[:, n % 2, :], in0=U3[:, n % 2, :], scalar=0.0,
                                                      in1=L3[:, n % 2, :], op0=ALU.max, op1=ALU.add))
                    dve.sem_inc(named("ab_sp"), 1)
                    dve.wait_ge(named("ab_second"), n + 1)
                    dve.scalar_tensor_tensor(out=U3[:, n % 2, :], in0=PS[:, 2 + n % 2, 0:384], scalar=-1.0,
                                             in1=U3[:, n % 2, :], op0=ALU.mult,
                                             op1=ALU.add).then_inc(named("ab_sec_read"), 1)

            def finish(n):
                dve.wait_ge(named("ab_pv"), n + 1)
                b = 4 + n % 2
                if n < 4:
                    o = PS[:, b, 0:258].rearrange("p (t n) -> p t n", t=2)
                    dn = DN[:, n, :, :]
                    dve_then(dve.scalar_tensor_tensor(out=dn[:, 0, :], in0=o[:, :, 128], scalar=-1.0,
                                                      in1=GC[:, :, 32 + n], op0=ALU.mult, op1=ALU.max))
                    dve_then(dve.tensor_tensor(dn[:, 0, :], o[:, :, 128], dn[:, 0, :], ALU.max))
                    dve_then(dve.reciprocal(dn[:, 1, :], dn[:, 0, :]))
                    for t in range(TT):
                        ins = dve.tensor_scalar(OM2[:, t, n * P:(n + 1) * P], o[:, t, 0:P], dn[:, 1, t:t + 1], None,
                                                ALU.mult)
                    ins.then_inc(named("ab_o"), 1)
                else:
                    dve.tensor_copy(OM2[:, :, n * P:(n + 1) * P],
                                    PS[:, b, 0:T].rearrange("p (t n) -> p t n", t=2)).then_inc(named("ab_o"), 1)

            for n in range(10):
                if n < 8:
                    after_first(n)
                if 1 <= n <= 8:
                    after_l(n - 1)
                if n >= 2:
                    finish(n - 2)
                if n == 6:
                    dve.wait_ge(named("ab_o"), 4)
                    head_squares_dve(OM2[:, :, 0:512], HSQ, HST, 4, "ab_ssq")
                if n == 8:
                    dve.wait_ge(named("ab_hrs"), 1)
                    dve.wait_ge(named("gate_gain"), 2)
                    for t in range(TT):
                        head_gate_dve(OM2[:, :, 0:512], t, HST, 4, SGM, "ab_om")

        def head_squares_dve(o_all, sq, st, heads, told):
            for t in range(TT):
                o = o_all[:, t, :].rearrange("p (h d) -> p h d", h=heads)
                dve_then(dve.tensor_tensor(sq[:, t, :, :], o, o, ALU.mult))
                dve_then(dve.tensor_reduce(st[:, 0, heads * t:heads * (t + 1)], sq[:, t, :, :], AX.X, ALU.add))
            dve.sem_inc(named(told), 1)

        def head_gate_dve(o_all, t, st, heads, gate, done):
            o = o_all[:, t, :].rearrange("p (h d) -> p h d", h=heads)
            r = st[:, 2, heads * t:heads * (t + 1)].unsqueeze(2).to_broadcast([P, heads, P])
            dve_then(dve.tensor_tensor(o, o, r, ALU.mult))
            dve.tensor_tensor(o, o, gate[:, t, :].rearrange("p (h d) -> p h d", h=heads),
                              ALU.mult).then_inc(named(done), 1)

        def gate_gain_pool(gate, gain, heads, sem_name, per_tile, told):
            for t in range(TT):
                pool.wait_ge(named(sem_name), per_tile * (t + 1))
                g = gate[:, t, :].rearrange("p (h d) -> p h d", h=heads)
                pool.tensor_tensor(g, g, gain, ALU.mult).then_inc(named(told), 1)

        XQ = view(16 * 256, (8, T))
        XKS = [view(72 * 256, (8, T)), view(24 * 256, (8, T))]
        XV = view(32 * 256, (TT, D))
        XP = view(40 * 256, (3, T))
        XPT = view(43 * 256, (2, 2, T))
        XMN = view(47 * 256, (3, 8))
        XO = pair(48 * 256, 8)
        NX = 8

        def xa_k_pe(l):
            def free(u):
                pe.wait_ge(s_x, (4 * 6 if l else 4 * 2) + u + 1)
            for u in range(4):
                cols_unit(f"xk{l}", u, MEMT, G + u, free)

        def xa_v_pe(l):
            def free():
                pe.wait_ge(s_x, 4 * (4 + 3 * l))
                pe.wait_ge(named("xk_a"), 2 * l + 2)
                pe.wait_ge(named("xk_d"), 2 * l + 2)
            rows_product(f"xv{l}", MEMT, DC, free=free)

        def xa_k_evac(l, eng):
            k = 0 if eng is act else 1
            for u in (k, k + 2):
                cols_done(eng, f"xk{l}", u)
                src = PS[:, G + u, :].rearrange("p (c n) -> p c n", c=2)
                if k:
                    dve.tensor_copy(XKS[l][:, 2 * u:2 * u + 2, :], src).then_inc(named("xk_d"), 1)
                else:
                    act.activation(XKS[l][:, 2 * u:2 * u + 2, :], src, ACT.Copy).then_inc(named("xk_a"), 1)
            split_through(eng, f"xk{l}", 4)

        def xa_v_evac(l, eng):
            k = 0 if eng is act else 1
            for b in (k, k + 2):
                rows_done(eng, f"xv{l}", b)
                dst = XV[:, b // 2, (b % 2) * 512:(b % 2 + 1) * 512]
                if k:
                    dve.tensor_copy(dst, PS[:, G + b, :]).then_inc(named("xv_d"), 1)
                else:
                    act.activation(dst, PS[:, G + b, :], ACT.Copy).then_inc(named("xv_a"), 1)
            split_through(eng, f"xv{l}", 4)

        def xa_pe(l, turn):
            c0 = NX * l

            def free(u):
                if u == 0:
                    pe.wait_ge(named("xv_a"), 2 * l + 2)
                    pe.wait_ge(named("xv_d"), 2 * l + 2)
            for u in range(4):
                cols_unit(f"xq{l}", u, HT, G + u, free, turned(turn, pe))

            def scores(n):
                h, t = n // 2, n % 2
                if n == 0:
                    pe.wait_ge(s_tl, 4 * (turn + 1))
                pe.wait_ge(named(("xq_a", "xq_d")[h % 2]), 2 * l + h // 2 + 1)
                if n >= 2:
                    pe.wait_ge(named("xa_exp"), c0 + n - 1)
                for c in range(2):
                    mm = pe.matmul(PS[:, A + n % 2, 0:T], XQ[:, 2 * h + c, t * P:(t + 1) * P], XKS[l][:, 2 * h + c, :],
                                   start=(c == 0), stop=(c == 1))
                mm.then_inc(named("xa_s"), 1)

            def turn_p(n):
                pe.wait_ge(named("xa_norm"), c0 + n + 1)
                if n >= 2:
                    pe.wait_ge(named("xa_pt"), c0 + n - 1)
                for b in range(2):
                    mm = pe.transpose(PS[:, A + 2 + n % 2, b * P:(b + 1) * P], XP[:, n % 3, b * P:(b + 1) * P],
                                      ident[:, :])
                mm.then_inc(named("xa_tp"), 1)

            def weigh(h):
                pe.wait_ge(named("xa_pt"), c0 + 2 * h + 2)
                if h >= 2:
                    pe.wait_ge(named("xa_o"), 4 * l + h - 1)
                elif h == 0:
                    pe.wait_ge(named("xq_a"), 2 * l + 2)
                    pe.wait_ge(named("xq_d"), 2 * l + 2)
                for c in range(2):
                    for m in range(2):
                        mm = pe.matmul(PS[:, G + h % 2, c * T:(c + 1) * T],
                                       XV[:, m, h * T + c * P:h * T + (c + 1) * P], XPT[:, h % 2, m, :],
                                       start=(m == 0), stop=(m == 1))
                mm.then_inc(named("xa_pv"), 1)

            for n in range(NX + 3):
                if n < NX:
                    scores(n)
                if 2 <= n <= NX + 1:
                    turn_p(n - 2)
                if n >= 4 and n % 2 == 0:
                    weigh((n - 4) // 2)
            rows_product(f"xo{l}", XO, DC, ready=lambda k: pe.wait_ge(named("xa_o"), 4 * l + k // 2 + 1),
                         free=lambda: pe.wait_ge(named("xa_o"), 4 * l + 4))

        def xa_act(l):
            c0 = NX * l
            for u in (0, 2):
                cols_done(act, f"xq{l}", u)
                act.activation(XQ[:, 2 * u:2 * u + 2, :], PS[:, G + u, :].rearrange("p (c n) -> p c n", c=2),
                               ACT.Copy, scale=-1.0 / 16).then_inc(named("xq_a"), 1)
            split_through(act, f"xq{l}", 4)
            for n in range(NX + 4):
                if n < NX:
                    act.wait_ge(named("xa_min"), c0 + n + 1)
                    if n >= 3:
                        act.wait_ge(named("xa_tp"), c0 + n - 2)
                    act.activation(XP[:, n % 3, :], PS[:, A + n % 2, 0:T], ACT.Exp, bias=XMN[:, 0, n:n + 1],
                                   scale=-1.0, accum_out=XMN[:, 1, n:n + 1]).then_inc(named("xa_exp"), 1)
                if 2 <= n <= NX + 1:
                    m = n - 2
                    h, t = m // 2, m % 2
                    act.wait_ge(named("xa_tp"), c0 + m + 1)
                    if h >= 2:
                        act.wait_ge(named("xa_pv"), 4 * l + h - 1)
                    act.activation(XPT[:, h % 2, :, t * P:(t + 1) * P],
                                   PS[:, A + 2 + m % 2, 0:T].rearrange("p (m n) -> p m n", m=2),
                                   ACT.Copy).then_inc(named("xa_pt"), 1)
                if n >= 5 and n % 2:
                    h = (n - 5) // 2
                    act.wait_ge(named("xa_pv"), 4 * l + h + 1)
                    act.activation(XO[0][:, 2 * h:2 * h + 2, :], PS[:, G + h % 2, :].rearrange("p (c n) -> p c n", c=2),
                                   ACT.Copy).then_inc(named("xa_oh"), 1)

        def xa_dve(l):
            c0 = NX * l
            for u in (1, 3):
                cols_done(dve, f"xq{l}", u)
                dve.tensor_scalar(XQ[:, 2 * u:2 * u + 2, :], PS[:, G + u, :].rearrange("p (c n) -> p c n", c=2),
                                  -1.0 / 16, None, ALU.mult).then_inc(named("xq_d"), 1)
            split_through(dve, f"xq{l}", 4)
            for n in range(NX + 4):
                if n < NX:
                    dve.wait_ge(named("xa_s"), c0 + n + 1)
                    dve.tensor_reduce(XMN[:, 0, n:n + 1], PS[:, A + n % 2, 0:T], AX.X,
                                      ALU.min).then_inc(named("xa_min"), 1)
                if 1 <= n <= NX:
                    m = n - 1
                    dve.wait_ge(named("xa_exp"), c0 + m + 1)
                    dve_then(dve.reciprocal(XMN[:, 2, m:m + 1], XMN[:, 1, m:m + 1]))
                    dve.tensor_scalar(XP[:, m % 3, :], XP[:, m % 3, :], XMN[:, 2, m:m + 1], None,
                                      ALU.mult).then_inc(named("xa_norm"), 1)
                if n >= 5 and n % 2:
                    xo_out(l, (n - 5) // 2)

        def xo_out(l, h):
            dve.wait_ge(named("xa_oh"), 4 * l + h + 1)
            dve.tensor_tensor(XO[1][:, 2 * h:2 * h + 2, :], PS[:, G + h % 2, :].rearrange("p (c n) -> p c n", c=2),
                              XO[0][:, 2 * h:2 * h + 2, :].bitcast(F32), ALU.subtract).then_inc(named("xa_o"), 1)

        HID = pair(16 * 256, FF2_TILES)
        RLU = HN[:, 0, :].rearrange("p (a c n) -> p a c n", a=2, c=2)
        RSQ = HN[:, 1, :].rearrange("p (a c n) -> p a c n", a=2, c=2)
        NM1 = D_FF_2 // 256

        def mlp_pe(l, turn):
            def free(u):
                if u == 0:
                    pe.wait_ge(s_x, 4 * (5 + 3 * l))
                if u >= 4:
                    pe.wait_ge(named("m1_relu"), NM1 * l + u - 3)
            for u in range(NM1):
                cols_unit(f"m1{l}", u, HT, G + u % 4, free, turned(turn, pe))
            rows_product(f"m2{l}", HID, FF2_TILES, ready=lambda k: pe.wait_ge(named("m1_sq"), NM1 * l + k // 2 + 1),
                         free=lambda: pe.wait_ge(named("m1_relu"), NM1 * (l + 1)))

        def mlp_act(l):
            for u in range(NM1):
                cols_done(act, f"m1{l}", u)
                if u >= 2:
                    act.wait_ge(named("m1_f"), NM1 * l + u - 1)
                    act.wait_ge(named("m1_h"), NM1 * l + u - 1)
                act_then(act.activation(RLU[:, u % 2, :, :], PS[:, G + u % 4, :].rearrange("p (c n) -> p c n", c=2),
                                        ACT.Relu))
                act.sem_inc(named("m1_relu"), 1)
                act.activation(HID[0][:, 2 * u:2 * u + 2, :], RLU[:, u % 2, :, :], ACT.Square).then_inc(named("m1_h"), 1)

        def mlp_pool(l):
            for u in range(NM1):
                pool.wait_ge(named("m1_relu"), NM1 * l + u + 1)
                if u >= 2:
                    pool.wait_ge(named("m1_sq"), NM1 * l + u - 1)
                pool.tensor_tensor(RSQ[:, u % 2, :, :], RLU[:, u % 2, :, :], RLU[:, u % 2, :, :],
                                   ALU.mult).then_inc(named("m1_f"), 1)

        def mlp_dve(l):
            for u in range(NM1):
                cols_done(dve, f"m1{l}", u)
                dve.wait_ge(named("m1_h"), NM1 * l + u + 1)
                dve.wait_ge(named("m1_f"), NM1 * l + u + 1)
                dve.tensor_tensor(HID[1][:, 2 * u:2 * u + 2, :], RSQ[:, u % 2, :, :],
                                  HID[0][:, 2 * u:2 * u + 2, :].bitcast(F32), ALU.subtract
                                  ).then_inc(named("m1_sq"), 1)

        NCU = 12
        QKV = view(16 * 256, (24, T))
        CC = view(48 * 256, (4, 2, T))
        SGC = view(40 * 256, (TT, D))
        SQL = view(56 * 256, (2, 512))
        RSL = view(60 * 256, (2, 512))
        DEC = view(8 * 256, (2, 4, P))
        ATC = view(56 * 256, (4, 4, P))
        ATT = view(64 * 256, (4, 4, P))
        RV = view(48 * 256, (4, 4, P))
        RK = view(72 * 256, (2, 4, P))
        KD = view(76 * 256, (2, 4, P))
        QD = view(80 * 256, (2, 4, P))
        GAB = row[0:40, ROW_LAM:ROW_LAM + T]
        CR = [HN[0:8, 0, T * j:T * (j + 1)] for j in (0, 1)] + [PIN_t[0:8, 0, :]] + [
            HN[0:8, 0, T * j:T * (j + 1)] for j in (2, 3)] + [
            HN[0:8, 1, T * j:T * (j + 1)] for j in (2, 3)] + [PIN_t[0:8, 1, :]]
        LT = view(0, (4, 4, P))
        XI = view(8 * 256, (4, 4, P))
        XT = view(16 * 256, (4, 4, P))
        YI = view(24 * 256, (4, 4, P))
        VN0 = view(24 * 256, (2, 4, P))
        S1 = view(28 * 256, (2, 4, P))
        NW = view(8 * 256, (2, 4, P))
        VN1 = view(12 * 256, (2, 4, P))
        OC = view(32 * 256, (TT, D))
        OSQ = view(56 * 256, (8, P))
        TE = HN[:, 0, :].rearrange("p (a h n) -> p a h n", a=2, h=4)
        TQ = HN[:, 1, 0:512].rearrange("p (h n) -> p h n", h=4)
        LM = sb("level_masks", [P, 7, P])
        GCB = sb("gate_cols", [P, TT, 40])
        GX = sb("gate_col_exps", [P, 4, 8])
        CST = sb("c_stats", [P, 3, 16])
        DG = sb("g_last_diag", [8, 8])
        NEA = sb("a_exp", [8, 1])
        eps128_c = sb("eps128_c", [P, 1])
        LEVELS = 7

        def c_consts_pool():
            pool.memset(eps128_c[:, :], P * EPS)
            pool_then(pool.memset(LM[:, :, :], 0.0))
            for i in range(LEVELS):
                b = 1 << i
                m = LM[:, i, :].rearrange("p (n h b) -> p n h b", h=2, b=b)[:, :, 1, :]
                n = P // (2 * b)
                pool_then(pool.memset(m, 1.0))
                pool_then(pool.affine_select(out=m, in_=m, compare_op=ALU.is_ge, fill=0.0, base=0,
                                             pattern=[[-2 * b, n], [0, b]], channel_multiplier=1))
                pool_then(pool.affine_select(out=m, in_=m, compare_op=ALU.is_ge, fill=0.0, base=b - 1,
                                             pattern=[[2 * b, n], [0, b]], channel_multiplier=-1))
            pool.sem_inc(named("c_consts"), 1)

        def c_pe():
            def free(u):
                if u == 0:
                    pe.wait_ge(s_x, 4 * 6)
                if u >= 4:
                    pe.wait_ge(named("c_conv"), u - 3)
            for u in range(NCU):
                cols_unit("c_qkv", u, HT, G + u % 4, free, turned(9, pe))
            cols_unit("c_g", 0, HT, (A, A + 1), lambda u: pe.wait_ge(s_tl, 4 * 10))

            def sum_squares(i):
                pe.wait_ge(named("l2_sq"), i + 1)
                if i >= 2:
                    pe.wait_ge(named("l2_ln"), i - 1)
                pe.matmul(PS[:, A + 2 + i % 2, :], ones[:, :], SQL[:, i % 2, :], start=True,
                          stop=True).then_inc(named("l2_ss"), 1)
            rows_product("c_gate", HT, DC, ready=sum_squares, free=lambda: pe.wait_ge(named("c_conv"), NCU))
            pe.wait_ge(named("c_rows"), 1)
            for t in range(TT):
                pe.transpose(PS[:, A, 40 * t:40 * t + 40], GAB[:, t * P:(t + 1) * P], ident[0:40, 0:40])
            pe.matmul(PS[:, A, 128:136], ones[0:8, :], DG[:, :], start=True, stop=True).then_inc(named("c_cols"), 1)
            for gi in range(4):
                hg, c = gi // 2, gi % 2
                pe.wait_ge(named("c_sg"), gi + 1)
                if gi == 0:
                    pe.wait_ge(named("c_silu"), NCU)
                for j in range(4):
                    mm = pe.transpose(PS[:, gi, j * P:(j + 1) * P], QKV[:, 16 + 4 * hg + j, c * P:(c + 1) * P],
                                      ident[:, :])
                mm.then_inc(named("c_vt"), 1)
            for gi in range(4):
                hg, c = gi // 2, gi % 2
                if gi == 0:
                    pe.wait_ge(named("l2_done"), 8)
                    pe.wait_ge(named("c_gcb"), 1)
                for j in range(4):
                    mm = pe.transpose(PS[:, 4 + gi, j * P:(j + 1) * P], QKV[:, 8 + 4 * hg + j, c * P:(c + 1) * P],
                                      ident[:, :])
                mm.then_inc(named("c_kt"), 1)
            for gi in range(4):
                hg, c = gi // 2, gi % 2
                pb = 4 * (gi % 2)
                tok = slice(c * P, (c + 1) * P)
                if gi < 2:
                    pe.wait_ge(named("c_rv" if gi == 0 else "c_rk"), 4)
                else:
                    pe.wait_ge(named("c_prep"), gi - 1)
                for i, r in ((0, 7), (1, 2)):
                    for j in range(4):
                        mm = pe.matmul(PS[:, pb + i, j * P:(j + 1) * P], sel[:, 4 * hg + j, :], CR[r][:, tok],
                                       start=True, stop=True)
                    mm.then_inc(named("c_p"), 1)
                for i, q0 in ((2, 8), (3, 0)):
                    for j in range(4):
                        mm = pe.matmul(PS[:, pb + i, j * P:(j + 1) * P], QKV[:, 8 + 4 * hg + j, tok],
                                       QKV[:, q0 + 4 * hg + j, tok], start=True, stop=True)
                    mm.then_inc(named("c_p"), 1)
            for gi in range(4):
                pe.wait_ge(named("c_lt"), gi + 1)
                if gi == 0:
                    pe.wait_ge(named("c_prep"), 4)
                if gi >= 2:
                    pe.wait_ge(named("c_x"), gi - 1)
                for j in range(4):
                    mm = pe.transpose(PS[:, 6 + gi % 2, j * P:(j + 1) * P], LT[:, gi, j, :], ident[:, :])
                mm.then_inc(named("c_l0"), 1)

            NL = 4 * (LEVELS - 1)

            def y(n):
                gi = n % 4
                pe.wait_ge(named("c_x"), n + 1)
                pe.wait_ge(named("c_lt"), n + 5)
                if n >= 2:
                    pe.wait_ge(named("c_y"), n - 1)
                for j in range(4):
                    mm = pe.matmul(PS[:, gi % 2, j * P:(j + 1) * P], LT[:, gi, j, :], XI[:, gi, j, :], start=True,
                                   stop=True)
                mm.then_inc(named("c_ym"), 1)

            def pq(n):
                gi = n % 4
                pe.wait_ge(named("c_y"), n + 1)
                if n >= 2:
                    pe.wait_ge(named("c_x"), n + 3)
                if n < NL - 4:
                    for j in range(4):
                        pe.matmul(PS[:, 2 + gi % 2, j * P:(j + 1) * P], XT[:, gi, j, :], YI[:, gi, j, :], start=True,
                                  stop=True)
                for j in range(4):
                    mm = pe.matmul(PS[:, 4 + gi % 2, j * P:(j + 1) * P], YI[:, gi, j, :], XT[:, gi, j, :], start=True,
                                   stop=True)
                mm.then_inc(named("c_pq"), 1)

            for n in range(NL + 1):
                if n < NL:
                    y(n)
                if n >= 1:
                    pq(n - 1)

            def quad(bank, terms, told):
                for j in range(4):
                    for i, (l, r) in enumerate(terms):
                        mm = pe.matmul(PS[:, bank, j * P:(j + 1) * P], l[:, j, :], r[:, j, :], start=(i == 0),
                                       stop=(i == len(terms) - 1))
                mm.then_inc(named(told), 1)

            for hg in range(2):
                g0, g1 = 2 * hg, 2 * hg + 1
                pe.wait_ge(named("c_x"), 4 * LEVELS if hg else 4 * LEVELS - 2)
                if hg == 0:
                    pe.wait_ge(named("c_y"), NL)
                quad(hg, [(XT[:, g0], RV[:, g0])], "c_u0")
                quad(6 + hg, [(RK[:, hg], XT[:, g1])], "c_wt")
            for hg in range(2):
                pe.wait_ge(named("c_vn0"), hg + 1)
                quad(2 + hg, [(KD[:, hg], VN0[:, hg])], "c_s1m")
                quad(hg, [(ATT[:, 2 * hg], VN0[:, hg])], "c_o0")
            for hg in range(2):
                g1 = 2 * hg + 1
                pe.wait_ge(named("c_nw"), hg + 1)
                pe.wait_ge(named("c_s1"), hg + 1)
                quad(4 + hg, [(XT[:, g1], RV[:, g1]), (NW[:, hg], S1[:, hg])], "c_u1")
            for hg in range(2):
                pe.wait_ge(named("c_vn1"), hg + 1)
                quad(2 + hg, [(QD[:, hg], S1[:, hg]), (ATT[:, 2 * hg + 1], VN1[:, hg])], "c_o1")

        def c_act():
            def silu(u):
                act.wait_ge(named("c_conv"), u + 1)
                act.activation(QKV[:, 2 * u:2 * u + 2, :], CC[:, u % 4, :, :], ACT.Silu).then_inc(named("c_silu"), 1)

            for u in range(NCU):
                cols_done(act, "c_qkv", u)
                for f in range(2):
                    ins = act.activation(CC[:, u % 4, f, :], PS[:, G + u % 4, f * T:(f + 1) * T], ACT.Copy,
                                         scale=cconv_cols[:, 2 * u + f, 3:4])
                ins.then_inc(named("c_tap"), 1)
                if u:
                    silu(u - 1)
            silu(NCU - 1)
            split_through(act, "c_g", 3)
            act.preload_act_table_set(EXP_LN)
            R = lambda j: CR[j]
            act.wait_ge(named("c_za"), 1)
            act_then(act.activation(R(6), R(5), ACT.Exp))
            act.activation(R(6), R(6), ACT.Ln, bias=one_c[0:8, 0:1]).then_inc(named("c_la"), 1)
            act.activation(R(0), PS[0:8, A, 0:T], ACT.Exp, scale=-1.0).then_inc(named("c_eb"), 1)
            act.activation(NEA[:, :], gate_p[:, 3:4], ACT.Exp).then_inc(named("c_nea"), 1)
            for i in range(8):
                split_through(act, "c_g", i + 2)
                act.wait_ge(named("l2_ss"), i + 1)
                if i >= 2:
                    act.wait_ge(named("l2_done"), i - 1)
                q = i < 4
                act.activation(RSL[:, i % 2, :], PS[:, A + 2 + i % 2, :], ACT.Ln,
                               bias=(eps128_c if q else eps_c)[:, 0:1],
                               scale=(float(P) if q else 1.0)).then_inc(named("l2_ln"), 1)
                act.wait_ge(named("l2_ln"), i + 1)
                act.activation(RSL[:, i % 2, :], RSL[:, i % 2, :], ACT.Exp, scale=-0.5).then_inc(named("l2_rs"), 1)
            for b in range(4):
                rows_done(act, "c_gate", b)
                act.activation(SGC[:, b // 2, (b % 2) * 512:(b % 2 + 1) * 512], PS[:, G + b, :],
                               ACT.Silu).then_inc(named("c_sg"), 1)
            act.preload_act_table_set(EXP_LN)
            act.wait_ge(named("c_gcb"), 1)
            act.activation(GX[:, 0, :], GCB[:, 1, 0:8], ACT.Exp).then_inc(named("c_gx"), 1)
            act.activation(GX[:, 3, :], GX[:, 2, :], ACT.Exp).then_inc(named("c_gx"), 1)
            for gi in range(4):
                act.wait_ge(named("c_e"), gi + 1)
                if gi >= 2:
                    act.wait_ge(named("c_prep"), gi - 1)
                act.activation(DEC[:, gi % 2, :, :], TE[:, gi % 2, :, :], ACT.Exp).then_inc(named("c_dec"), 1)
                if gi % 2:
                    if gi == 3:
                        act.wait_ge(named("c_qd"), 1)
                    act.activation(TQ, PS[:, 4 * (gi % 2), :].rearrange("p (h n) -> p h n", h=4),
                                   ACT.Exp).then_inc(named("c_tq"), 1)
            for n in range(4 * (LEVELS - 1)):
                act.wait_ge(named("c_ym"), n + 1)
                act.activation(YI[:, n % 4, :, :], PS[:, (n % 4) % 2, :].rearrange("p (h n) -> p h n", h=4),
                               ACT.Copy).then_inc(named("c_y"), 1)
                if n in (9, 13):
                    split_through(act, "c_gate", 3 + (n == 13))
            for hg in range(2):
                act.wait_ge(named("c_wt"), hg + 1)
                act.activation(NW[:, hg, :, :], PS[:, 6 + hg, :].rearrange("p (h n) -> p h n", h=4), ACT.Copy,
                               scale=-1.0).then_inc(named("c_nw"), 1)
            for hg in range(2):
                act.wait_ge(named("c_s1m"), hg + 1)
                act.activation(S1[:, hg, :, :], PS[:, 2 + hg, :].rearrange("p (h n) -> p h n", h=4),
                               ACT.Copy).then_inc(named("c_s1"), 1)
            for hg in range(2):
                act.wait_ge(named("c_o0"), hg + 1)
                act.activation(OC[:, 0, half(hg)], PS[:, hg, :], ACT.Copy).then_inc(named("c_oc0"), 1)
            for t in range(TT):
                act.wait_ge(named(("c_oc0", "c_oc1")[t]), 2)
                for h in range(8):
                    ins = act.activation(OSQ[:, h, :], OC[:, t, h * P:(h + 1) * P], ACT.Square,
                                         accum_out=CST[:, 0, 8 * t + h:8 * t + h + 1])
                act_then(ins)
                r = slice(8 * t, 8 * t + 8)
                act_then(act.activation(CST[:, 1, r], CST[:, 0, r], ACT.Ln, bias=eps_c[:, 0:1], scale=1.0 / P))
                act.activation(CST[:, 2, r], CST[:, 1, r], ACT.Exp, scale=-0.5).then_inc(named("c_hrs"), 1)

        def c_pool():
            pool.wait_ge(named("c_silu"), 8)
            for i in range(8):
                if i >= 2:
                    pool.wait_ge(named("l2_ss"), i - 1)
                pool.tensor_tensor(SQL[:, i % 2, :].rearrange("p (c n) -> p c n", c=2), QKV[:, 2 * i:2 * i + 2, :],
                                   QKV[:, 2 * i:2 * i + 2, :], ALU.mult).then_inc(named("l2_sq"), 1)
            gate_gain_pool(SGC, row[:, ROW_CHEAD:ROW_CHEAD + P].unsqueeze(1).to_broadcast([P, 8, P]), 8, "c_sg", 2,
                           "gate_gain")
            def qd(hg):
                pool.wait_ge(named("c_tq"), hg + 1)
                pool.tensor_tensor(QD[:, hg, :, :], QKV[:, 4 * hg:4 * hg + 4, P:T], TQ, ALU.mult).then_inc(named("c_qd"), 1)

            qd(0)
            for n in range(4 * LEVELS):
                lvl, gi = n // 4, n % 4
                if n == 2:
                    qd(1)
                if lvl == 0:
                    pool.wait_ge(named("c_prep"), gi + 1)
                elif lvl == 1:
                    pool.wait_ge(named("c_x"), gi + 1)
                elif lvl > 1:
                    pool.wait_ge(named("c_ym"), n - 7)
                pool.tensor_tensor(LT[:, gi, :, :], ATC[:, gi, :, :],
                                   LM[:, lvl, :].unsqueeze(1).to_broadcast([P, 4, P]), ALU.mult
                                   ).then_inc(named("c_lt"), 1)

        def c_dve():
            for u in range(NCU):
                cols_done(dve, "c_qkv", u)
                dve.wait_ge(named("c_tap"), u + 1)
                for tap in (2, 1, 0):
                    lag = 3 - tap
                    for f in range(2):
                        ins = dve.scalar_tensor_tensor(
                            out=CC[:, u % 4, f, lag:T], in0=PS[:, G + u % 4, f * T:(f + 1) * T - lag],
                            scalar=cconv_cols[:, 2 * u + f, tap:tap + 1], in1=CC[:, u % 4, f, lag:T], op0=ALU.mult,
                            op1=ALU.add)
                    if tap:
                        dve_then(ins)
                ins.then_inc(named("c_conv"), 1)
            R = lambda j: CR[j]
            cols_done(dve, "c_g", 0)
            split_through(dve, "c_g", 3)
            dve_then(dve.tensor_scalar(R(3), PS[0:8, A + 1, 0:T], gate_p[:, 4:5], None, ALU.add))
            dve_then(dve.tensor_scalar(R(4), R(3), 0.0, None, ALU.min))
            dve.scalar_tensor_tensor(out=R(5), in0=R(4), scalar=2.0, in1=R(3), op0=ALU.mult,
                                     op1=ALU.subtract).then_inc(named("c_za"), 1)
            dve.memset(GAB[:, :], 0.0)
            dve.wait_ge(named("c_eb"), 1)
            dve_then(dve.tensor_scalar(R(1), R(0), 1.0, None, ALU.add))
            dve_then(dve.reciprocal(R(2), R(1)))
            dve.wait_ge(named("c_la"), 1)
            dve.wait_ge(named("c_nea"), 1)
            dve_then(dve.tensor_tensor(R(3), R(3), R(6), ALU.add))
            dve_then(dve.tensor_tensor(R(3), R(3), R(4), ALU.subtract))
            dve_then(dve.tensor_scalar(R(5), R(3), NEA[:, 0:1], -1.0, ALU.mult, ALU.mult))
            for c in range(2):
                s_ = CR[5][:, c * P:(c + 1) * P]
                ins = dve.tensor_tensor_scan(CR[7][:, c * P:(c + 1) * P], s_, s_, 0.0, ALU.add, ALU.bypass)
            dve_then(ins)
            dve.tensor_scalar(DG[:, :], ident[0:8, 0:8], CR[7][:, P - 1:P], None, ALU.mult)
            dve.tensor_copy(GAB[0:8, :], R(7))
            dve_then(dve.tensor_copy(GAB[32:40, :], R(2)))
            dve.sem_inc(named("c_rows"), 1)
            for i in range(8):
                split_through(dve, "c_g", i + 2)
                dve.wait_ge(named("l2_rs"), i + 1)
                o = QKV[:, 2 * i:2 * i + 2, :]
                dve.tensor_tensor(o, o, RSL[:, i % 2, :].rearrange("p (c n) -> p c n", c=2),
                                  ALU.mult).then_inc(named("l2_done"), 1)
            split_through(dve, "c_gate", 2)
            dve.wait_ge(named("c_cols"), 1)
            dve_then(dve.tensor_copy(GCB[:, :, :], PS[:, A, 0:80].rearrange("p (t n) -> p t n", t=2)))
            dve_then(dve.tensor_tensor(GX[:, 2, :], PS[:, A, 128:136], GCB[:, 0, 0:8], ALU.subtract))
            dve.sem_inc(named("c_gcb"), 1)

            def bc(col):
                return col.unsqueeze(2).to_broadcast([P, 4, P])

            def quad(bank):
                return PS[:, bank, :].rearrange("p (h n) -> p h n", h=4)

            for gi in range(4):
                hg, c = gi // 2, gi % 2
                dve.wait_ge(named("c_vt"), gi + 1)
                dve.tensor_tensor(RV[:, gi, :, :], quad(gi), bc(GCB[:, c, 32 + 4 * hg:36 + 4 * hg]),
                                  ALU.mult).then_inc(named("c_rv"), 1)
            dve.wait_ge(named("c_gx"), 2)
            dve_then(dve.tensor_tensor(GX[:, 1, :], GX[:, 0, :], GCB[:, 1, 32:40], ALU.mult))
            for gi in range(4):
                hg, c = gi // 2, gi % 2
                dve.wait_ge(named("c_kt"), gi + 1)
                dst, col = (RK, 1) if c else (KD, 3)
                dve.tensor_tensor(dst[:, hg, :, :], quad(4 + gi), bc(GX[:, col, 4 * hg:4 * hg + 4]),
                                  ALU.mult).then_inc(named("c_rk"), 1)
            for gi in range(4):
                hg, c = gi // 2, gi % 2
                pb = 4 * (gi % 2)
                dve.wait_ge(named("c_p"), 4 * gi + 1)
                if gi >= 2:
                    dve.wait_ge(named("c_dec"), gi - 1)
                for j in range(4):
                    ins = dve.scalar_tensor_tensor(out=TE[:, gi % 2, j, :], in0=PS[:, pb, j * P:(j + 1) * P],
                                                   scalar=GCB[:, c, 4 * hg + j:4 * hg + j + 1], in1=neg_ge[:, 0, :],
                                                   op0=ALU.subtract, op1=ALU.add)
                ins.then_inc(named("c_e"), 1)
                dve.wait_ge(named("c_dec"), gi + 1)
                dve.wait_ge(named("c_p"), 4 * gi + 4)
                dec = DEC[:, gi % 2, :, :]
                dve_then(dve.tensor_tensor(ATC[:, gi, :, :], quad(pb + 2), dec, ALU.mult))
                dve.tensor_tensor(ATT[:, gi, :, :], quad(pb + 3), dec, ALU.mult)
                if c:
                    dve.wait_ge(named("c_tq"), hg + 1)
                dve_then(dve.tensor_tensor(ATC[:, gi, :, :], quad(pb + 1), ATC[:, gi, :, :], ALU.mult))
                dve.sem_inc(named("c_prep"), 1)
            idb = ident[:, :].unsqueeze(1).to_broadcast([P, 4, P])
            for gi in range(4):
                dve.wait_ge(named("c_l0"), gi + 1)
                dve.tensor_tensor(XT[:, gi, :, :], idb, LT[:, gi, :, :], ALU.subtract)
                dve_then(dve.scalar_tensor_tensor(out=XI[:, gi, :, :], in0=quad(6 + gi % 2), scalar=-1.0, in1=idb,
                                                  op0=ALU.mult, op1=ALU.add))
                dve.sem_inc(named("c_x"), 1)
            NL = 4 * (LEVELS - 1)
            for n in range(NL):
                gi = n % 4
                dve.wait_ge(named("c_pq"), n + 1)
                if n < NL - 4:
                    dve.tensor_tensor(XI[:, gi, :, :], XI[:, gi, :, :], quad(2 + gi % 2), ALU.subtract)
                dve_then(dve.tensor_tensor(XT[:, gi, :, :], XT[:, gi, :, :], quad(4 + gi % 2), ALU.subtract))
                dve.sem_inc(named("c_x"), 1)
                if n in (9, 13):
                    split_through(dve, "c_gate", 3 + (n == 13))
            for hg in range(2):
                dve.wait_ge(named("c_u0"), hg + 1)
                dve.tensor_copy(VN0[:, hg, :, :], quad(hg)).then_inc(named("c_vn0"), 1)
            for hg in range(2):
                dve.wait_ge(named("c_u1"), hg + 1)
                dve.tensor_copy(VN1[:, hg, :, :], quad(4 + hg)).then_inc(named("c_vn1"), 1)
            for hg in range(2):
                dve.wait_ge(named("c_o1"), hg + 1)
                dve.tensor_copy(OC[:, 1, half(hg)], PS[:, 2 + hg, :]).then_inc(named("c_oc1"), 1)
            dve.wait_ge(named("c_oc1"), 2)
            dve.wait_ge(named("gate_gain"), 4)
            for t in range(TT):
                dve.wait_ge(named("c_hrs"), t + 1)
                head_gate_dve(OC, t, CST, 8, SGC, "c_om")

        def final_act():
            norm_stats_act(10, X, resid(9))

        def final_dve():
            for t in range(TT):
                if t:
                    first_half_dve(10, 1)
                dve.wait_ge(s_rstd, 2 * 10 + t + 1)
                dve.scalar_tensor_tensor(out=HN[:, t, :], in0=X[:, t, :], scalar=rstd[:, t:t + 1],
                                         in1=row[:, ROW_FINAL:ROW_FINAL + D], op0=ALU.mult,
                                         op1=ALU.mult).then_inc(named("final"), 1)

        def final_sp(sp):
            for t in range(TT):
                sp.wait_ge(named("final"), t + 1)
                sp.dma_start(out[t * P:(t + 1) * P, :], HN[:, t, :]).then_inc(s_out, 16)
            sp.wait_ge(s_out, 16 * TT)

        block = ctx.enter_context(nc.Block())

        @block.sync
        def _(sp):
            early_sp(sp)
            weights_sp(sp, 0, RING)
            small_sp(sp)
            weights_sp(sp, RING, len(plan))
            final_sp(sp)

        @block.gpsimd
        def _(p_):
            consts_pool()
            c_consts_pool()
            up_pool()
            gate_gain_pool(SGM, row[:, ROW_ABHEAD:ROW_ABHEAD + 512].rearrange("p (h d) -> p h d", h=4), 4,
                           "ab_sgm", 1, "gate_gain")
            for l in range(2):
                if l:
                    c_pool()
                mlp_pool(l)

        @block.tensor
        def _(p_):
            pe.wait_ge(s_const, 1)
            turn_pe(0, HN, norm_ready_pe(0))
            qk_pe()
            v_pe()
            attn_pe()
            turn_pe(2, OM, lambda t, h: (pe.wait_ge(named("mix_out"), t + 1), pe.wait_ge(named("at_o"), NA)))
            rows_product("w_out", HT, DC, ready=turned(2, pe), free=lambda: pe.wait_ge(named("v1_ready"), 4))
            turn_pe(3, HN, norm_ready_pe(2))
            up_pe()
            ple_p_pe()
            down_pe()
            ple_proj_pe()
            turn_pe(4, HN, norm_ready_pe(3))
            ple_gate_pe()
            xa_k_pe(0)
            turn_pe(5, HN, norm_ready_pe(4))
            ab_pe()
            turn_pe(6, OM2, lambda t, h: (pe.wait_ge(named("ab_om"), t + 1), pe.wait_ge(named("ab_o"), 8)))
            rows_product("ab_out", HT, DC, ready=turned(6, pe))
            for l in range(2):
                if l:
                    turn_pe(9, HN, norm_ready_pe(7))
                    c_pe()
                    turn_pe(10, OC, lambda t, h: pe.wait_ge(named("c_om"), t + 1))
                    rows_product("c_out", HT, DC, ready=turned(10, pe))
                (xa_k_pe if l else xa_v_pe)(l)
                turn_pe(7 + 4 * l, HN, norm_ready_pe(5 + 3 * l))
                if l:
                    xa_v_pe(l)
                xa_pe(l, 7 + 4 * l)
                turn_pe(8 + 4 * l, HN, norm_ready_pe(6 + 3 * l))
                mlp_pe(l, 8 + 4 * l)

        @block.scalar
        def _(p_):
            act.preload_act_table_set(EXP_LN)
            act.wait_ge(s_const, 1)
            norm_act(0, X, lambda e, b: e.wait_ge(s_x_in[b // 2], 16))
            split(act, 1)
            act.wait_ge(s_early, 16 * 3)
            turn_act(0, HT, LN_MIX)
            qk_act()
            v_act()
            attn_act()
            turn_act(2, HT)
            norm_act(2, X, resid(1))
            turn_act(3, HT, LN_FFN)
            up_act()
            ple_p_act()
            act.preload_act_table_set(EXP_LN)
            norm_act(3, X, resid(2))
            split_through(act, "ple_proj", 4)
            turn_act(4, HT, LN_PLE)
            ple_act()
            act.preload_act_table_set(EXP_LN)
            split_through(act, "ple_gate", 4)
            norm_act(4, X, resid(3))
            xa_k_evac(0, act)
            turn_act(5, HT, LN_MIX0)
            ab_act()
            turn_act(6, HT)
            for l in range(2):
                if l:
                    norm_act(7, X, resid(6))
                    turn_act(9, HT, LN_MIX1)
                    c_act()
                    turn_act(10, HT)
                norm_act(5 + 3 * l, X, resid(4 + 3 * l))
                (xa_k_evac if l else xa_v_evac)(l, act)
                turn_act(7 + 4 * l, HT, LN_XA0 + 3 * l)
                if l:
                    xa_v_evac(l, act)
                xa_act(l)
                norm_act(6 + 3 * l, X, resid(5 + 3 * l))
                turn_act(8 + 4 * l, HT, LN_MLP0 + 3 * l)
                mlp_act(l)
            final_act()

        @block.vector
        def _(p_):
            dve.wait_ge(s_const, 1)
            norm_dve(0, X, lambda e, b: e.wait_ge(s_x_in[b // 2], 16))
            split(dve, 1)
            dve.wait_ge(s_early, 16 * 3)
            turn_dve(0, HT, LN_MIX)
            early_dve()
            qk_dve()
            fg_dve()
            mem_dve()
            lam_dve()
            attn_dve()
            turn_dve(2, HT)
            resid_add_dve("w_out", 2)
            norm_dve(2, X)
            turn_dve(3, HT, LN_FFN)
            up_dve()
            ple_p_dve()
            resid_add_dve("down", 3)
            norm_dve(3, X)
            split_through(dve, "ple_proj", 4)
            turn_dve(4, HT, LN_PLE)
            ple_dve()
            split_through(dve, "ple_gate", 4)
            norm_dve(4, X)
            xa_k_evac(0, dve)
            turn_dve(5, HT, LN_MIX0)
            ab_dve()
            turn_dve(6, HT)
            resid_add_dve("ab_out", 5)
            for l in range(2):
                if l:
                    norm_dve(7, X)
                    turn_dve(9, HT, LN_MIX1)
                    c_dve()
                    turn_dve(10, HT)
                    resid_add_dve("c_out", 8)
                norm_dve(5 + 3 * l, X)
                (xa_k_evac if l else xa_v_evac)(l, dve)
                turn_dve(7 + 4 * l, HT, LN_XA0 + 3 * l)
                if l:
                    xa_v_evac(l, dve)
                xa_dve(l)
                resid_add_dve(f"xo{l}", 6 + 3 * l)
                norm_dve(6 + 3 * l, X)
                turn_dve(8 + 4 * l, HT, LN_MLP0 + 3 * l)
                mlp_dve(l)
                resid_add_dve(f"m2{l}", 7 + 3 * l)
            final_dve()


def laid_out(v):
    import numpy as np

    f = {k: np.asarray(a) for k, a in v.items()}
    wi, ab, cw = f["w_in"][0], f["ab_w_in_2"][0], f["c_w_in_2"][0]
    a = {"x": f["x"][0], "mem": f["mem_2"][0], "p": f["p"][0, 0]}
    a["w_in"] = np.concatenate([wi[:, 0:1024], wi[:, 1280:2048], wi[:, 2438:3206], wi[:, 1024:1280],
                                wi[:, 2048:2432], wi[:, 3206:3590]], axis=1)
    a["w_out"], a["w_up"], a["w_down"] = f["w_out"][0], f["w_up"][0], f["w_down"][0]
    a["w_ple_gate"], a["w_ple_proj"] = f["w_ple_gate"][0], f["w_ple_proj"][0]
    a["ab_w_in"] = np.concatenate([ab[:, 1544:2568], ab[:, 0:512], ab[:, 512:1536], ab[:, 2568:3080]], axis=1)
    a["ab_w_out"], a["c_w_out"] = f["ab_w_out_2"][0], f["c_w_out_2"][0]
    a["c_w_in"] = cw[:, 0:4096]
    for l in range(2):
        for n in ("xa_wq", "xa_wk", "xa_wv", "xa_wo", "mlp_w1", "mlp_w2"):
            a[f"{n}{l}"] = f[f"{n}_2"][l]
    g = np.zeros((1024, 768), np.float32)
    for at, cols in ((0, wi[:, 2432:2438]), (256, ab[:, 1536:1540]), (384, ab[:, 1540:1544]),
                     (512, cw[:, 4096:4104]), (640, cw[:, 4104:4112])):
        g[:, at:at + cols.shape[1]] = cols
    a["gates"] = g
    lns = np.stack([f["ln_mix"][0], f["ln_ffn"][0], f["ln_ple"][0], f["mem_norm_2"], f["mix_norm_2"][0],
                    f["xa_norm_2"][0], f["mlp_norm_2"][0], f["mix_norm_2"][1], f["xa_norm_2"][1], f["mlp_norm_2"][1]])
    a["ln_cols"] = lns.reshape(10, 8, 128).transpose(2, 0, 1).reshape(128, 80)
    a["qk_cols"] = np.concatenate([f["qk_gain"][0].T, f["qk_gain"][0].T], axis=0)
    a["row"] = np.concatenate([f["subln_gain"][0], f["ab_head_gain_2"][0].reshape(-1), f["c_head_gain_2"][0],
                               f["lam_params"][0].reshape(-1), f["final_norm_2"]])[None, :]
    cc = np.concatenate([f["conv_w"][0], f["conv_b"]], axis=0)
    a["conv_cols"] = cc.reshape(4, 44, 128).transpose(2, 1, 0).reshape(128, 176)
    a["cconv_cols"] = f["c_conv_w_2"][0].reshape(4, 24, 128).transpose(2, 1, 0).reshape(128, 96)
    gp = np.zeros((8, 5), np.float32)
    gp[0:6, 0], gp[0:4, 1], gp[0:4, 2] = f["fgate_bias"][0], f["ab_b_i_2"][0], f["ab_b_f_2"][0]
    gp[:, 3], gp[:, 4] = f["c_a_log_2"][0], f["c_dt_bias_2"][0]
    a["gate_p"] = gp
    a["rel_rev"] = f["rel_bias"][0][:, ::-1]
    return {k: np.ascontiguousarray(x) for k, x in a.items()}


def kernel(**inputs):
    import numpy as _np
    import concourse.bacc as _bacc
    from concourse import mybir as _mybir
    from concourse.bass_utils import run_bass_kernel_spmd as _run

    nc = _bacc.Bacc("TRN2", target_bir_lowering=False, num_devices=1)
    arrays = laid_out(inputs)
    I = {n: nc.dram_tensor(f"in_{n}", a.shape, _mybir.dt.from_np(a.dtype), kind="ExternalInput").ap()
         for n, a in arrays.items()}
    out = nc.dram_tensor("out_0", (T, D), _mybir.dt.float32, kind="ExternalOutput").ap()
    scratch = nc.dram_tensor("rel_rows", (6, P, 511), _mybir.dt.float32).ap()
    build_two_blocks(nc, I, out, scratch)
    r = _run(nc, [{f"in_{n}": a for n, a in arrays.items()}], core_ids=[0])
    return _np.asarray(r.results[0]["out_0"]).reshape(1, T, D)
```
